# Optimizing a Trainium2 kernel written in Bass

```python
import math
import jax
import jax.numpy as jnp
from jax import lax
import numpy as np

D_MODEL = 1024
BATCH = 1
SEQ = 128
DEPTH = 2
DEC_BATCH = 1
DEC_SEQ = 128
PAST_LEN = 128

GRID_W = 64
N_MIXERS = 2
N_ATTN_LAYERS = (DEPTH + N_MIXERS - 1) // N_MIXERS
N_CONV_LAYERS = DEPTH // N_MIXERS
N_HEADS = 8
HEAD_DIM = 64
V_DIM = 2 * HEAD_DIM
ROPE_THETA = 10000.0
Q_BLOCK = 128
CONV_WIDTH = 31
N_EXPERTS = 16
N_GROUPS = 4
EXPERTS_PER_GROUP = N_EXPERTS // N_GROUPS
TOP_K = 2
D_EXPERT = 512
EPS = 1e-6

kernel_name = 'hybrid_diffattn_conformer_moe_prefix_dit_step'

def rmsnorm(x, g):
    xf = x.astype(jnp.float32)
    y = xf * lax.rsqrt(jnp.mean(xf * xf, axis=-1, keepdims=True) + EPS)
    return (y * g.astype(jnp.float32)).astype(x.dtype)

def layernorm(x, g, b):
    xf = x.astype(jnp.float32)
    mu = jnp.mean(xf, axis=-1, keepdims=True)
    var = jnp.mean(jnp.square(xf - mu), axis=-1, keepdims=True)
    y = (xf - mu) * lax.rsqrt(var + EPS)
    return (y * g.astype(jnp.float32) + b.astype(jnp.float32)).astype(x.dtype)

def modulation(cond, w_ada, b_ada):
    m = jax.nn.silu(cond) @ w_ada + b_ada
    return jnp.split(m, 6, axis=-1)

def modulate(h, shift, scale):
    return h * (1.0 + scale) + shift

def axial_rope_tables(n_tokens):
    n_rows = n_tokens // GRID_W
    row = jnp.repeat(jnp.arange(n_rows, dtype=jnp.float32), GRID_W)
    col = jnp.tile(jnp.arange(GRID_W, dtype=jnp.float32), n_rows)
    n_freq = HEAD_DIM // 4
    inv_freq = ROPE_THETA ** (-jnp.arange(n_freq, dtype=jnp.float32) / n_freq)
    ang = jnp.stack([row[:, None] * inv_freq, col[:, None] * inv_freq], axis=1)
    return jnp.cos(ang), jnp.sin(ang)

def apply_axial_rope(x, cos, sin):
    shp = x.shape
    xs = x.astype(jnp.float32).reshape(shp[:-1] + (2, 2, HEAD_DIM // 4))
    x1, x2 = xs[..., 0, :], xs[..., 1, :]
    c = cos[None, :, None, None]
    s = sin[None, :, None, None]
    out = jnp.stack([x1 * c - x2 * s, x1 * s + x2 * c], axis=-2)
    return out.reshape(shp).astype(x.dtype)

def diff_attn_project(h, w_qkv):
    b, t, _ = h.shape
    q, k, v = jnp.split(h @ w_qkv, 3, axis=-1)
    q = q.reshape(b, t, N_HEADS, 2, HEAD_DIM)
    k = k.reshape(b, t, N_HEADS, 2, HEAD_DIM)
    v = v.reshape(b, t, N_HEADS, V_DIM)
    return q, k, v

def diff_attention_core(q, k, v, lam):
    b, tq = q.shape[:2]
    nb = tq // Q_BLOCK
    qb = q.reshape(b, nb, Q_BLOCK, N_HEADS, 2, HEAD_DIM).swapaxes(0, 1)
    scale = HEAD_DIM ** -0.5

    def one_block(qblk):
        s = jnp.einsum('bqhmd,bkhmd->bhmqk', qblk, k, preferred_element_type=jnp.float32) * scale
        p = jax.nn.softmax(s, axis=-1)
        a = p[:, :, 0] - lam * p[:, :, 1]
        return jnp.einsum('bhqk,bkhe->bqhe', a.astype(v.dtype), v)

    out = lax.map(one_block, qb)
    return out.swapaxes(0, 1).reshape(b, tq, N_HEADS, V_DIM)

def diff_attn_output(o, subln_g, w_o, lambda_init):
    b, t = o.shape[:2]
    o = rmsnorm(o, subln_g) * (1.0 - lambda_init)
    return o.reshape(b, t, D_MODEL) @ w_o

def conformer_conv(h, w_pw1, b_pw1, w_dw, b_dw, ln_g, ln_b, w_pw2, b_pw2):
    a, g = jnp.split(h @ w_pw1 + b_pw1, 2, axis=-1)
    u = a * jax.nn.sigmoid(g)
    u = lax.conv_general_dilated(
        u, w_dw[:, None, :].astype(u.dtype), window_strides=(1,),
        padding=[(CONV_WIDTH // 2, CONV_WIDTH // 2)],
        dimension_numbers=('NWC', 'WIO', 'NWC'),
        feature_group_count=D_MODEL) + b_dw
    u = jax.nn.silu(layernorm(u, ln_g, ln_b))
    return u @ w_pw2 + b_pw2

def grouped_moe(h, router_w, router_bias, w_gate, w_up, w_down):
    b, t, d = h.shape
    hf = h.reshape(b * t, d)
    scores = jax.nn.sigmoid(jnp.dot(hf, router_w, preferred_element_type=jnp.float32))
    sel = scores + router_bias.astype(jnp.float32)
    gscore = lax.top_k(sel.reshape(-1, N_GROUPS, EXPERTS_PER_GROUP), TOP_K)[0].sum(-1)
    best = jnp.argmax(gscore, axis=-1)
    in_group = (jnp.arange(N_EXPERTS) // EXPERTS_PER_GROUP)[None, :] == best[:, None]
    _, idx = lax.top_k(jnp.where(in_group, sel, -jnp.inf), TOP_K)
    wts = jnp.take_along_axis(scores, idx, axis=-1)
    wts = wts / jnp.sum(wts, axis=-1, keepdims=True)
    gates = jnp.einsum('nk,nke->ne', wts, jax.nn.one_hot(idx, N_EXPERTS, dtype=jnp.float32))
    gact = jnp.einsum('nd,edf->nef', hf, w_gate)
    up = jnp.einsum('nd,edf->nef', hf, w_up)
    act = jax.nn.silu(gact) * up * gates.astype(h.dtype)[:, :, None]
    y = jnp.einsum('nef,efd->nd', act, w_down)
    return y.reshape(b, t, d)

def setup_inputs(seed: int = 0) -> dict:
    key = jax.random.key(seed)
    ks = list(jax.random.split(key, 40))

    def nrm(i, shape, scale):
        return jax.random.normal(ks[i], shape, jnp.float32) * scale

    D = D_MODEL
    return {
        'x_prompt': nrm(0, (BATCH, SEQ, D), 1.0),
        'x_sample': nrm(1, (DEC_BATCH, DEC_SEQ, D), 1.0),
        'cache_k': nrm(2, (DEC_BATCH, N_ATTN_LAYERS, PAST_LEN, N_HEADS, 2 * HEAD_DIM), 1.0),
        'cache_v': nrm(3, (DEC_BATCH, N_ATTN_LAYERS, PAST_LEN, N_HEADS, V_DIM), 1.0),
        'c': nrm(4, (DEC_BATCH, D), 1.0),
        'c_ctx': nrm(5, (D,), 1.0),
        'norm1_g': 1.0 + nrm(6, (DEPTH, D), 0.02),
        'norm2_g': 1.0 + nrm(7, (DEPTH, D), 0.02),
        'ada_w': nrm(8, (DEPTH, D, 6 * D), 0.5 * D ** -0.5),
        'ada_b': nrm(9, (DEPTH, 6 * D), 0.01),
        'attn_w_qkv': nrm(10, (N_ATTN_LAYERS, D, 3 * D), D ** -0.5),
        'attn_w_o': nrm(11, (N_ATTN_LAYERS, D, D), D ** -0.5),
        'attn_lambda_q1': nrm(12, (N_ATTN_LAYERS, HEAD_DIM), 0.1),
        'attn_lambda_k1': nrm(13, (N_ATTN_LAYERS, HEAD_DIM), 0.1),
        'attn_lambda_q2': nrm(14, (N_ATTN_LAYERS, HEAD_DIM), 0.1),
        'attn_lambda_k2': nrm(15, (N_ATTN_LAYERS, HEAD_DIM), 0.1),
        'attn_subln_g': 1.0 + nrm(16, (N_ATTN_LAYERS, V_DIM), 0.02),
        'conv_w_pw1': nrm(17, (N_CONV_LAYERS, D, 2 * D), D ** -0.5),
        'conv_b_pw1': nrm(18, (N_CONV_LAYERS, 2 * D), 0.01),
        'conv_w_dw': nrm(19, (N_CONV_LAYERS, CONV_WIDTH, D), CONV_WIDTH ** -0.5),
        'conv_b_dw': nrm(20, (N_CONV_LAYERS, D), 0.01),
        'conv_ln_g': 1.0 + nrm(21, (N_CONV_LAYERS, D), 0.02),
        'conv_ln_b': nrm(22, (N_CONV_LAYERS, D), 0.01),
        'conv_w_pw2': nrm(23, (N_CONV_LAYERS, D, D), D ** -0.5),
        'conv_b_pw2': nrm(24, (N_CONV_LAYERS, D), 0.01),
        'router_w': nrm(25, (D, N_EXPERTS), D ** -0.5),
        'router_bias': nrm(26, (N_EXPERTS,), 0.01),
        'moe_w_gate': nrm(27, (DEPTH, N_EXPERTS, D, D_EXPERT), D ** -0.5),
        'moe_w_up': nrm(28, (DEPTH, N_EXPERTS, D, D_EXPERT), D ** -0.5),
        'moe_w_down': nrm(29, (DEPTH, N_EXPERTS, D_EXPERT, D), D_EXPERT ** -0.5),
        'final_norm_g': 1.0 + nrm(30, (D,), 0.02),
    }

def reference(x_prompt, x_sample, cache_k, cache_v, c, c_ctx, norm1_g, norm2_g, ada_w, ada_b,
              attn_w_qkv, attn_w_o, attn_lambda_q1, attn_lambda_k1, attn_lambda_q2, attn_lambda_k2,
              attn_subln_g, conv_w_pw1, conv_b_pw1, conv_w_dw, conv_b_dw, conv_ln_g, conv_ln_b,
              conv_w_pw2, conv_b_pw2, router_w, router_bias, moe_w_gate, moe_w_up, moe_w_down,
              final_norm_g):
    xc = x_prompt
    xl = x_sample
    b_ctx, t_ctx = xc.shape[:2]
    b_lat, t_lat = xl.shape[:2]
    cond_ctx = c_ctx[None, None, :]
    cond_lat = c[:, None, :]
    cos, sin = axial_rope_tables(t_lat)
    new_k, new_v = [], []

    for layer in range(DEPTH):
        mc = modulation(cond_ctx, ada_w[layer], ada_b[layer])
        ml = modulation(cond_lat, ada_w[layer], ada_b[layer])
        hc = modulate(rmsnorm(xc, norm1_g[layer]), mc[0], mc[1])
        hl = modulate(rmsnorm(xl, norm1_g[layer]), ml[0], ml[1])
        j = layer // N_MIXERS
        if layer % N_MIXERS == 0:
            lambda_init = 0.8 - 0.6 * math.exp(-0.3 * layer)
            lam = (jnp.exp(jnp.sum(attn_lambda_q1[j].astype(jnp.float32) * attn_lambda_k1[j].astype(jnp.float32)))
                   - jnp.exp(jnp.sum(attn_lambda_q2[j].astype(jnp.float32) * attn_lambda_k2[j].astype(jnp.float32)))
                   + lambda_init)
            qc, kc, vc = diff_attn_project(hc, attn_w_qkv[j])
            oc = diff_attention_core(qc, kc, vc, lam)
            new_k.append(kc.reshape(b_ctx, t_ctx, N_HEADS, 2 * HEAD_DIM))
            new_v.append(vc)
            ql, kl, vl = diff_attn_project(hl, attn_w_qkv[j])
            ql = apply_axial_rope(ql, cos, sin)
            kl = apply_axial_rope(kl, cos, sin)
            past = cache_k.shape[2]
            k_all = jnp.concatenate(
                [cache_k[:, j].reshape(b_lat, past, N_HEADS, 2, HEAD_DIM).astype(kl.dtype), kl], axis=1)
            v_all = jnp.concatenate([cache_v[:, j].astype(vl.dtype), vl], axis=1)
            ol = diff_attention_core(ql, k_all, v_all, lam)
            mix_c = diff_attn_output(oc, attn_subln_g[j], attn_w_o[j], lambda_init)
            mix_l = diff_attn_output(ol, attn_subln_g[j], attn_w_o[j], lambda_init)
        else:
            conv_args = (conv_w_pw1[j], conv_b_pw1[j], conv_w_dw[j], conv_b_dw[j],
                         conv_ln_g[j], conv_ln_b[j], conv_w_pw2[j], conv_b_pw2[j])
            mix_c = conformer_conv(hc, *conv_args)
            mix_l = conformer_conv(hl, *conv_args)
        xc = xc + mc[2] * mix_c
        xl = xl + ml[2] * mix_l

        hc = modulate(rmsnorm(xc, norm2_g[layer]), mc[3], mc[4])
        hl = modulate(rmsnorm(xl, norm2_g[layer]), ml[3], ml[4])
        xc = xc + mc[5] * grouped_moe(hc, router_w, router_bias, moe_w_gate[layer], moe_w_up[layer], moe_w_down[layer])
        xl = xl + ml[5] * grouped_moe(hl, router_w, router_bias, moe_w_gate[layer], moe_w_up[layer], moe_w_down[layer])

    y_prompt = rmsnorm(xc, final_norm_g)
    y_sample = rmsnorm(xl, final_norm_g)
    new_cache_k = jnp.stack(new_k, axis=1)
    new_cache_v = jnp.stack(new_v, axis=1)
    return (y_prompt, y_sample, new_cache_k, new_cache_v)


_drawn_inputs = setup_inputs


def setup_inputs(seed=0):
    import zlib

    import numpy as np

    out = dict(_drawn_inputs(seed))
    spreads = {}
    factors = {'norm1_g': 2.8,
     'attn_lambda_q2': 8.396,
     'attn_subln_g': 3.379,
     'conv_b_pw1': 18.183,
     'conv_b_dw': 11.588,
     'conv_ln_g': 10.573,
     'conv_ln_b': 30.456,
     'conv_b_pw2': 8.0,
     'final_norm_g': 7.506,
     'cache_k': 8.0,
     'cache_v': 8.0}
    for name, (base, spread) in spreads.items():
        noise = np.random.default_rng([zlib.crc32(name.encode()), seed]).standard_normal(out[name].shape)
        drawn = base * np.exp(spread * noise) if base else spread * noise
        out[name] = jnp.asarray(drawn.astype(out[name].dtype))
    for name, factor in factors.items():
        out[name] = (out[name] * factor).astype(out[name].dtype)
    return out
```

```python
from contextlib import ExitStack

import numpy as np

import concourse.bass as bass
from concourse import mybir

F32 = mybir.dt.float32
F32R = mybir.dt.float32r
I32 = mybir.dt.int32
ALU = mybir.AluOpType
ACT = mybir.ActivationFunctionType
AX = mybir.AxisListType.X

P = 128
D = 1024
DC = D // P
T = 128
HT = T // 2
NH = 8
HD = 64
NE = 16
NG = 4
FE = 512
FC = FE // P
KW = 31
PAD = KW // 2
EPS = 1e-6
LAMBDA_INIT = 0.2
SLOTS = 64
CAP = 64
OVER = 3
FAR = 4096.0
BIG = 1e30

RING = 12
SPLIT = 3
ADA_BLOCKS = 24
QKV_BLOCKS = 12
WO_BLOCKS = 4
PW1_BLOCKS = 8
PW2_BLOCKS = 4
MOE_BLOCKS = 96
MIX0_BLOCKS = ADA_BLOCKS + QKV_BLOCKS + WO_BLOCKS
MIX1_BLOCKS = ADA_BLOCKS + PW1_BLOCKS + PW2_BLOCKS
BASE_MIX = [0, MIX0_BLOCKS + MOE_BLOCKS]
BASE_MOE = [MIX0_BLOCKS, MIX0_BLOCKS + MOE_BLOCKS + MIX1_BLOCKS]

C_ID, C_ONE, C_TRI, C_SLOT, C_COS, C_SIN, C_PR4, C_PR16 = 0, 128, 256, 384, 512, 544, 576, 580
C_OVER = 596
C_ALL = C_OVER + 64
MIX_END = [MIX0_BLOCKS, MIX0_BLOCKS + MIX1_BLOCKS]
CONV_DVE = DC
OV_DVE, OV_PE = 18, 5
QK_ITEMS = [(2, 0, 0), (2, 0, 1), (1, 0, 0), (1, 0, 1), (0, 0, 0), (0, 0, 1),
            (0, 1, 0), (0, 1, 1), (1, 1, 0), (1, 1, 1)]
R_ADA = [0, 12]
R_G1 = [24, 26]
R_G2 = [28, 30]
R_FIN = 32
R_PW2 = 34
R_ALL = 36
V_BPW1, V_BDW, V_LNG, V_LNB, V_SUB, V_ALL = 0, 16, 24, 32, 40, 41


def constants():
    c = np.zeros((P, C_ALL), np.float32)
    c[:, C_ID:C_ID + P] = np.eye(P)
    c[:, C_ONE:C_ONE + P] = 1.0
    c[:, C_TRI:C_TRI + P] = np.triu(np.ones((P, P)), 1)
    slot = np.arange(P) % SLOTS
    c[:, C_SLOT:C_SLOT + P] = np.where(slot < CAP, slot, -1.0)
    c[:, C_OVER:C_OVER + SLOTS] = np.arange(SLOTS) + CAP
    grid_w = 64
    rows = np.repeat(np.arange(T // grid_w, dtype=np.float32), grid_w)
    cols = np.tile(np.arange(grid_w, dtype=np.float32), T // grid_w)
    n_freq = HD // 4
    inv = (np.float32(10000.0) ** (-np.arange(n_freq, dtype=np.float32) / np.float32(n_freq))).astype(np.float32)
    ang = np.stack([rows[:, None] * inv, cols[:, None] * inv], axis=1).astype(np.float32)
    c[:, C_COS:C_COS + 32] = np.cos(ang).reshape(T, 32)
    c[:, C_SIN:C_SIN + 32] = np.sin(ang).reshape(T, 32)
    c[:, C_PR4:C_PR4 + NG] = np.arange(NG, 0, -1)
    c[:, C_PR16:C_PR16 + NE] = np.arange(NE, 0, -1)
    return c


def block_of(e, j):
    return j if e == 0 else 6 * e - 2 + j


def trunk_kernel(nc, a, y_prompt, y_sample, new_k, new_v):
    ctx = ExitStack()
    with ctx:
        base = 16512
        place = [base]

        def at(name, off, shape, dt=F32):
            return nc.alloc_sbuf_tensor_at(name, shape, dt, offset=off)

        def take(n_bytes):
            off = place[0]
            place[0] += (n_bytes + 31) // 32 * 32
            return off

        def sb(name, shape, dt=F32):
            return at(name, take(4 * int(np.prod(shape[1:]))), shape, dt)

        ring = sb("ring", [P, RING, 4, 512])
        split_at = take(2 * SPLIT * 8192)
        w_hi = at("w_hi", split_at, [P, SPLIT, 4, 512], F32R)
        w_lo = at("w_lo", split_at + SPLIT * 8192, [P, SPLIT, 4, 512], F32R)
        x = sb("x", [P, 2, D])
        h = sb("h", [P, 2, D])
        mod_at = take(6 * 4096)
        mod = at("mod", mod_at, [P, 6, D])
        hT_at = take(8192)
        hT = at("hT", hT_at, [P, DC, 2, T])
        hTm = at("hTm", hT_at, [P, DC, 2, P])
        moe_tmp = at("moe_tmp", hT_at, [P, 4, 512])
        condT = at("condT", hT_at, [P, DC, P])
        xs = at("xs", hT_at, [P, 2, DC, P], F32R)
        yh = at("yh", mod_at, [P, 2, 512], F32R)
        yl = at("yl", mod_at + 4096, [P, 2, 512], F32R)
        g_lo = at("g_lo", mod_at + 8192, [SLOTS, FE])
        g_sum = at("g_sum", mod_at + 10240, [SLOTS, FE])
        g_silu = at("g_silu", mod_at + 12288, [SLOTS, FE])
        u_lo = at("u_lo", mod_at + 14336, [SLOTS, FE])
        u_sum = at("u_sum", mod_at + 16384, [SLOTS, FE])
        act = at("act", mod_at + 18432, [P, FE])
        moe_at = take(2048 + 1024 + 2048)
        actT = at("actT", moe_at, [P, FC, P], F32R)
        selT = at("selT", moe_at + 2048, [P, 2, P], F32R)
        p2 = at("p2", moe_at + 3072, [P, 2, 2, P])
        cache_v_sb = at("cache_v_sb", moe_at, [P, D])
        qkv = at("qkv", split_at, [P, 2, 3 * D])
        qT = at("qT", split_at + 24576, [P, NH, 2, T])
        kT = at("kT", split_at + 32768, [P, NH, 2, T])
        cache_k_sb = at("cache_k_sb", split_at + 40960, [P, D])
        ckT = at("ckT", split_at + 45056, [P, NH, T])
        probs = at("probs", split_at, [P, 2, 512])
        probsT = at("probsT", split_at + 12288, [P, 2, 2, P])
        rope_tmp = at("rope_tmp", split_at + 24576, [P, 2, 32, 2, 16])
        oT = at("oT", split_at + 24576, [P, NH, 2, P])
        o_sq = at("o_sq", split_at + 32768, [P, 2, D])
        u_pad = at("u_pad", split_at, [P, DC, 2, T + 2 * PAD])
        conv = at("conv", split_at + 10112, [P, DC, 2, T])
        conv_sq = at("conv_sq", split_at + 18304, [P, DC, 2, T])
        conv_act = at("conv_act", split_at + 26496, [P, DC, 2, 2, HT])
        mean = at("mean", split_at + 34688, [P, 2 * T])
        rstd_c = at("rstd_c", split_at + 35712, [P, 2 * T])
        sig = at("sig", split_at + 36736, [P, 2, 2 * T])
        wdw_rows = at("wdw_rows", split_at + 38784, [KW, D])
        over_w = at("over_w", split_at, [P, 6, 4, 512])
        over_p = at("over_p", moe_at, [P, 2, SLOTS])
        over_pT = at("over_pT", moe_at + 512, [SLOTS, 2, P])
        over_x = at("over_x", hT_at, [P, DC, SLOTS])
        over_aT = at("over_aT", hT_at + 2048, [P, FC, SLOTS])
        over_y = at("over_y", mod_at, [SLOTS, D])
        over_t = at("over_t", mod_at + 4096, [P, 2, D])
        over_g = at("over_g", mod_at + 12288, [P, 2, FE])
        cst = sb("cst", [P, C_ALL])
        rows = sb("rows", [R_ALL, 512])
        router = sb("router", [P, DC, NE])
        bias_b = sb("bias_b", [P, NE])
        chan_rows = sb("chan_rows", [V_ALL, P])
        chan = sb("chan", [P, V_ALL])
        wdw = sb("wdw", [P, DC, KW])
        cond = sb("cond", [P, 2, DC])
        silu_c = sb("silu_c", [P, 2, DC])
        lam_in = sb("lam_in", [P, 4, HD])
        lam = sb("lam", [P, 8])
        stat = sb("stat", [P, 72])
        asg = sb("asg", [P, 2, NE])
        rs = sb("rs", [P, 12, 2 * NE])
        pos = sb("pos", [P, 2, NE])
        gates = sb("gates", [P, 2, NE])
        gate_tok = sb("gate_tok", [P, 2, 2])
        gate_slot = sb("gate_slot", [P, 1])
        flag = sb("flag", [P, 2], I32)
        assert place[0] <= nc.sbuf_usable_end, place[0]

        ident = cst[:, C_ID:C_ID + P]
        ones = cst[:, C_ONE:C_ONE + P]
        bank = [ctx.enter_context(nc.psum_tensor(f"bank{i}", [P, 512], F32)) for i in range(8)]
        ACC, G, U, DN, X = bank[0:4], bank[4], bank[5], bank[6], bank[7]

        def sem(name):
            return ctx.enter_context(nc.semaphore(name))

        landed = [sem(f"landed{i}") for i in range(RING)]
        pe_used = sem("pe_used")
        hi_done, lo_done = sem("hi_done"), sem("lo_done")
        split_used = sem("split_used")
        in_cst, in_x, in_vec = sem("in_cst"), sem("in_x"), sem("in_vec")
        in_cache_k, in_cache_v, in_wdw = sem("in_cache_k"), sem("in_cache_v"), sem("in_wdw")
        out_kv, out_y = sem("out_kv"), sem("out_y")
        act_chain, dve_chain = sem("act_chain"), sem("dve_chain")
        cond_silu, condT_ready = sem("cond_silu"), sem("condT_ready")
        ada_evac, ada_gmm, ada_gcopy = sem("ada_evac"), sem("ada_gmm"), sem("ada_gcopy")
        chan_mm, chan_ready = sem("chan_mm"), sem("chan_ready")
        lam_sums, lam_exp = sem("lam_sums"), sem("lam_exp")
        ssq, ms_ready, rms_ready, h_ready = sem("ssq"), sem("ms_ready"), sem("rms_ready"), sem("h_ready")
        hT_mm, hT_act, hT_dve = sem("hT_mm"), sem("hT_act"), sem("hT_dve")
        x_mix, x_add, x_moe = sem("x_mix"), sem("x_add"), sem("x_moe")
        qkv_c, qkv_l, roped = sem("qkv_c"), sem("qkv_l"), sem("roped")
        qk_mm, qkT_act, qkT_dve = sem("qk_mm"), sem("qkT_act"), sem("qkT_dve")
        scores_mm, max_done, exp_done = sem("scores_mm"), sem("max_done"), sem("exp_done")
        combined, pT_mm, pT_evac = sem("combined"), sem("pT_mm"), sem("pT_evac")
        pv_mm, o_evac, o_normed, oT_mm, oT_evac = (sem("pv_mm"), sem("o_evac"), sem("o_normed"),
                                                   sem("oT_mm"), sem("oT_evac"))
        sub_ms, sub_rms = sem("sub_ms"), sem("sub_rms")
        wdw_mm, wdw_ready, sig_done, u_done = sem("wdw_mm"), sem("wdw_ready"), sem("sig_done"), sem("u_done")
        pads_zero, conv_dve = sem("pads_zero"), sem("conv_dve")
        sum_mm, centred, squared, var_mm = sem("sum_mm"), sem("centred"), sem("squared"), sem("var_mm")
        var_ready, std_ready, scaled, conv_silu = (sem("var_ready"), sem("std_ready"), sem("scaled"),
                                                   sem("conv_silu"))
        logits_mm, scores_ready, assigned, pos_mm, routed = (
            sem("logits_mm"), sem("scores_ready"), sem("assigned"), sem("pos_mm"), sem("routed"))
        p2_built, gathered, xs_hi, xs_lo = sem("p2_built"), sem("gathered"), sem("xs_hi"), sem("xs_lo")
        g_low, g_folded = sem("g_low"), sem("g_folded")
        u_low, u_folded, silu_done = sem("u_low"), sem("u_folded"), sem("silu_done")
        sel_mm, sel_evac, act_done, actT_mm = sem("sel_mm"), sem("sel_evac"), sem("act_done"), sem("actT_mm")
        as_hi, as_lo = sem("as_hi"), sem("as_lo")
        yh_done, yl_done, scat = sem("yh_done"), sem("yl_done"), sem("scat")
        over = [{n: sem(f"over{k}_{n}") for n in ("w", "pe", "act", "dve")} for k in range(2)]
        fin_mm = sem("fin_mm")

        block = ctx.enter_context(nc.Block())

        def wait_block(eng, n, i=None):
            v = 16 * (n // RING + 1)
            eng.wait_ge(landed[n % RING], v if i is None else i * 16 + v)

        def lin(i, per_i, const):
            return const if i is None else i * per_i + const

        def ada_block(layer, n):
            src = a["ada_w"][layer].rearrange("(p c) n -> p c n", c=DC)
            g, hf = n // 2, n % 2
            return src[:, 4 * hf:4 * hf + 4, g * 512:(g + 1) * 512]

        def qkv_block(n):
            src = a["attn_w_qkv"][0].rearrange("(p c) n -> p c n", c=DC)
            g, hf = n // 2, n % 2
            return src[:, 4 * hf:4 * hf + 4, g * 512:(g + 1) * 512]

        def wo_block(n):
            src = a["attn_w_o"][0].rearrange("(c p) n -> p c n", p=P)
            g, hf = n // 2, n % 2
            return src[:, 4 * hf:4 * hf + 4, g * 512:(g + 1) * 512]

        PW1_ORDER = [0, 2, 1, 3]

        def pw1_block(n):
            src = a["conv_w_pw1"][0].rearrange("(p c) n -> p c n", c=DC)
            g, hf = PW1_ORDER[n // 2], n % 2
            return src[:, 4 * hf:4 * hf + 4, g * 512:(g + 1) * 512]

        def pw2_block(n):
            src = a["conv_w_pw2"][0].rearrange("(c p) n -> p c n", p=P)
            g, hf = n // 2, n % 2
            return src[:, 4 * hf:4 * hf + 4, g * 512:(g + 1) * 512]

        def expert_block(layer, e, j):
            if j < 4:
                src = a["moe_w_gate" if j < 2 else "moe_w_up"][layer, e].rearrange("(p c) f -> p c f", c=DC)
                return src[:, 4 * (j % 2):4 * (j % 2) + 4, :]
            src = a["moe_w_down"][layer, e].rearrange("(p c) n -> p c n", c=FC)
            return src[:, :, 512 * (j - 4):512 * (j - 4) + 512]

        def mixed(dram, t, g):
            return dram[t * HT:(t + 1) * HT, :]

        xp, xl = a["x_prompt"][0], a["x_sample"][0]

        def evac_transposed(copy, ni, t, q):
            src = bank[2 * t + q][:, :]
            if ni % 2:
                return copy(hTm[:, 4 * q:4 * q + 4, t, :], src.rearrange("p (c i) -> p c i", c=4))
            return copy(hT[:, 4 * q:4 * q + 4, :, t * HT:(t + 1) * HT],
                        src.rearrange("p (c g i) -> p c g i", c=4, g=2))

        def qk_target(m):
            what, g, q = QK_ITEMS[m]
            return (ckT[:, 4 * q:4 * q + 4, :] if what == 2
                    else (qT, kT)[what][:, 4 * q:4 * q + 4, g, :])

        SMALL = [
            (cond[:, 0, :], a["c_ctx"].rearrange("(p c) -> p c", c=DC)),
            (cond[:, 1, :], a["c"][0].rearrange("(p c) -> p c", c=DC)),
            (rows[0:24, :], a["ada_b"].rearrange("l (r n) -> (l r) n", n=512)),
            (rows[24:28, :], a["norm1_g"].rearrange("l (r n) -> (l r) n", n=512)),
            (rows[28:32, :], a["norm2_g"].rearrange("l (r n) -> (l r) n", n=512)),
            (rows[32:34, :], a["final_norm_g"].rearrange("(r n) -> r n", n=512)),
            (rows[34:36, :], a["conv_b_pw2"][0].rearrange("(r n) -> r n", n=512)),
            (chan_rows[0:16, :], a["conv_b_pw1"][0].rearrange("(r n) -> r n", n=P)),
            (chan_rows[16:24, :], a["conv_b_dw"][0].rearrange("(r n) -> r n", n=P)),
            (chan_rows[24:32, :], a["conv_ln_g"][0].rearrange("(r n) -> r n", n=P)),
            (chan_rows[32:40, :], a["conv_ln_b"][0].rearrange("(r n) -> r n", n=P)),
            (chan_rows[40:41, :], a["attn_subln_g"]),
            (router[:, :, :], a["router_w"].rearrange("(p c) e -> p c e", c=DC)),
            (bias_b[:, :], a["router_bias"].partition_broadcast(P)),
            (lam_in[:, 0, :], a["attn_lambda_q1"][0].partition_broadcast(P)),
            (lam_in[:, 1, :], a["attn_lambda_k1"][0].partition_broadcast(P)),
            (lam_in[:, 2, :], a["attn_lambda_q2"][0].partition_broadcast(P)),
            (lam_in[:, 3, :], a["attn_lambda_k2"][0].partition_broadcast(P)),
        ]
        IN_VEC = 16 * len(SMALL)

        @block.sync
        def _(sp):
            def load(n, src, i=None):
                sp.dma_start(ring[:, n % RING, :, :], src).then_inc(landed[n % RING], 16)

            def free_mix(m):
                sp.wait_ge(pe_used, m + 1 if m < MIX0_BLOCKS else m + 1 - MOE_BLOCKS)

            def free(n):
                if n < 0:
                    return
                for layer in range(2):
                    if BASE_MOE[layer] <= n < BASE_MOE[layer] + MOE_BLOCKS:
                        sp.wait_ge(lo_done, MOE_BLOCKS * layer + n - BASE_MOE[layer] + 1)
                        return
                free_mix(n)

            def moe_stream(layer):
                def expert_step(e0, i=None):
                    e = lin(i, 2, e0)
                    for j in range(6):
                        if (j >= 4 and e0 == 0) or (j < 4 and e0 == NE):
                            continue
                        k = block_of(e0, j if e0 < NE else j - 4)
                        n = BASE_MOE[layer] + k
                        if i is None:
                            free(n - RING)
                        else:
                            sp.wait_ge(lo_done, i * RING + MOE_BLOCKS * layer + k - RING + 1)
                        load(n, expert_block(layer, e if j < 4 else e - 1, j))

                for e0 in range(4):
                    expert_step(e0)
                with sp.Fori(0, 5) as i:
                    for e0 in (4, 5):
                        expert_step(e0, i)
                for e0 in range(14, NE + 1):
                    expert_step(e0)

            def overflow(layer):
                sp.wait_ge(routed, 3 * layer + 3)
                n_over = sp.value_load(flag[0:1, 0:1], min_val=0, max_val=1)
                with sp.If(n_over > 0):
                    o = over[layer]
                    for r in range(OVER):
                        with sp.Fori(0, NE) as e:
                            sp.wait_ge(o["dve"], e * OV_DVE + (r * NE * OV_DVE + 1))
                            for j in range(6):
                                sp.dma_start(over_w[:, j, :, :], expert_block(layer, e, j)).then_inc(o["w"], 16)

            for n in range(ADA_BLOCKS):
                free(n - RING)
                load(n, ada_block(0, n))
            for n in range(QKV_BLOCKS):
                free(ADA_BLOCKS + n - RING)
                load(ADA_BLOCKS + n, qkv_block(n))
            for n in range(WO_BLOCKS):
                free(ADA_BLOCKS + QKV_BLOCKS + n - RING)
                load(ADA_BLOCKS + QKV_BLOCKS + n, wo_block(n))
            moe_stream(0)
            overflow(0)
            b = BASE_MIX[1]
            for n in range(ADA_BLOCKS):
                free(b + n - RING)
                load(b + n, ada_block(1, n))
            b += ADA_BLOCKS
            for n in range(PW1_BLOCKS):
                free(b + n - RING)
                load(b + n, pw1_block(n))
            b += PW1_BLOCKS
            for n in range(PW2_BLOCKS):
                free(b + n - RING)
                load(b + n, pw2_block(n))
            moe_stream(1)
            overflow(1)
            sp.wait_ge(h_ready, 10)
            for t in range(2):
                sp.dma_start(mixed(y_prompt[0], t, 0), h[0:HT, t, :]).then_inc(out_y, 16)
                sp.dma_start(mixed(y_sample[0], t, 1), h[HT:P, t, :]).then_inc(out_y, 16)
            sp.wait_ge(out_y, 64)
            sp.wait_ge(out_kv, 32)

        @block.tensor
        def _(pe):
            def row_bcast(out, r, stop):
                return pe.matmul(out, ident[0:R_ALL, r:r + 1].broadcast_to([R_ALL, P]), rows[:, :],
                                 start=True, stop=stop)

            def adaln(layer):
                pe.wait_ge(condT_ready, 2 * layer + 2)
                if layer:
                    pe.wait_ge(x_moe, layer)
                for i in range(2):
                    for j in range(6):
                        n = 6 * i + j
                        if i:
                            pe.wait_ge(ada_evac, 12 * layer + j + 1)
                        row_bcast(bank[j][:, :], R_ADA[layer] + n, False)
                        for c in range(DC):
                            b = BASE_MIX[layer] + 2 * n + c // 4
                            if c % 4 == 0:
                                wait_block(pe, b)
                            mm = pe.matmul(bank[j][:, :], condT[:, c, :], ring[:, b % RING, c % 4, :],
                                           start=False, stop=(c == DC - 1))
                            if c % 4 == 3:
                                mm.then_inc(pe_used, 1)
                        if j in (2, 3):
                            if i or layer:
                                pe.wait_ge(ada_gcopy, 4 * layer + 2 * i + j - 3)
                            row = (R_G2 if i else R_G1)[layer] + j - 2
                            row_bcast(bank[4 + j][:, :], row, True).then_inc(ada_gmm, 1)

            def transpose_h(ni):
                for t in range(2):
                    pe.wait_ge(h_ready, 2 * ni + t + 1)
                    for q in range(2):
                        for k in range(4):
                            c = 4 * q + k
                            mm = pe.transpose(bank[2 * t + q][:, k * P:(k + 1) * P],
                                              h[:, t, c::DC], ident)
                        mm.then_inc(hT_mm, 1)
                pe.wait_ge(hT_act, 2 * ni + 2)
                pe.wait_ge(hT_dve, 2 * ni + 2)

            def qkv_proj():
                for n in range(6):
                    if n >= 2:
                        pe.wait_ge(qkv_c, n - 1)
                        pe.wait_ge(qkv_l, n - 1)
                    for hf in range(2):
                        b = ADA_BLOCKS + 2 * n + hf
                        wait_block(pe, b)
                        for k in range(4):
                            for g in range(2):
                                c = 4 * hf + k
                                mm = pe.matmul(bank[4 + 2 * (n % 2) + g][:, :], hT[:, c, g, :],
                                               ring[:, b % RING, k, :], start=(c == 0), stop=(c == DC - 1))
                        mm.then_inc(pe_used, 1)

            def qk_transposes():
                pe.wait_ge(qkv_c, 6)
                pe.wait_ge(in_cache_k, 16)
                for m, (what, g, q) in enumerate(QK_ITEMS):
                    if g == 1:
                        pe.wait_ge(roped, 1)
                    if m >= 4:
                        pe.wait_ge(qkT_act if m % 2 == 0 else qkT_dve, (m - 4) // 2 + 1)
                    for k in range(4):
                        hd = 4 * q + k
                        src = (cache_k_sb[:, hd * P:(hd + 1) * P] if what == 2
                               else qkv[:, g, what * D + hd * P:what * D + (hd + 1) * P])
                        mm = pe.transpose(bank[m % 4][:, k * P:(k + 1) * P], src, ident)
                    mm.then_inc(qk_mm, 1)
                pe.wait_ge(qkT_act, len(QK_ITEMS) // 2)
                pe.wait_ge(qkT_dve, len(QK_ITEMS) // 2)
                pe.wait_ge(qkv_l, 6)
                pe.wait_ge(in_cache_v, 16)

            def scores(un):
                hd, g = un // 2, un % 2
                if un >= 2:
                    pe.wait_ge(exp_done, 2 * (un - 1))
                for m in range(2):
                    out = bank[4 + 2 * (un % 2) + m]
                    q = qT[HD * m:HD * m + HD, hd, g, :]
                    if g == 1:
                        pe.matmul(out[:, 0:P], q, ckT[HD * m:HD * m + HD, hd, :], start=True, stop=True)
                    mm = pe.matmul(out[:, g * P:(g + 1) * P], q, kT[HD * m:HD * m + HD, hd, g, :],
                                   start=True, stop=True)
                mm.then_inc(scores_mm, 1)

            def probs_transpose(un):
                g = un % 2
                pe.wait_ge(combined, un + 1)
                if un >= 2:
                    pe.wait_ge(pT_evac, un - 1)
                for kc in range(g + 1):
                    mm = pe.transpose(bank[un % 2][:, kc * P:(kc + 1) * P],
                                      probs[:, un % 2, kc * P:(kc + 1) * P], ident)
                mm.then_inc(pT_mm, 1)

            def pv(un):
                hd, g = un // 2, un % 2
                pe.wait_ge(pT_evac, un + 1)
                if un >= 2:
                    pe.wait_ge(o_evac, un - 1)
                for kc in range(g + 1):
                    val = (cache_v_sb[:, hd * P:(hd + 1) * P] if kc < g
                           else qkv[:, g, 2 * D + hd * P:2 * D + (hd + 1) * P])
                    mm = pe.matmul(bank[2 + un % 2][:, 0:P], probsT[:, un % 2, kc, :], val,
                                   start=(kc == 0), stop=(kc == g))
                mm.then_inc(pv_mm, 1)

            def attention():
                qkv_proj()
                qk_transposes()
                for un in range(2 * NH + 2):
                    if un < 2 * NH:
                        scores(un)
                    if 1 <= un <= 2 * NH:
                        probs_transpose(un - 1)
                    if un >= 2:
                        pv(un - 2)
                pe.wait_ge(o_normed, 1)
                pe.wait_ge(pT_evac, 2 * NH)
                for g in range(2):
                    for q in range(2):
                        for k in range(4):
                            hd = 4 * q + k
                            mm = pe.transpose(bank[2 * g + q][:, k * P:(k + 1) * P],
                                              h[:, g, hd * P:(hd + 1) * P], ident)
                        mm.then_inc(oT_mm, 1)
                pe.wait_ge(oT_evac, 4)
                for n in range(2):
                    for hf in range(2):
                        b = ADA_BLOCKS + QKV_BLOCKS + 2 * n + hf
                        wait_block(pe, b)
                        for k in range(4):
                            for t in range(2):
                                c = 4 * hf + k
                                mm = pe.matmul(bank[4 + 2 * n + t][:, :], oT[:, c, t, :],
                                               ring[:, b % RING, k, :], start=(c == 0), stop=(c == DC - 1))
                        mm.then_inc(pe_used, 1)

            def convolution():
                b0 = BASE_MIX[1] + ADA_BLOCKS
                for n in range(4):
                    b = b0 + 2 * n
                    wait_block(pe, b)
                    wait_block(pe, b + 1)
                    if n == 2:
                        pe.wait_ge(wdw_ready, 1)
                    for k in range(4):
                        for c in range(DC):
                            mm = pe.matmul(bank[2 * n + k // 2][:, (k % 2) * 256:(k % 2) * 256 + 256],
                                           ring[:, (b + c // 4) % RING, c % 4, k * P:(k + 1) * P],
                                           hT[:, c, :, :], start=(c == 0), stop=(c == DC - 1))
                            if k == 3 and c % 4 == 3:
                                mm.then_inc(pe_used, 1)
                pe.wait_ge(conv_dve, CONV_DVE * KW)
                for c in range(DC):
                    mm = pe.matmul(bank[0][:, 0:256], ones, conv[:, c, :, :], start=(c == 0), stop=(c == DC - 1))
                mm.then_inc(sum_mm, 1)
                pe.wait_ge(squared, 1)
                for c in range(DC):
                    mm = pe.matmul(bank[1][:, 0:256], ones, conv_sq[:, c, :, :], start=(c == 0),
                                   stop=(c == DC - 1))
                mm.then_inc(var_mm, 1)
                pe.wait_ge(conv_silu, DC)
                for n in range(2):
                    for t in range(2):
                        row_bcast(bank[4 + 2 * n + t][:, :], R_PW2 + n, False)
                    for hf in range(2):
                        b = b0 + PW1_BLOCKS + 2 * n + hf
                        wait_block(pe, b)
                        for k in range(4):
                            for t in range(2):
                                c = 4 * hf + k
                                mm = pe.matmul(bank[4 + 2 * n + t][:, :], conv_act[:, c, t, :, :],
                                               ring[:, b % RING, k, :], start=False, stop=(c == DC - 1))
                        mm.then_inc(pe_used, 1)

            def routing(layer):
                pe.wait_ge(x_mix, 4 * layer + 4)
                for t in range(2):
                    for c in range(DC):
                        mm = pe.matmul(G[:, t * NE:(t + 1) * NE], hTm[:, c, t, :], router[:, c, :],
                                       start=(c == 0), stop=(c == DC - 1))
                mm.then_inc(logits_mm, 1)
                pe.wait_ge(assigned, layer + 1)
                tri = cst[:, C_TRI:C_TRI + P]
                pe.matmul(U[:, 0:NE], tri, asg[:, 0, :], start=True, stop=True)
                pe.matmul(U[:, NE:2 * NE], ones, asg[:, 0, :], start=True, stop=False)
                pe.matmul(U[:, NE:2 * NE], tri, asg[:, 1, :], start=False, stop=True)
                pe.matmul(U[:, 2 * NE:3 * NE], ones, asg[:, 0, :], start=True, stop=False)
                pe.matmul(U[:, 2 * NE:3 * NE], ones, asg[:, 1, :], start=False, stop=True).then_inc(pos_mm, 1)

            def experts(layer):
                eo, ko = NE * layer, MOE_BLOCKS * layer

                def gather(e0, i=None):
                    par = e0 % 2
                    pe.wait_ge(p2_built, lin(i, 6, 3 * (eo + e0 + 1)))
                    for c in range(DC):
                        for t in range(2):
                            mm = pe.matmul(X[:, c * SLOTS:(c + 1) * SLOTS], h[:, t, c::DC],
                                           p2[:, par, t, 0:SLOTS], start=(t == 0), stop=(t == 1))
                    mm.then_inc(gathered, 1)

                def split_product(out, lhs, k0, k_i, i, chunks, first, last):
                    slot = k0 % SPLIT
                    pe.wait_ge(lo_done, lin(i, RING, ko + k0 + 1))
                    for c in range(4):
                        for part, w in enumerate((w_hi, w_lo)):
                            mm = pe.matmul(out, lhs(chunks + c), w[:, slot, c, :],
                                           start=(first and c == 0 and part == 0),
                                           stop=(last and c == 3 and part == 1))
                            if c == 3 and part == 1:
                                mm.then_inc(split_used, 1)

                def expert_step(e0, i=None):
                    par, prev = e0 % 2, 1 - e0 % 2
                    if e0 < NE:
                        pe.wait_ge(xs_lo, lin(i, 2, eo + e0 + 1))
                        if eo + e0:
                            pe.wait_ge(g_folded, lin(i, 2, eo + e0))
                        for q in range(2):
                            split_product(G[:, :], lambda c: xs[:, par, c, :], block_of(e0, q), RING, i,
                                          4 * q, q == 0, q == 1)
                    if e0:
                        pe.wait_ge(act_done, lin(i, 2, eo + e0))
                        pe.wait_ge(sel_evac, lin(i, 4, 2 * (eo + e0)))
                        for c in range(FC):
                            mm = pe.transpose(X[:, c * P:(c + 1) * P], act[:, c::FC], ident)
                        mm.then_inc(actT_mm, 1)
                    if e0 < NE:
                        if eo + e0:
                            pe.wait_ge(u_folded, lin(i, 2, eo + e0))
                        for q in range(2):
                            split_product(U[:, :], lambda c: xs[:, par, c, :], block_of(e0, 2 + q), RING, i,
                                          4 * q, q == 0, q == 1)
                    for hf in range(2):
                        if e0:
                            k0 = block_of(e0, (4 if e0 < NE else 0) + hf)
                            if hf == 0:
                                pe.wait_ge(as_lo, lin(i, 2, eo + e0))
                            if 2 * (eo + e0 - 1) + hf:
                                pe.wait_ge(yl_done, lin(i, 4, 2 * (eo + e0 - 1) + hf))
                            split_product(DN[:, :], lambda c: actT[:, c, :], k0, RING, i, 0, True, True)
                        if hf == 0 and e0 + 1 < NE:
                            if e0:
                                pe.wait_ge(as_lo, lin(i, 2, eo + e0))
                            gather(e0 + 1, i)
                    if e0:
                        for hf in range(2):
                            pe.wait_ge(yl_done, lin(i, 4, 2 * (eo + e0 - 1) + hf + 1))
                            for t in range(2):
                                for y in (yh, yl):
                                    mm = pe.matmul(ACC[2 * t + hf][:, :], selT[:, t, :], y[:, hf, :],
                                                   start=(e0 == 1 and y is yh), stop=(e0 == NE and y is yl))
                            mm.then_inc(scat, 1)
                    if e0 < NE:
                        if e0 + 1 < NE:
                            pe.wait_ge(xs_lo, lin(i, 2, eo + e0 + 2))
                        else:
                            pe.wait_ge(as_lo, lin(i, 2, eo + e0))
                        for t in range(2):
                            pe.transpose(X[:, t * P:(t + 1) * P], p2[:, par, t, :], ident)
                        for t in range(2):
                            mm = pe.matmul(X[:, 2 * P:2 * P + 1], p2[:, par, t, :], gate_tok[:, par, t:t + 1],
                                           start=(t == 0), stop=(t == 1))
                        mm.then_inc(sel_mm, 1)

                gather(0)
                expert_step(0)
                expert_step(1)
                with pe.Fori(0, 6) as i:
                    expert_step(2, i)
                    expert_step(3, i)
                for e0 in range(14, NE + 1):
                    expert_step(e0)

            def overflow(layer):
                o = over[layer]
                n_over = pe.value_load(flag[0:1, 0:1], min_val=0, max_val=1)
                with pe.If(n_over > 0):
                    for r in range(OVER):
                        with pe.Fori(0, NE) as e:
                            def dve_at(s):
                                pe.wait_ge(o["dve"], e * OV_DVE + (r * NE * OV_DVE + 1 + s))

                            dve_at(3)
                            for c in range(DC):
                                for t in range(2):
                                    pe.matmul(bank[0][:, c * SLOTS:(c + 1) * SLOTS], h[:, t, c::DC],
                                              over_p[:, t, :], start=(t == 0), stop=(t == 1))
                            for t in range(2):
                                pe.transpose(bank[1][0:SLOTS, t * P:(t + 1) * P], over_p[:, t, :], ident)
                            for t in range(2):
                                mm = pe.matmul(bank[2][0:SLOTS, 0:1], over_p[:, t, :], gate_tok[:, 0, t:t + 1],
                                               start=(t == 0), stop=(t == 1))
                            mm.then_inc(o["pe"], 1)
                            dve_at(6)
                            pe.wait_ge(o["w"], e * 96 + (r * NE * 96 + 96))
                            for q, out in enumerate((G, U)):
                                for c in range(DC):
                                    mm = pe.matmul(out[0:SLOTS, :], over_x[:, c, :],
                                                   over_w[:, 2 * q + c // 4, c % 4, :],
                                                   start=(c == 0), stop=(c == DC - 1))
                            mm.then_inc(o["pe"], 1)
                            dve_at(7)
                            for c in range(FC):
                                mm = pe.transpose(bank[3][:, c * P:(c + 1) * P], over_g[:, 1, c::FC], ident)
                            mm.then_inc(o["pe"], 1)
                            dve_at(8)
                            for hf, out in enumerate((DN, X)):
                                for c in range(FC):
                                    mm = pe.matmul(out[0:SLOTS, :], over_aT[:, c, :], over_w[:, 4 + hf, c, :],
                                                   start=(c == 0), stop=(c == FC - 1))
                            mm.then_inc(o["pe"], 1)
                            dve_at(10)
                            for t in range(2):
                                for hf in range(2):
                                    mm = pe.matmul(ACC[2 * t + hf][:, :], over_pT[:, t, :],
                                                   over_y[:, hf * 512:(hf + 1) * 512], start=True, stop=True)
                            mm.then_inc(o["pe"], 1)

            pe.wait_ge(in_cst, 16)
            pe.wait_ge(in_vec, IN_VEC)
            pe.transpose(X[:, 0:V_ALL], chan_rows[:, :], ident[0:V_ALL, 0:V_ALL]).then_inc(chan_mm, 1)
            pe.wait_ge(chan_ready, 2)
            for layer in range(2):
                adaln(layer)
                if layer == 1:
                    pe.wait_ge(in_wdw, 16)
                    pe.wait_ge(ada_gcopy, 8)
                    for c in range(DC):
                        mm = pe.transpose(X[:, c * KW:(c + 1) * KW], wdw_rows[:, c * P:(c + 1) * P],
                                          ident[0:KW, 0:KW])
                    mm.then_inc(wdw_mm, 1)
                pe.wait_ge(ada_evac, 12 * layer + 12)
                pe.wait_ge(ada_gcopy, 4 * layer + 4)
                transpose_h(2 * layer)
                if layer == 0:
                    attention()
                else:
                    convolution()
                pe.wait_ge(x_mix, 4 * layer + 4)
                transpose_h(2 * layer + 1)
                routing(layer)
                pe.wait_ge(routed, 3 * layer + 3)
                experts(layer)
                overflow(layer)
            pe.wait_ge(x_moe, 2)
            for q in range(2):
                mm = row_bcast(bank[4 + q][:, :], R_FIN + q, True)
            mm.then_inc(fin_mm, 1)

        @block.scalar
        def _(sc):
            def square_sums(ni):
                for t in range(2):
                    sc.activation(h[:, t, :], x[:, t, :], ACT.Square,
                                  accum_out=stat[:, t:t + 1]).then_inc(ssq, 1)
                sc.wait_ge(ms_ready, ni + 1)
                sc.activation(stat[:, 4:6], stat[:, 2:4], ACT.Sqrt).then_inc(rms_ready, 1)

            def evac_hT(ni):
                for q in range(2):
                    sc.wait_ge(hT_mm, 4 * ni + q + 1)
                    evac_transposed(lambda o, i_: sc.activation(o, i_, ACT.Copy), ni, 0, q).then_inc(hT_act, 1)

            def adaln(layer):
                if layer:
                    sc.wait_ge(x_moe, layer)
                for i in range(2):
                    for q in range(2):
                        sc.wait_ge(ada_gmm, 4 * layer + 2 * i + q + 1)
                        sc.activation(mod[:, 3 * i + 1, q * 512:(q + 1) * 512], bank[6 + q][:, :],
                                      ACT.Copy).then_inc(ada_gcopy, 1)

            def attention():
                for n in range(6):
                    sc.wait_ge(pe_used, ADA_BLOCKS + 2 * n + 2)
                    sc.activation(qkv[:, 0, n * 512:(n + 1) * 512], bank[4 + 2 * (n % 2)][:, :],
                                  ACT.Copy).then_inc(qkv_c, 1)
                sc.wait_ge(qkv_c, 6)
                sc.dma_start(new_k, qkv[:, 0, D:2 * D]).then_inc(out_kv, 16)
                sc.dma_start(new_v, qkv[:, 0, 2 * D:3 * D]).then_inc(out_kv, 16)
                for m in range(0, len(QK_ITEMS), 2):
                    sc.wait_ge(qk_mm, m + 1)
                    if QK_ITEMS[m][:2] == (0, 0):
                        sc.wait_ge(roped, 1)
                    sc.activation(qk_target(m), bank[m % 4][:, :], ACT.Copy).then_inc(qkT_act, 1)
                for un in range(2 * NH + 2):
                    if un < 2 * NH:
                        g = un % 2
                        w = (g + 1) * P
                        sc.wait_ge(max_done, un + 1)
                        if un >= 2:
                            sc.wait_ge(pT_mm, un - 1)
                        else:
                            sc.wait_ge(qk_mm, len(QK_ITEMS))
                        for m in range(2):
                            sc.activation(probs[:, un % 2, m * 256:m * 256 + w],
                                          bank[4 + 2 * (un % 2) + m][:, 0:w], ACT.Exp,
                                          bias=stat[:, 8 + 2 * (un % 2) + m:9 + 2 * (un % 2) + m],
                                          scale=HD ** -0.5,
                                          accum_out=stat[:, 12 + 2 * (un % 2) + m:13 + 2 * (un % 2) + m])\
                              .then_inc(exp_done, 1)
                    if 1 <= un <= 2 * NH:
                        v = un - 1
                        w = (v % 2 + 1) * P
                        sc.wait_ge(pT_mm, v + 1)
                        if v >= 2:
                            sc.wait_ge(pv_mm, v - 1)
                        sc.activation(probsT[:, v % 2, 0:v % 2 + 1, :], bank[v % 2][:, 0:w],
                                      ACT.Copy).then_inc(pT_evac, 1)
                    if un >= 2:
                        v = un - 2
                        sc.wait_ge(pv_mm, v + 1)
                        sc.activation(h[:, v % 2, (v // 2) * P:(v // 2 + 1) * P], bank[2 + v % 2][:, 0:P],
                                      ACT.Copy).then_inc(o_evac, 1)
                sc.wait_ge(sub_ms, 1)
                sc.activation(stat[:, 32:48], stat[:, 16:32], ACT.Sqrt).then_inc(sub_rms, 1)
                for m in range(4):
                    g, q = m // 2, m % 2
                    sc.wait_ge(oT_mm, m + 1)
                    sc.activation(oT[:, 4 * q:4 * q + 4, :, g * HT:(g + 1) * HT],
                                  bank[m][:, :].rearrange("p (c t i) -> p c t i", c=4, t=2),
                                  ACT.Copy, scale=chan[:, V_SUB:V_SUB + 1]).then_inc(oT_evac, 1)

            def convolution():
                for cc in range(DC):
                    q, k = cc // 4, cc % 4
                    sc.wait_ge(pe_used, MIX0_BLOCKS + ADA_BLOCKS + 4 * q + 4)
                    if cc >= 2:
                        sc.wait_ge(u_done, cc - 1)
                    sc.activation(sig[:, cc % 2, :], bank[4 * q + 2 + k // 2][:, (k % 2) * 256:(k % 2) * 256 + 256],
                                  ACT.Sigmoid, bias=chan[:, V_BPW1 + DC + cc:V_BPW1 + DC + cc + 1])\
                      .then_inc(sig_done, 1)
                sc.wait_ge(centred, 1)
                sc.activation(conv_sq[:, :, :, :], conv[:, :, :, :], ACT.Square).then_inc(squared, 1)
                sc.wait_ge(var_ready, 1)
                sc.activation(rstd_c[:, :], mean[:, :], ACT.Sqrt).then_inc(std_ready, 1)
                sc.wait_ge(scaled, 1)
                for c in range(DC):
                    sc.activation(conv_act[:, c, :, :, :].rearrange("p t g i -> p g t i"),
                                  conv[:, c, :, :].rearrange("p g (t i) -> p g t i", t=2),
                                  ACT.Silu, bias=chan[:, V_LNB + c:V_LNB + c + 1],
                                  scale=chan[:, V_LNG + c:V_LNG + c + 1]).then_inc(conv_silu, 1)

            def experts(layer):
                eo, ko = NE * layer, MOE_BLOCKS * layer

                def high(k0, i=None):
                    wait_block(sc, BASE_MOE[layer] + k0, i)
                    if ko + k0 >= SPLIT:
                        sc.wait_ge(split_used, lin(i, RING, ko + k0 - SPLIT + 1))
                    n = (BASE_MOE[layer] + k0) % RING
                    sc.activation(w_hi[:, k0 % SPLIT, :, :], ring[:, n, :, :], ACT.Copy).then_inc(hi_done, 1)

                def high_tokens(e0, i=None):
                    par = e0 % 2
                    sc.wait_ge(gathered, lin(i, 2, eo + e0 + 1))
                    if eo + e0 >= 2:
                        sc.wait_ge(split_used, lin(i, RING, ko + (block_of(e0 - 2, 3) + 1 if e0 >= 2 else 0)))
                    sc.activation(xs[:, par, :, 0:SLOTS], X[:, :].rearrange("p (c s) -> p c s", c=DC),
                                  ACT.Copy).then_inc(xs_hi, 1)

                def expert_step(e0, i=None):
                    if e0 < NE:
                        high(block_of(e0, 2), i)
                        sc.wait_ge(split_used, lin(i, RING, ko + block_of(e0, 1) + 1))
                        if eo + e0:
                            sc.wait_ge(g_folded, lin(i, 2, eo + e0))
                        sc.activation(g_lo[:, :], G[SLOTS:P, :], ACT.Copy).then_inc(g_low, 1)
                    if e0:
                        sc.wait_ge(actT_mm, lin(i, 2, eo + e0))
                        if eo + e0 >= 2:
                            sc.wait_ge(split_used, lin(i, RING, ko + (block_of(e0 - 1, 5) + 1 if e0 >= 2 else 0)))
                        sc.activation(actT[:, :, 0:SLOTS], X[:, :].rearrange("p (c s) -> p c s", c=FC)[:, :, 0:SLOTS],
                                      ACT.Copy).then_inc(as_hi, 1)
                    if e0 < NE:
                        high(block_of(e0, 3), i)
                    if e0:
                        high(block_of(e0, 4 if e0 < NE else 0), i)
                    if e0 < NE:
                        sc.wait_ge(g_folded, lin(i, 2, eo + e0 + 1))
                        if eo + e0:
                            sc.wait_ge(act_done, lin(i, 2, eo + e0))
                        sc.activation(g_silu[:, :], g_sum[:, :], ACT.Silu).then_inc(silu_done, 1)
                        sc.wait_ge(split_used, lin(i, RING, ko + block_of(e0, 3) + 1))
                        if eo + e0:
                            sc.wait_ge(u_folded, lin(i, 2, eo + e0))
                        sc.activation(u_lo[:, :], U[SLOTS:P, :], ACT.Copy).then_inc(u_low, 1)
                    if e0:
                        high_result(e0, 0, i)
                        high(block_of(e0, 5 if e0 < NE else 1), i)
                    if e0 + 1 < NE:
                        high_tokens(e0 + 1, i)
                        high(block_of(e0 + 1, 0), i)
                    if e0:
                        high_result(e0, 1, i)
                    if e0 + 1 < NE:
                        high(block_of(e0 + 1, 1), i)
                    if e0 < NE:
                        sc.wait_ge(sel_mm, lin(i, 2, eo + e0 + 1))
                        if eo + e0:
                            sc.wait_ge(scat, lin(i, 4, 2 * (eo + e0)))
                            sc.wait_ge(act_done, lin(i, 2, eo + e0))
                        sc.activation(selT[:, :, :], X[:, 0:2 * P], ACT.Copy).then_inc(sel_evac, 1)
                        sc.activation(gate_slot[:, :], X[:, 2 * P:2 * P + 1], ACT.Copy).then_inc(sel_evac, 1)

                def high_result(e0, hf, i=None):
                    k0 = block_of(e0, (4 if e0 < NE else 0) + hf)
                    sc.wait_ge(split_used, lin(i, RING, ko + k0 + 1))
                    if eo + e0 >= 2:
                        sc.wait_ge(scat, lin(i, 4, 2 * (eo + e0 - 2) + hf + 1))
                    sc.activation(yh[:, hf, :], DN[:, :], ACT.Copy).then_inc(yh_done, 1)

                sc.wait_ge(out_kv, 32)
                high_tokens(0)
                high(0)
                high(1)
                expert_step(0)
                expert_step(1)
                with sc.Fori(0, 6) as i:
                    expert_step(2, i)
                    expert_step(3, i)
                for e0 in range(14, NE + 1):
                    expert_step(e0)

            def overflow(layer):
                o = over[layer]
                n_over = sc.value_load(flag[0:1, 0:1], min_val=0, max_val=1)
                with sc.If(n_over > 0):
                    for r in range(OVER):
                        with sc.Fori(0, NE) as e:
                            sc.wait_ge(o["pe"], e * OV_PE + (r * NE * OV_PE + 2))
                            sc.activation(over_g[0:SLOTS, 0, :], G[0:SLOTS, :], ACT.Silu).then_inc(o["act"], 1)

            sc.dma_start(cst[:, :], a["consts"]).then_inc(in_cst, 16)
            for dst, src in SMALL:
                sc.dma_start(dst, src).then_inc(in_vec, 16)
            for t in range(2):
                sc.dma_start(x[0:HT, t, :], mixed(xp, t, 0)).then_inc(in_x, 16)
                sc.dma_start(x[HT:P, t, :], mixed(xl, t, 1)).then_inc(in_x, 16)
            sc.dma_start(cache_k_sb[:, :], a["cache_k"][0, 0].rearrange("t h e -> t (h e)")).then_inc(in_cache_k, 16)
            sc.dma_start(cache_v_sb[:, :], a["cache_v"][0, 0].rearrange("t h e -> t (h e)")).then_inc(in_cache_v, 16)
            sc.wait_ge(in_vec, IN_VEC)
            sc.activation(silu_c[:, :, :], cond[:, :, :], ACT.Silu).then_inc(cond_silu, 1)
            sc.wait_ge(lam_sums, 2)
            sc.activation(lam[:, 2:4], lam[:, 0:2], ACT.Exp).then_inc(lam_exp, 1)
            for layer in range(2):
                adaln(layer)
                if layer:
                    sc.dma_start(wdw_rows[:, :], a["conv_w_dw"][0]).then_inc(in_wdw, 16)
                else:
                    sc.wait_ge(in_x, 64)
                square_sums(2 * layer)
                evac_hT(2 * layer)
                if layer == 0:
                    attention()
                else:
                    convolution()
                sc.wait_ge(x_mix, 4 * layer + 4)
                square_sums(2 * layer + 1)
                evac_hT(2 * layer + 1)
                sc.wait_ge(logits_mm, layer + 1)
                sc.activation(rs[:, 0, :], G[:, 0:2 * NE], ACT.Sigmoid).then_inc(scores_ready, 1)
                sc.wait_ge(routed, 3 * layer + 3)
                experts(layer)
                overflow(layer)
            sc.wait_ge(x_moe, 2)
            square_sums(4)

        def depthwise(eng, chunks, done):
            n = len(chunks)
            for k in range(KW):
                for ci, c in enumerate(chunks):
                    if k:
                        eng.wait_ge(done, (k - 1) * n + ci + 1)
                    shifted = u_pad[:, c, :, k:k + T]
                    if k == 0:
                        ins = eng.tensor_scalar(conv[:, c, :, :], shifted, wdw[:, c, 0:1],
                                                chan[:, V_BDW + c:V_BDW + c + 1], ALU.mult, ALU.add)
                    else:
                        ins = eng.scalar_tensor_tensor(out=conv[:, c, :, :], in0=shifted,
                                                       scalar=wdw[:, c, k:k + 1], in1=conv[:, c, :, :],
                                                       op0=ALU.mult, op1=ALU.add)
                    ins.then_inc(done, 1)

        @block.gpsimd
        def _(pool):
            pool.wait_ge(x_moe, 1)
            for lo in (0, PAD + T):
                pool.memset(u_pad[:, :, :, lo:lo + PAD], 0.0).then_inc(pads_zero, 1)

        @block.vector
        def _(ve):
            chain = [0]

            def link(ins):
                chain[0] += 1
                ins.then_inc(dve_chain, 1)
                ve.wait_ge(dve_chain, chain[0])

            def adaln(layer):
                if layer:
                    ve.wait_ge(x_moe, layer)
                else:
                    ve.wait_ge(cond_silu, 1)
                for g in range(2):
                    ve.tensor_copy(condT[:, :, g * HT:(g + 1) * HT],
                                   silu_c[:, g, :].unsqueeze(2).broadcast_to([P, DC, HT])).then_inc(condT_ready, 1)
                for i in range(2):
                    for j in range(6):
                        n = 6 * i + j
                        ve.wait_ge(pe_used, (MIX0_BLOCKS if layer else 0) + 2 * n + 2)
                        dst = mod[:, 3 * i + j // 2, (j % 2) * 512:(j % 2) * 512 + 512]
                        if j in (2, 3):
                            ve.wait_ge(ada_gcopy, 4 * layer + 2 * i + j - 1)
                            ins = ve.scalar_tensor_tensor(out=dst, in0=bank[j][:, :], scalar=1.0, in1=dst,
                                                          op0=ALU.add, op1=ALU.mult)
                        else:
                            ins = ve.tensor_copy(dst, bank[j][:, :])
                        ins.then_inc(ada_evac, 1)

            def rms(ni):
                ve.wait_ge(ssq, 2 * ni + 2)
                ve.tensor_scalar(stat[:, 2:4], stat[:, 0:2], 1.0 / D, EPS, ALU.mult, ALU.add).then_inc(ms_ready, 1)
                ve.wait_ge(rms_ready, ni + 1)
                link(ve.reciprocal(stat[:, 6:8], stat[:, 4:6]))

            def norm_mod(ni):
                layer, w = ni // 2, ni % 2
                rms(ni)
                ve.wait_ge(ada_evac, 12 * layer + 6 * w + 4)
                for t in range(2):
                    link(ve.scalar_tensor_tensor(out=h[:, t, :], in0=x[:, t, :], scalar=stat[:, 6 + t:7 + t],
                                                 in1=mod[:, 3 * w + 1, :], op0=ALU.mult, op1=ALU.mult))
                    ve.tensor_tensor(h[:, t, :], h[:, t, :], mod[:, 3 * w, :], ALU.add).then_inc(h_ready, 1)
                for q in range(2):
                    ve.wait_ge(hT_mm, 4 * ni + 2 + q + 1)
                    evac_transposed(ve.tensor_copy, ni, 1, q).then_inc(hT_dve, 1)

            def add_gated(layer, gate):
                for n in range(2):
                    ve.wait_ge(pe_used, MIX_END[layer] - 2 + 2 * n)
                    for t in range(2):
                        cols = slice(n * 512, (n + 1) * 512)
                        link(ve.tensor_tensor(h[:, t, cols], bank[4 + 2 * n + t][:, :], mod[:, gate, cols], ALU.mult))
                        ve.tensor_tensor(x[:, t, cols], x[:, t, cols], h[:, t, cols], ALU.add).then_inc(x_mix, 1)
                ve.wait_ge(x_mix, 4 * layer + 4)

            def attention():
                for n in range(6):
                    ve.wait_ge(pe_used, ADA_BLOCKS + 2 * n + 2)
                    ve.tensor_copy(qkv[:, 1, n * 512:(n + 1) * 512], bank[5 + 2 * (n % 2)][:, :]).then_inc(qkv_l, 1)
                ve.wait_ge(qkv_l, 6)
                qk = qkv[:, 1, 0:2 * D].rearrange("p (n a two f) -> p n a two f", n=32, a=2, two=2)
                x1, x2 = qk[:, :, :, 0, :], qk[:, :, :, 1, :]
                cos, sin = (cst[:, c0:c0 + 32].rearrange("p (a f) -> p a f", a=2).unsqueeze(1)
                            .broadcast_to([P, 32, 2, 16]) for c0 in (C_COS, C_SIN))
                s1, s2 = rope_tmp[:, 0], rope_tmp[:, 1]
                ve.tensor_tensor(s1, x1, sin, ALU.mult)
                link(ve.tensor_tensor(s2, x2, sin, ALU.mult))
                ve.tensor_tensor(x1, x1, cos, ALU.mult)
                link(ve.tensor_tensor(x2, x2, cos, ALU.mult))
                ve.tensor_tensor(x1, x1, s2, ALU.subtract)
                ve.tensor_tensor(x2, x2, s1, ALU.add).then_inc(roped, 1)
                for m in range(1, len(QK_ITEMS), 2):
                    ve.wait_ge(qk_mm, m + 1)
                    if QK_ITEMS[m][0] == 0:
                        ve.wait_ge(roped, 1)
                    ve.tensor_copy(qk_target(m), bank[m % 4][:, :].rearrange("p (c i) -> p c i", c=4))\
                      .then_inc(qkT_dve, 1)
                for un in range(2 * NH + 1):
                    if un < 2 * NH:
                        b = un % 2
                        w = (b + 1) * P
                        ve.wait_ge(scores_mm, un + 1)
                        for m in range(2):
                            ins = ve.reduce_max(stat[:, 48 + 2 * b + m:49 + 2 * b + m],
                                                bank[4 + 2 * b + m][:, 0:w], AX)
                        link(ins)
                        ve.tensor_scalar(stat[:, 8 + 2 * b:10 + 2 * b], stat[:, 48 + 2 * b:50 + 2 * b],
                                         -HD ** -0.5, None, ALU.mult).then_inc(max_done, 1)
                    if un:
                        v = un - 1
                        b = v % 2
                        w = (b + 1) * P
                        ve.wait_ge(exp_done, 2 * v + 2)
                        link(ve.reciprocal(stat[:, 52 + 2 * b:54 + 2 * b], stat[:, 12 + 2 * b:14 + 2 * b]))
                        link(ve.tensor_tensor(stat[:, 53 + 2 * b:54 + 2 * b], stat[:, 53 + 2 * b:54 + 2 * b],
                                              lam[:, 4:5], ALU.mult))
                        link(ve.tensor_scalar(probs[:, b, 256:256 + w], probs[:, b, 256:256 + w],
                                              stat[:, 53 + 2 * b:54 + 2 * b], None, ALU.mult))
                        ve.scalar_tensor_tensor(out=probs[:, b, 0:w], in0=probs[:, b, 0:w],
                                                scalar=stat[:, 52 + 2 * b:53 + 2 * b],
                                                in1=probs[:, b, 256:256 + w], op0=ALU.mult,
                                                op1=ALU.subtract).then_inc(combined, 1)
                ve.wait_ge(o_evac, 2 * NH)
                link(ve.tensor_tensor(o_sq[:, :, :], h[:, :, :], h[:, :, :], ALU.mult))
                link(ve.reduce_sum(stat[:, 16:32], o_sq[:, :, :].rearrange("p g (n e) -> p (g n) e", n=NH), AX))
                ve.tensor_scalar(stat[:, 16:32], stat[:, 16:32], 1.0 / P, EPS, ALU.mult, ALU.add).then_inc(sub_ms, 1)
                ve.wait_ge(sub_rms, 1)
                link(ve.reciprocal(stat[:, 56:72], stat[:, 32:48]))
                o = h[:, :, :].rearrange("p g (n e) -> p (g n) e", n=NH)
                ve.tensor_tensor(o, o, stat[:, 56:72].unsqueeze(2).broadcast_to([P, 16, P]), ALU.mult)\
                  .then_inc(o_normed, 1)

            def convolution():
                ve.wait_ge(pads_zero, 2)
                for cc in range(DC):
                    q, k = cc // 4, cc % 4
                    ve.wait_ge(sig_done, cc + 1)
                    ve.scalar_tensor_tensor(out=u_pad[:, cc, :, PAD:PAD + T],
                                            in0=bank[4 * q + k // 2][:, (k % 2) * 256:(k % 2) * 256 + 256]
                                            .rearrange("p (g i) -> p g i", g=2),
                                            scalar=chan[:, V_BPW1 + cc:V_BPW1 + cc + 1],
                                            in1=sig[:, cc % 2, :].rearrange("p (g i) -> p g i", g=2),
                                            op0=ALU.add, op1=ALU.mult).then_inc(u_done, 1)
                ve.wait_ge(u_done, DC)
                depthwise(ve, range(CONV_DVE), conv_dve)
                ve.wait_ge(sum_mm, 1)
                link(ve.tensor_scalar(mean[:, :], bank[0][:, 0:256], 1.0 / D, None, ALU.mult))
                all_c = conv[:, :, :, :].rearrange("p c g i -> p c (g i)")
                ve.tensor_tensor(all_c, all_c, mean[:, :].unsqueeze(1).broadcast_to([P, DC, 2 * T]),
                                 ALU.subtract).then_inc(centred, 1)
                ve.wait_ge(var_mm, 1)
                ve.wait_ge(centred, 1)
                ve.tensor_scalar(mean[:, :], bank[1][:, 0:256], 1.0 / D, EPS, ALU.mult, ALU.add)\
                  .then_inc(var_ready, 1)
                ve.wait_ge(std_ready, 1)
                link(ve.reciprocal(rstd_c[:, :], rstd_c[:, :]))
                ve.tensor_tensor(all_c, all_c, rstd_c[:, :].unsqueeze(1).broadcast_to([P, DC, 2 * T]),
                                 ALU.mult).then_inc(scaled, 1)

            def first_max(out, v, n, prio, scratch, top):
                shape = [P, 2, n]
                link(ve.tensor_reduce(top, v, AX, ALU.max))
                link(ve.tensor_tensor(scratch, v, top.unsqueeze(2).broadcast_to(shape), ALU.is_equal))
                link(ve.tensor_tensor(scratch, scratch, prio.unsqueeze(1).broadcast_to(shape), ALU.mult))
                link(ve.tensor_reduce(top, scratch, AX, ALU.max))
                link(ve.tensor_tensor(out, scratch, top.unsqueeze(2).broadcast_to(shape), ALU.is_equal))

            def routing(layer):
                ve.wait_ge(scores_ready, layer + 1)
                def row(k, n=NE):
                    return rs[:, k, 0:2 * n].rearrange("p (t e) -> p t e", t=2)

                score, sel = row(0), row(1)
                prio4 = cst[:, C_PR4:C_PR4 + NG]
                prio16 = cst[:, C_PR16:C_PR16 + NE]
                link(ve.tensor_tensor(sel, score, bias_b[:, :].unsqueeze(1).broadcast_to([P, 2, NE]), ALU.add))
                s = rs[:, 1, :].rearrange("p (g k) -> p g k", k=4)
                pair = rs[:, 2:4, :].rearrange("p a b -> p (a b)")[:, 0:48].rearrange("p (g k) -> p g k", k=6)
                ve.tensor_tensor(pair[:, :, 0:2], s[:, :, 0:4:2], s[:, :, 1:4:2], ALU.add)
                ve.tensor_tensor(pair[:, :, 2:4], s[:, :, 0:2], s[:, :, 2:4], ALU.add)
                ve.tensor_tensor(pair[:, :, 4:5], s[:, :, 0:1], s[:, :, 3:4], ALU.add)
                link(ve.tensor_tensor(pair[:, :, 5:6], s[:, :, 1:2], s[:, :, 2:3], ALU.add))
                link(ve.tensor_reduce(rs[:, 4, 0:8], pair, AX, ALU.max))
                best = row(6, NG)
                first_max(best, row(4, NG), NG, prio4, row(5, NG), rs[:, 7, 0:2])
                link(ve.tensor_scalar(best, best, BIG, -BIG, ALU.mult, ALU.add))
                v4 = rs[:, 8, :].rearrange("p (g k) -> p g k", k=4)
                link(ve.tensor_tensor(v4, s, rs[:, 6, 0:8].unsqueeze(2).broadcast_to([P, 8, 4]), ALU.add))
                v, one, two = row(8), row(9), row(10)
                first_max(one, v, NE, prio16, row(5), rs[:, 7, 0:2])
                link(ve.scalar_tensor_tensor(out=v, in0=one, scalar=-2.0 * BIG, in1=v, op0=ALU.mult, op1=ALU.add))
                first_max(two, v, NE, prio16, row(5), rs[:, 7, 0:2])
                ve.tensor_tensor(asg[:, :, :], one, two, ALU.add).then_inc(assigned, 1)
                ve.wait_ge(assigned, layer + 1)
                link(ve.tensor_tensor(row(11), score, asg[:, :, :], ALU.mult))
                link(ve.reduce_sum(rs[:, 7, 0:2], row(11), AX))
                link(ve.reciprocal(rs[:, 7, 2:4], rs[:, 7, 0:2]))
                ve.tensor_tensor(gates[:, :, :], row(11), rs[:, 7, 2:4].unsqueeze(2).broadcast_to([P, 2, NE]),
                                 ALU.mult).then_inc(routed, 1)
                link(ve.tensor_scalar(row(9), asg[:, :, :], -FAR, FAR, ALU.mult, ALU.add))
                ve.wait_ge(pos_mm, layer + 1)
                ve.tensor_tensor(pos[:, :, :], row(9), U[:, 0:2 * NE].rearrange("p (t e) -> p t e", t=2),
                                 ALU.add).then_inc(routed, 1)
                link(ve.reduce_max(rs[:, 7, 4:5], U[:, 2 * NE:3 * NE], AX))
                link(ve.tensor_scalar(rs[:, 7, 5:6], rs[:, 7, 4:5], CAP + 0.5, None, ALU.is_gt))
                ve.tensor_copy(flag[:, 0:1], rs[:, 7, 5:6]).then_inc(routed, 1)
                ve.wait_ge(routed, 3 * layer + 3)

            def experts(layer):
                eo, ko = NE * layer, MOE_BLOCKS * layer

                def build_p2(e0, i=None):
                    e = lin(i, 2, e0)
                    par = e0 % 2
                    if eo + e0 >= 2:
                        ve.wait_ge(sel_mm, lin(i, 2, eo + e0 - 1))
                    for t in range(2):
                        ve.tensor_scalar(p2[:, par, t, :], cst[:, C_SLOT:C_SLOT + P], pos[:, t, bass.ds(e, 1)],
                                         None, ALU.is_equal).then_inc(p2_built, 1)
                    ve.tensor_copy(gate_tok[:, par, :], gates[:, :, bass.ds(e, 1)].rearrange("p t o -> p (t o)"))\
                      .then_inc(p2_built, 1)

                def low(k0, i=None):
                    ve.wait_ge(hi_done, lin(i, RING, ko + k0 + 1))
                    n = (BASE_MOE[layer] + k0) % RING
                    ve.tensor_tensor(w_lo[:, k0 % SPLIT, :, :], ring[:, n, :, :], w_hi[:, k0 % SPLIT, :, :],
                                     ALU.subtract).then_inc(lo_done, 1)

                def low_tokens(e0, i=None):
                    par = e0 % 2
                    ve.wait_ge(xs_hi, lin(i, 2, eo + e0 + 1))
                    ve.tensor_tensor(xs[:, par, :, SLOTS:P], X[:, :].rearrange("p (c s) -> p c s", c=DC),
                                     xs[:, par, :, 0:SLOTS], ALU.subtract).then_inc(xs_lo, 1)

                def low_result(e0, hf, i=None):
                    ve.wait_ge(yh_done, lin(i, 4, 2 * (eo + e0 - 1) + hf + 1))
                    ve.tensor_tensor(yl[:, hf, :], DN[:, :], yh[:, hf, :], ALU.subtract).then_inc(yl_done, 1)

                def expert_step(e0, i=None):
                    if e0:
                        ve.wait_ge(silu_done, lin(i, 2, eo + e0))
                        ve.wait_ge(u_folded, lin(i, 2, eo + e0))
                        ve.wait_ge(sel_evac, lin(i, 4, 2 * (eo + e0)))
                        if eo + e0 >= 2:
                            ve.wait_ge(actT_mm, lin(i, 2, eo + e0 - 1))
                        ve.scalar_tensor_tensor(out=act[0:SLOTS, :], in0=g_silu[:, :], scalar=gate_slot[0:SLOTS, :],
                                                in1=u_sum[:, :], op0=ALU.mult, op1=ALU.mult).then_inc(act_done, 1)
                    if e0 < NE:
                        low(block_of(e0, 2), i)
                        ve.wait_ge(g_low, lin(i, 2, eo + e0 + 1))
                        if eo + e0:
                            ve.wait_ge(silu_done, lin(i, 2, eo + e0))
                        ve.tensor_tensor(g_sum[:, :], G[0:SLOTS, :], g_lo[:, :], ALU.add).then_inc(g_folded, 1)
                    if e0:
                        ve.wait_ge(as_hi, lin(i, 2, eo + e0))
                        ve.tensor_tensor(actT[:, :, SLOTS:P],
                                         X[:, :].rearrange("p (c s) -> p c s", c=FC)[:, :, 0:SLOTS],
                                         actT[:, :, 0:SLOTS], ALU.subtract).then_inc(as_lo, 1)
                    if e0 < NE:
                        low(block_of(e0, 3), i)
                    if e0:
                        low(block_of(e0, 4 if e0 < NE else 0), i)
                    if e0 + 1 < NE:
                        build_p2(e0 + 1, i)
                    if e0 < NE:
                        ve.wait_ge(u_low, lin(i, 2, eo + e0 + 1))
                        if eo + e0:
                            ve.wait_ge(act_done, lin(i, 2, eo + e0))
                        ve.tensor_tensor(u_sum[:, :], U[0:SLOTS, :], u_lo[:, :], ALU.add).then_inc(u_folded, 1)
                    if e0:
                        low_result(e0, 0, i)
                        low(block_of(e0, 5 if e0 < NE else 1), i)
                    if e0 + 1 < NE:
                        low_tokens(e0 + 1, i)
                        low(block_of(e0 + 1, 0), i)
                    if e0:
                        low_result(e0, 1, i)
                    if e0 + 1 < NE:
                        low(block_of(e0 + 1, 1), i)

                ve.memset(act[SLOTS:P, :], 0.0)
                build_p2(0)
                low_tokens(0)
                low(0)
                low(1)
                expert_step(0)
                expert_step(1)
                with ve.Fori(0, 6) as i:
                    expert_step(2, i)
                    expert_step(3, i)
                for e0 in range(14, NE + 1):
                    expert_step(e0)
                ve.wait_ge(scat, 2 * NE * (layer + 1))
                for t in range(2):
                    for hf in range(2):
                        cols = slice(hf * 512, (hf + 1) * 512)
                        link(ve.tensor_tensor(moe_tmp[:, 2 * t + hf, :], ACC[2 * t + hf][:, :], mod[:, 5, cols],
                                              ALU.mult))
                        ve.tensor_tensor(x[:, t, cols], x[:, t, cols], moe_tmp[:, 2 * t + hf, :],
                                         ALU.add).then_inc(x_add, 1)
                ve.wait_ge(x_add, 4 * layer + 4)

            def overflow(layer):
                o = over[layer]
                n_over = ve.value_load(flag[0:1, 0:1], min_val=0, max_val=1)
                with ve.If(n_over > 0):
                    ve.memset(over_g[SLOTS:P, 1, :], 0.0).then_inc(o["dve"], 1)
                    for r in range(OVER):
                        with ve.Fori(0, NE) as e:
                            done = [0]

                            def sig_step(ins):
                                done[0] += 1
                                ins.then_inc(o["dve"], 1)
                                ve.wait_ge(o["dve"], e * OV_DVE + (r * NE * OV_DVE + 1 + done[0]))

                            def pe_at(s):
                                ve.wait_ge(o["pe"], e * OV_PE + (r * NE * OV_PE + s))

                            for t in range(2):
                                sig_step(ve.tensor_scalar(over_p[:, t, :], cst[:, C_OVER:C_OVER + SLOTS],
                                                          float(r * SLOTS), pos[:, t, bass.ds(e, 1)],
                                                          ALU.add, ALU.is_equal))
                            sig_step(ve.tensor_copy(gate_tok[:, 0, :],
                                                    gates[:, :, bass.ds(e, 1)].rearrange("p t o -> p (t o)")))
                            pe_at(1)
                            sig_step(ve.tensor_copy(over_x[:, :, :],
                                                    bank[0][:, :].rearrange("p (c s) -> p c s", c=DC)))
                            sig_step(ve.tensor_copy(gate_slot[0:SLOTS, :], bank[2][0:SLOTS, 0:1]))
                            sig_step(ve.tensor_copy(over_pT[:, :, :], bank[1][0:SLOTS, 0:2 * P]
                                                    .rearrange("p (t i) -> p t i", t=2)))
                            ve.wait_ge(o["act"], e + (r * NE + 1))
                            sig_step(ve.scalar_tensor_tensor(out=over_g[0:SLOTS, 1, :],
                                                             in0=over_g[0:SLOTS, 0, :],
                                                             scalar=gate_slot[0:SLOTS, :], in1=U[0:SLOTS, :],
                                                             op0=ALU.mult, op1=ALU.mult))
                            pe_at(3)
                            sig_step(ve.tensor_copy(over_aT[:, :, :], bank[3][:, :]
                                                    .rearrange("p (c s) -> p c s", c=FC)[:, :, 0:SLOTS]))
                            pe_at(4)
                            for hf, y in enumerate((DN, X)):
                                sig_step(ve.tensor_copy(over_y[:, hf * 512:(hf + 1) * 512], y[0:SLOTS, :]))
                            pe_at(5)
                            for t in range(2):
                                for hf in range(2):
                                    cols = slice(hf * 512, (hf + 1) * 512)
                                    sig_step(ve.tensor_tensor(over_t[:, t, cols], ACC[2 * t + hf][:, :],
                                                              mod[:, 5, cols], ALU.mult))
                            for t in range(2):
                                for hf in range(2):
                                    cols = slice(hf * 512, (hf + 1) * 512)
                                    sig_step(ve.tensor_tensor(x[:, t, cols], x[:, t, cols],
                                                              over_t[:, t, cols], ALU.add))
                            assert done[0] == OV_DVE
                ve.memset(lam[:, 7:8], 0.0).then_inc(x_moe, 1)

            ve.wait_ge(in_vec, IN_VEC)
            ve.wait_ge(in_cst, 16)
            for k in range(2):
                link(ve.tensor_tensor(lam_in[:, 2 * k, :], lam_in[:, 2 * k, :], lam_in[:, 2 * k + 1, :], ALU.mult))
                ve.reduce_sum(lam[:, k:k + 1], lam_in[:, 2 * k, :], AX).then_inc(lam_sums, 1)
            ve.wait_ge(lam_exp, 1)
            link(ve.scalar_tensor_tensor(out=lam[:, 4:5], in0=lam[:, 2:3], scalar=LAMBDA_INIT, in1=lam[:, 3:4],
                                         op0=ALU.add, op1=ALU.subtract))
            ve.wait_ge(chan_mm, 1)
            ve.tensor_copy(chan[:, 0:V_SUB], X[:, 0:V_SUB]).then_inc(chan_ready, 1)
            ve.tensor_scalar(chan[:, V_SUB:V_ALL], X[:, V_SUB:V_ALL], 1.0 - LAMBDA_INIT, None, ALU.mult)\
              .then_inc(chan_ready, 1)
            for layer in range(2):
                adaln(layer)
                if layer:
                    ve.wait_ge(wdw_mm, 1)
                    ve.tensor_copy(wdw[:, :, :], X[:, 0:DC * KW].rearrange("p (c k) -> p c k", c=DC))\
                      .then_inc(wdw_ready, 1)
                norm_mod(2 * layer)
                if layer == 0:
                    attention()
                else:
                    convolution()
                add_gated(layer, 2)
                norm_mod(2 * layer + 1)
                routing(layer)
                experts(layer)
                overflow(layer)
            rms(4)
            ve.wait_ge(fin_mm, 1)
            for t in range(2):
                for q in range(2):
                    cols = slice(q * 512, (q + 1) * 512)
                    ins = ve.scalar_tensor_tensor(out=h[:, t, cols], in0=x[:, t, cols],
                                                  scalar=stat[:, 6 + t:7 + t], in1=bank[4 + q][:, :],
                                                  op0=ALU.mult, op1=ALU.mult)
                ins.then_inc(h_ready, 1)


_INS = ['x_prompt', 'x_sample', 'cache_k', 'cache_v', 'c', 'c_ctx', 'norm1_g', 'norm2_g', 'ada_w', 'ada_b',
        'attn_w_qkv', 'attn_w_o', 'attn_lambda_q1', 'attn_lambda_k1', 'attn_lambda_q2', 'attn_lambda_k2',
        'attn_subln_g', 'conv_w_pw1', 'conv_b_pw1', 'conv_w_dw', 'conv_b_dw', 'conv_ln_g', 'conv_ln_b',
        'conv_w_pw2', 'conv_b_pw2', 'router_w', 'router_bias', 'moe_w_gate', 'moe_w_up', 'moe_w_down',
        'final_norm_g']


def kernel(**inputs):
    import concourse.bacc as bacc
    from concourse.bass_utils import run_bass_kernel_spmd

    nc = bacc.Bacc("TRN2", target_bir_lowering=False, num_devices=1)
    arrays, a = {}, {}
    for name in _INS:
        arr = np.ascontiguousarray(inputs[name])
        arrays[f"in_{name}"] = arr
        a[name] = nc.dram_tensor(f"in_{name}", arr.shape, F32, kind="ExternalInput").ap()
    arrays["in_consts"] = constants()
    a["consts"] = nc.dram_tensor("in_consts", (P, C_ALL), F32, kind="ExternalInput").ap()
    shapes = [(1, T, D), (1, T, D), (1, 1, T, NH, 2 * HD), (1, 1, T, NH, 2 * HD)]
    outs = [nc.dram_tensor(f"out_{i}", s, F32, kind="ExternalOutput").ap() for i, s in enumerate(shapes)]
    trunk_kernel(nc, a, outs[0], outs[1], outs[2][0, 0].rearrange("t h e -> t (h e)"),
                 outs[3][0, 0].rearrange("t h e -> t (h e)"))
    r = run_bass_kernel_spmd(nc, [arrays], core_ids=[0])
    return tuple(r.results[0][f"out_{i}"] for i in range(4))
```

```python
from contextlib import ExitStack

import numpy as np

import concourse.bass as bass
from concourse import mybir

F32 = mybir.dt.float32
F32R = mybir.dt.float32r
I32 = mybir.dt.int32
ALU = mybir.AluOpType
ACT = mybir.ActivationFunctionType
AX = mybir.AxisListType.X

P = 128
D = 1024
DC = D // P
T = 128
HT = T // 2
NH = 8
HD = 64
NE = 16
NG = 4
FE = 512
FC = FE // P
KW = 31
PAD = KW // 2
EPS = 1e-6
LAMBDA_INIT = 0.2
SLOTS = 64
CAP = 64
OVER = 3
FAR = 4096.0
BIG = 1e30

RING = 12
HI = 6
ADA_BLOCKS = 24
QKV_BLOCKS = 12
WO_BLOCKS = 4
PW1_BLOCKS = 8
PW2_BLOCKS = 4
MOE_BLOCKS = 96
MIX0_BLOCKS = ADA_BLOCKS + QKV_BLOCKS + WO_BLOCKS
MIX1_BLOCKS = ADA_BLOCKS + PW1_BLOCKS + PW2_BLOCKS
BASE_MIX = [0, MIX0_BLOCKS + MOE_BLOCKS]
BASE_MOE = [MIX0_BLOCKS, MIX0_BLOCKS + MOE_BLOCKS + MIX1_BLOCKS]

C_ID, C_ONE, C_TRI, C_SLOT, C_COS, C_SIN, C_PR4, C_PR16 = 0, 128, 256, 384, 512, 544, 576, 580
C_OVER = 596
C_FOLD = C_OVER + 64
C_ALL = C_FOLD + P
CONV_DVE = DC
OV_DVE, OV_PE = 18, 5
QK_ITEMS = [(2, 0, 0), (2, 0, 1), (1, 0, 0), (1, 0, 1), (0, 0, 0), (0, 0, 1),
            (0, 1, 0), (0, 1, 1), (1, 1, 0), (1, 1, 1)]
R_ADA = [0, 12]
R_G1 = [24, 26]
R_G2 = [28, 30]
R_FIN = 32
R_PW2 = 34
R_ALL = 36
V_BPW1, V_BDW, V_LNG, V_LNB, V_SUB, V_ALL = 0, 16, 24, 32, 40, 41


def constants():
    c = np.zeros((P, C_ALL), np.float32)
    c[:, C_ID:C_ID + P] = np.eye(P)
    c[:, C_ONE:C_ONE + P] = 1.0
    c[:, C_TRI:C_TRI + P] = np.triu(np.ones((P, P)), 1)
    slot = np.arange(P) % SLOTS
    c[:, C_SLOT:C_SLOT + P] = np.where(slot < CAP, slot, -1.0)
    c[:, C_OVER:C_OVER + SLOTS] = np.arange(SLOTS) + CAP
    for m in range(P):
        c[64 * (m // 64), C_FOLD + m] = c[64 * (m // 64) + 32, C_FOLD + m] = 1.0
    grid_w = 64
    rows = np.repeat(np.arange(T // grid_w, dtype=np.float32), grid_w)
    cols = np.tile(np.arange(grid_w, dtype=np.float32), T // grid_w)
    n_freq = HD // 4
    inv = (np.float32(10000.0) ** (-np.arange(n_freq, dtype=np.float32) / np.float32(n_freq))).astype(np.float32)
    ang = np.stack([rows[:, None] * inv, cols[:, None] * inv], axis=1).astype(np.float32)
    c[:, C_COS:C_COS + 32] = np.cos(ang).reshape(T, 32)
    c[:, C_SIN:C_SIN + 32] = np.sin(ang).reshape(T, 32)
    c[:, C_PR4:C_PR4 + NG] = np.arange(NG, 0, -1)
    c[:, C_PR16:C_PR16 + NE] = np.arange(NE, 0, -1)
    return c


def split_index(n):
    return n - sum(min(max(n - (BASE_MIX[k] + ADA_BLOCKS), 0), BASE_MOE[k] - BASE_MIX[k] - ADA_BLOCKS)
                   for k in range(2))


def expert_place(e, what):
    kind, half = "GDU".index(what[0]), int(what[1])
    if e == 0:
        return (0, None, 2)[kind] + half
    return 6 * e - 2 + (half if e == NE else 2 * kind + half)


def blocks_ahead(e):
    for step, what in ((e, "D1"), (e, "U0"), (e, "U1"), (e + 1, "G0"), (e + 1, "G1"), (e + 1, "D0")):
        exists = step <= NE and (step > 0 if what[0] == "D" else step < NE)
        yield expert_place(step, what) if exists else None


def trunk_kernel(nc, a, y_prompt, y_sample, new_k, new_v):
    ctx = ExitStack()
    with ctx:
        base = 16512
        place = [base]

        def at(name, off, shape, dt=F32):
            return nc.alloc_sbuf_tensor_at(name, shape, dt, offset=off)

        def take(n_bytes):
            off = place[0]
            place[0] += (n_bytes + 31) // 32 * 32
            return off

        def sb(name, shape, dt=F32):
            return at(name, take(4 * int(np.prod(shape[1:]))), shape, dt)

        ring = sb("ring", [P, RING, 4, 512])
        w_lo = [at(f"w_lo{k}", base + 8192 * k, [P, 4, 512], F32R) for k in range(RING)]
        split_at = take(HI * 8192)
        w_hi = at("w_hi", split_at, [P, HI, 4, 512], F32R)
        x = sb("x", [P, 2, D])
        h = sb("h", [P, 2, D])
        mod_at = take(6 * 4096)
        mod = at("mod", mod_at, [P, 6, D])
        hT_at = take(8192)
        hT = at("hT", hT_at, [P, DC, 2, T])
        hTm = at("hTm", hT_at, [P, DC, 2, P])
        moe_tmp = at("moe_tmp", hT_at, [P, 4, 512])
        condT = at("condT", hT_at, [P, DC, 4, 32], F32R)
        ada_part = at("ada_part", hT_at + 4096, [P, 2, 512])
        xs = at("xs", hT_at, [P, 2, DC, P], F32R)
        yh = at("yh", mod_at, [P, 2, 512], F32R)
        yl = at("yl", mod_at + 4096, [P, 2, 512], F32R)
        g_lo = at("g_lo", mod_at + 8192, [SLOTS, FE])
        g_sum = at("g_sum", mod_at + 10240, [SLOTS, FE])
        g_silu = at("g_silu", mod_at + 12288, [SLOTS, FE])
        u_lo = at("u_lo", mod_at + 14336, [SLOTS, FE])
        u_sum = at("u_sum", mod_at + 16384, [SLOTS, FE])
        act = at("act", mod_at + 18432, [P, FE])
        moe_at = take(2048 + 2048 + 2048)
        actT = at("actT", moe_at, [P, FC, P], F32R)
        selT = at("selT", moe_at + 2048, [P, 2, 2, P], F32R)
        p2 = at("p2", moe_at + 4096, [P, 2, 2, P])
        cache_v_sb = at("cache_v_sb", moe_at, [P, D])
        qkv = at("qkv", split_at, [P, 2, 3 * D])
        qT = at("qT", split_at + 24576, [P, NH, 2, T])
        kT = at("kT", split_at + 32768, [P, NH, 2, T])
        cache_k_sb = at("cache_k_sb", split_at + 40960, [P, D])
        ckT = at("ckT", split_at + 45056, [P, NH, T])
        probs = at("probs", split_at, [P, 2, 512])
        probsT = at("probsT", split_at + 12288, [P, 2, 2, P])
        rope_tmp = at("rope_tmp", split_at + 24576, [P, 2, 32, 2, 16])
        oT = at("oT", split_at + 24576, [P, NH, 2, P])
        o_sq = at("o_sq", split_at + 32768, [P, 2, D])
        u_pad = at("u_pad", split_at, [P, DC, 2, T + 2 * PAD])
        conv = at("conv", split_at + 10112, [P, DC, 2, T])
        conv_sq = at("conv_sq", split_at + 18304, [P, DC, 2, T])
        conv_act = at("conv_act", split_at + 26496, [P, DC, 2, 2, HT])
        mean = at("mean", split_at + 34688, [P, 2 * T])
        rstd_c = at("rstd_c", split_at + 35712, [P, 2 * T])
        sig = at("sig", split_at + 36736, [P, 2, 2 * T])
        wdw_rows = at("wdw_rows", split_at + 38784, [KW, D])
        over_w = at("over_w", split_at, [P, 6, 4, 512])
        over_p = at("over_p", moe_at, [P, 2, SLOTS])
        over_pT = at("over_pT", moe_at + 512, [SLOTS, 2, P])
        over_x = at("over_x", hT_at, [P, DC, SLOTS])
        over_aT = at("over_aT", hT_at + 2048, [P, FC, SLOTS])
        over_y = at("over_y", mod_at, [SLOTS, D])
        over_t = at("over_t", mod_at + 4096, [P, 2, D])
        over_g = at("over_g", mod_at + 12288, [P, 2, FE])
        cst = sb("cst", [P, C_ALL])
        rows = sb("rows", [R_ALL, 512])
        router = sb("router", [P, DC, NE])
        bias_b = sb("bias_b", [P, NE])
        chan_rows = sb("chan_rows", [V_ALL, P])
        chan = sb("chan", [P, V_ALL])
        wdw = sb("wdw", [P, DC, KW])
        cond = sb("cond", [P, 2, DC])
        silu_c = sb("silu_c", [P, 2, DC])
        lam_in = at("lam_in", mod_at + 20480, [P, 4, HD])
        lam = sb("lam", [P, 8])
        stat = sb("stat", [P, 72])
        asg = sb("asg", [P, 2, NE])
        rs = at("rs", mod_at, [P, 12, 2 * NE])
        pos = sb("pos", [P, 2, NE])
        gates = sb("gates", [P, 2, NE])
        gate_tok = sb("gate_tok", [P, 2, 2])
        gate_slot = sb("gate_slot", [P, 1])
        flag = sb("flag", [P, 2], I32)
        assert place[0] <= nc.sbuf_usable_end, place[0]

        ident = cst[:, C_ID:C_ID + P]
        ones = cst[:, C_ONE:C_ONE + P]
        bank = [ctx.enter_context(nc.psum_tensor(f"bank{i}", [P, 512], F32)) for i in range(8)]
        ACC, G, U, DN, X = bank[0:4], bank[4], bank[5], bank[6], bank[7]

        def sem(name):
            return ctx.enter_context(nc.semaphore(name))

        landed = [sem(f"landed{i}") for i in range(RING)]
        pe_used = sem("pe_used")
        hi_done, lo_done = sem("hi_done"), sem("lo_done")
        in_first, in_x, in_vec = sem("in_first"), sem("in_x"), sem("in_vec")
        in_cache_k, in_cache_v, in_wdw = sem("in_cache_k"), sem("in_cache_v"), sem("in_wdw")
        out_kv, out_y = sem("out_kv"), sem("out_y")
        act_chain, dve_chain = sem("act_chain"), sem("dve_chain")
        cond_silu, condT_ready = sem("cond_silu"), sem("condT_ready")
        ada_mm, part_evac, ada_evac = sem("ada_mm"), sem("part_evac"), sem("ada_evac")
        ada_gmm, ada_gcopy = sem("ada_gmm"), sem("ada_gcopy")
        chan_mm, chan_ready = sem("chan_mm"), sem("chan_ready")
        lam_sums, lam_exp = sem("lam_sums"), sem("lam_exp")
        ssq, ms_ready, rms_ready, h_ready = sem("ssq"), sem("ms_ready"), sem("rms_ready"), sem("h_ready")
        hT_mm, hT_act, hT_dve = sem("hT_mm"), sem("hT_act"), sem("hT_dve")
        x_mix, x_add, x_moe = sem("x_mix"), sem("x_add"), sem("x_moe")
        qkv_c, qkv_l, roped = sem("qkv_c"), sem("qkv_l"), sem("roped")
        qk_mm, qkT_act, qkT_dve = sem("qk_mm"), sem("qkT_act"), sem("qkT_dve")
        scores_mm, max_done, exp_done = sem("scores_mm"), sem("max_done"), sem("exp_done")
        combined, pT_mm, pT_evac = sem("combined"), sem("pT_mm"), sem("pT_evac")
        pv_mm, o_evac, o_normed, oT_mm, oT_evac = (sem("pv_mm"), sem("o_evac"), sem("o_normed"),
                                                   sem("oT_mm"), sem("oT_evac"))
        sub_ms, sub_rms = sem("sub_ms"), sem("sub_rms")
        wdw_mm, wdw_ready, sig_done, u_done = sem("wdw_mm"), sem("wdw_ready"), sem("sig_done"), sem("u_done")
        pads_zero, conv_dve = sem("pads_zero"), sem("conv_dve")
        sum_mm, centred, squared, var_mm = sem("sum_mm"), sem("centred"), sem("squared"), sem("var_mm")
        var_ready, std_ready, scaled, conv_silu = (sem("var_ready"), sem("std_ready"), sem("scaled"),
                                                   sem("conv_silu"))
        logits_mm, scores_ready, assigned, pos_mm, routed = (
            sem("logits_mm"), sem("scores_ready"), sem("assigned"), sem("pos_mm"), sem("routed"))
        p2_built, gathered, xs_hi, xs_lo = sem("p2_built"), sem("gathered"), sem("xs_hi"), sem("xs_lo")
        g_low, g_folded = sem("g_low"), sem("g_folded")
        u_low, u_folded, silu_done = sem("u_low"), sem("u_folded"), sem("silu_done")
        sel_mm, sel_evac, act_done, actT_mm = sem("sel_mm"), sem("sel_evac"), sem("act_done"), sem("actT_mm")
        as_hi, as_lo = sem("as_hi"), sem("as_lo")
        yh_done, yl_done, scat = sem("yh_done"), sem("yl_done"), sem("scat")
        over = [{n: sem(f"over{k}_{n}") for n in ("w", "pe", "act", "dve")} for k in range(2)]
        fin_mm = sem("fin_mm")

        block = ctx.enter_context(nc.Block())

        def wait_block(eng, n, i=None):
            v = 16 * (n // RING + 1)
            eng.wait_ge(landed[n % RING], v if i is None else i * 16 + v)

        def high(sc, n, i=None):
            k = split_index(n)
            wait_block(sc, n, i)
            if k >= HI:
                sc.wait_ge(pe_used, lin(i, RING, block_before(k - HI) + 1))
            sc.activation(w_hi[:, k % HI, :, :], ring[:, n % RING, :, :], ACT.Copy).then_inc(hi_done, 1)

        def low(ve, n, i=None):
            k = split_index(n)
            ve.wait_ge(hi_done, lin(i, RING, k + 1))
            ve.tensor_tensor(w_lo[n % RING][:, :, :], ring[:, n % RING, :, :], w_hi[:, k % HI, :, :],
                             ALU.subtract).then_inc(lo_done, 1)

        def block_before(k):
            return next(n for n in range(BASE_MOE[1] + MOE_BLOCKS) if split_index(n + 1) == k + 1)

        def lin(i, per_i, const):
            return const if i is None else i * per_i + const

        def ada_block(layer, n):
            src = a["ada_w"][layer].rearrange("(p c) n -> p c n", c=DC)
            g, hf = n // 2, n % 2
            return src[:, 4 * hf:4 * hf + 4, g * 512:(g + 1) * 512]

        def qkv_block(n):
            src = a["attn_w_qkv"][0].rearrange("(p c) n -> p c n", c=DC)
            g, hf = n // 2, n % 2
            return src[:, 4 * hf:4 * hf + 4, g * 512:(g + 1) * 512]

        def wo_block(n):
            src = a["attn_w_o"][0].rearrange("(c p) n -> p c n", p=P)
            g, hf = n // 2, n % 2
            return src[:, 4 * hf:4 * hf + 4, g * 512:(g + 1) * 512]

        PW1_ORDER = [0, 2, 1, 3]

        def pw1_block(n):
            src = a["conv_w_pw1"][0].rearrange("(p c) n -> p c n", c=DC)
            g, hf = PW1_ORDER[n // 2], n % 2
            return src[:, 4 * hf:4 * hf + 4, g * 512:(g + 1) * 512]

        def pw2_block(n):
            src = a["conv_w_pw2"][0].rearrange("(c p) n -> p c n", p=P)
            g, hf = n // 2, n % 2
            return src[:, 4 * hf:4 * hf + 4, g * 512:(g + 1) * 512]

        def expert_block(layer, e, what):
            half = int(what[1])
            if what[0] == "D":
                src = a["moe_w_down"][layer, e].rearrange("(p c) n -> p c n", c=FC)
                return src[:, :, 512 * half:512 * half + 512]
            src = a["moe_w_gate" if what[0] == "G" else "moe_w_up"][layer, e].rearrange("(p c) f -> p c f", c=DC)
            return src[:, 4 * half:4 * half + 4, :]

        def mixed(dram, t, g):
            return dram[t * HT:(t + 1) * HT, :]

        xp, xl = a["x_prompt"][0], a["x_sample"][0]

        def evac_transposed(copy, ni, t, q):
            src = bank[2 * t + q][:, :]
            if ni % 2:
                return copy(hTm[:, 4 * q:4 * q + 4, t, :], src.rearrange("p (c i) -> p c i", c=4))
            return copy(hT[:, 4 * q:4 * q + 4, :, t * HT:(t + 1) * HT],
                        src.rearrange("p (c g i) -> p c g i", c=4, g=2))

        def qk_target(m):
            what, g, q = QK_ITEMS[m]
            return (ckT[:, 4 * q:4 * q + 4, :] if what == 2
                    else (qT, kT)[what][:, 4 * q:4 * q + 4, g, :])

        FIRST = [
            (cst[:, :], a["consts"]),
            (cond[:, 0, :], a["c_ctx"].rearrange("(p c) -> p c", c=DC)),
            (cond[:, 1, :], a["c"][0].rearrange("(p c) -> p c", c=DC)),
            (rows[0:24, :], a["ada_b"].rearrange("l (r n) -> (l r) n", n=512)),
            (rows[24:28, :], a["norm1_g"].rearrange("l (r n) -> (l r) n", n=512)),
            (rows[28:32, :], a["norm2_g"].rearrange("l (r n) -> (l r) n", n=512)),
            (rows[32:34, :], a["final_norm_g"].rearrange("(r n) -> r n", n=512)),
            (rows[34:36, :], a["conv_b_pw2"][0].rearrange("(r n) -> r n", n=512)),
        ]
        SMALL = [
            (chan_rows[0:16, :], a["conv_b_pw1"][0].rearrange("(r n) -> r n", n=P)),
            (chan_rows[16:24, :], a["conv_b_dw"][0].rearrange("(r n) -> r n", n=P)),
            (chan_rows[24:32, :], a["conv_ln_g"][0].rearrange("(r n) -> r n", n=P)),
            (chan_rows[32:40, :], a["conv_ln_b"][0].rearrange("(r n) -> r n", n=P)),
            (chan_rows[40:41, :], a["attn_subln_g"]),
            (router[:, :, :], a["router_w"].rearrange("(p c) e -> p c e", c=DC)),
            (bias_b[:, :], a["router_bias"].partition_broadcast(P)),
            (lam_in[:, 0, :], a["attn_lambda_q1"][0].partition_broadcast(P)),
            (lam_in[:, 1, :], a["attn_lambda_k1"][0].partition_broadcast(P)),
            (lam_in[:, 2, :], a["attn_lambda_q2"][0].partition_broadcast(P)),
            (lam_in[:, 3, :], a["attn_lambda_k2"][0].partition_broadcast(P)),
        ]
        IN_FIRST, IN_VEC = 16 * len(FIRST), 16 * len(SMALL)

        @block.sync
        def _(sp):
            def load(n, src, i=None):
                sp.dma_start(ring[:, n % RING, :, :], src).then_inc(landed[n % RING], 16)

            def free(n, i=None):
                if n >= 0:
                    sp.wait_ge(pe_used, lin(i, RING, n + 1))

            def moe_stream(layer):
                def expert_step(e0, i=None):
                    e = lin(i, 2, e0)
                    for what in ("G0", "G1", "D0", "D1", "U0", "U1"):
                        if (what[0] == "D" and e0 == 0) or (what[0] != "D" and e0 == NE):
                            continue
                        n = BASE_MOE[layer] + expert_place(e0, what)
                        free(n - RING, i)
                        load(n, expert_block(layer, e - 1 if what[0] == "D" else e, what))

                expert_step(0)
                expert_step(1)
                with sp.Fori(0, 6) as i:
                    expert_step(2, i)
                    expert_step(3, i)
                for e0 in range(14, NE + 1):
                    expert_step(e0)

            def overflow(layer):
                sp.wait_ge(routed, 3 * layer + 3)
                n_over = sp.value_load(flag[0:1, 0:1], min_val=0, max_val=1)
                with sp.If(n_over > 0):
                    o = over[layer]
                    for r in range(OVER):
                        with sp.Fori(0, NE) as e:
                            sp.wait_ge(o["dve"], e * OV_DVE + (r * NE * OV_DVE + 1))
                            for j, what in enumerate(("G0", "G1", "U0", "U1", "D0", "D1")):
                                sp.dma_start(over_w[:, j, :, :], expert_block(layer, e, what)).then_inc(o["w"], 16)

            for dst, src in FIRST:
                sp.dma_start(dst, src).then_inc(in_first, 16)
            for n in range(ADA_BLOCKS):
                free(n - RING)
                load(n, ada_block(0, n))
            for n in range(QKV_BLOCKS):
                free(ADA_BLOCKS + n - RING)
                load(ADA_BLOCKS + n, qkv_block(n))
            for n in range(WO_BLOCKS):
                free(ADA_BLOCKS + QKV_BLOCKS + n - RING)
                load(ADA_BLOCKS + QKV_BLOCKS + n, wo_block(n))
            moe_stream(0)
            overflow(0)
            b = BASE_MIX[1]
            for n in range(ADA_BLOCKS):
                free(b + n - RING)
                load(b + n, ada_block(1, n))
            b += ADA_BLOCKS
            for n in range(PW1_BLOCKS):
                free(b + n - RING)
                load(b + n, pw1_block(n))
            b += PW1_BLOCKS
            for n in range(PW2_BLOCKS):
                free(b + n - RING)
                load(b + n, pw2_block(n))
            moe_stream(1)
            overflow(1)
            sp.wait_ge(h_ready, 10)
            for t in range(2):
                sp.dma_start(mixed(y_prompt[0], t, 0), h[0:HT, t, :]).then_inc(out_y, 16)
                sp.dma_start(mixed(y_sample[0], t, 1), h[HT:P, t, :]).then_inc(out_y, 16)
            sp.wait_ge(out_y, 64)
            sp.wait_ge(out_kv, 32)

        @block.tensor
        def _(pe):
            def row_bcast(out, r, stop):
                return pe.matmul(out, ident[0:R_ALL, r:r + 1].broadcast_to([R_ALL, P]), rows[:, :],
                                 start=True, stop=stop)

            def adaln(layer):
                pe.wait_ge(condT_ready, 4 * layer + 4)
                if layer:
                    pe.wait_ge(x_moe, layer)

                def products(n):
                    if n >= 2:
                        pe.wait_ge(part_evac, 12 * layer + n - 1)
                    for hf in range(2):
                        b = BASE_MIX[layer] + 2 * n + hf
                        pe.wait_ge(lo_done, split_index(b) + 1)
                        for k in range(4):
                            for part, w in enumerate((w_hi[:, split_index(b) % HI], w_lo[b % RING][:, :, :])):
                                mm = pe.matmul(bank[n % 2][:, :], condT[:, 4 * hf + k, :, :], w[:, k, :],
                                               start=(hf == 0 and k == 0 and part == 0),
                                               stop=(hf == 1 and k == 3 and part == 1))
                        mm.then_inc(pe_used, 1)


                def fold(n):
                    pe.wait_ge(part_evac, 12 * layer + n + 1)
                    if n >= 4:
                        pe.wait_ge(ada_evac, 12 * layer + n - 3)
                    row_bcast(bank[2 + n % 4][:, :], R_ADA[layer] + n, False)
                    pe.matmul(bank[2 + n % 4][:, :], cst[:, C_FOLD:C_FOLD + P], ada_part[:, n % 2, :],
                              start=False, stop=True).then_inc(ada_mm, 1)
                    i, j = n // 6, n % 6
                    if j in (2, 3):
                        if i or layer:
                            pe.wait_ge(ada_evac, 12 * layer + 6 * i + j - 6 + 1)
                        row_bcast(bank[4 + j][:, :], (R_G2 if i else R_G1)[layer] + j - 2, True)\
                            .then_inc(ada_gmm, 1)

                for n in range(13):
                    if n < 12:
                        products(n)
                    if n:
                        fold(n - 1)

            def transpose_h(ni):
                for t in range(2):
                    pe.wait_ge(h_ready, 2 * ni + t + 1)
                    for q in range(2):
                        for k in range(4):
                            c = 4 * q + k
                            mm = pe.transpose(bank[2 * t + q][:, k * P:(k + 1) * P],
                                              h[:, t, c::DC], ident)
                        mm.then_inc(hT_mm, 1)
                pe.wait_ge(hT_act, 2 * ni + 2)
                pe.wait_ge(hT_dve, 2 * ni + 2)

            def qkv_proj():
                for n in range(6):
                    if n >= 2:
                        pe.wait_ge(qkv_c, n - 1)
                        pe.wait_ge(qkv_l, n - 1)
                    for hf in range(2):
                        b = ADA_BLOCKS + 2 * n + hf
                        wait_block(pe, b)
                        for k in range(4):
                            for g in range(2):
                                c = 4 * hf + k
                                mm = pe.matmul(bank[4 + 2 * (n % 2) + g][:, :], hT[:, c, g, :],
                                               ring[:, b % RING, k, :], start=(c == 0), stop=(c == DC - 1))
                        mm.then_inc(pe_used, 1)

            def qk_transposes():
                pe.wait_ge(qkv_c, 6)
                pe.wait_ge(in_cache_k, 16)
                for m, (what, g, q) in enumerate(QK_ITEMS):
                    if g == 1:
                        pe.wait_ge(roped, 1)
                    if m >= 4:
                        pe.wait_ge(qkT_act if m % 2 == 0 else qkT_dve, (m - 4) // 2 + 1)
                    for k in range(4):
                        hd = 4 * q + k
                        src = (cache_k_sb[:, hd * P:(hd + 1) * P] if what == 2
                               else qkv[:, g, what * D + hd * P:what * D + (hd + 1) * P])
                        mm = pe.transpose(bank[m % 4][:, k * P:(k + 1) * P], src, ident)
                    mm.then_inc(qk_mm, 1)
                pe.wait_ge(qkT_act, len(QK_ITEMS) // 2)
                pe.wait_ge(qkT_dve, len(QK_ITEMS) // 2)
                pe.wait_ge(qkv_l, 6)
                pe.wait_ge(in_cache_v, 16)

            def scores(un):
                hd, g = un // 2, un % 2
                if un >= 2:
                    pe.wait_ge(exp_done, 2 * (un - 1))
                for m in range(2):
                    out = bank[4 + 2 * (un % 2) + m]
                    q = qT[HD * m:HD * m + HD, hd, g, :]
                    if g == 1:
                        pe.matmul(out[:, 0:P], q, ckT[HD * m:HD * m + HD, hd, :], start=True, stop=True)
                    mm = pe.matmul(out[:, g * P:(g + 1) * P], q, kT[HD * m:HD * m + HD, hd, g, :],
                                   start=True, stop=True)
                mm.then_inc(scores_mm, 1)

            def probs_transpose(un):
                g = un % 2
                pe.wait_ge(combined, un + 1)
                if un >= 2:
                    pe.wait_ge(pT_evac, un - 1)
                for kc in range(g + 1):
                    mm = pe.transpose(bank[un % 2][:, kc * P:(kc + 1) * P],
                                      probs[:, un % 2, kc * P:(kc + 1) * P], ident)
                mm.then_inc(pT_mm, 1)

            def pv(un):
                hd, g = un // 2, un % 2
                pe.wait_ge(pT_evac, un + 1)
                if un >= 2:
                    pe.wait_ge(o_evac, un - 1)
                for kc in range(g + 1):
                    val = (cache_v_sb[:, hd * P:(hd + 1) * P] if kc < g
                           else qkv[:, g, 2 * D + hd * P:2 * D + (hd + 1) * P])
                    mm = pe.matmul(bank[2 + un % 2][:, 0:P], probsT[:, un % 2, kc, :], val,
                                   start=(kc == 0), stop=(kc == g))
                mm.then_inc(pv_mm, 1)

            def attention():
                qkv_proj()
                qk_transposes()
                for un in range(2 * NH + 2):
                    if un < 2 * NH:
                        scores(un)
                    if 1 <= un <= 2 * NH:
                        probs_transpose(un - 1)
                    if un >= 2:
                        pv(un - 2)
                pe.wait_ge(o_normed, 1)
                pe.wait_ge(pT_evac, 2 * NH)
                for g in range(2):
                    for q in range(2):
                        for k in range(4):
                            hd = 4 * q + k
                            mm = pe.transpose(bank[2 * g + q][:, k * P:(k + 1) * P],
                                              h[:, g, hd * P:(hd + 1) * P], ident)
                        mm.then_inc(oT_mm, 1)
                pe.wait_ge(oT_evac, 4)
                for n in range(2):
                    for hf in range(2):
                        b = ADA_BLOCKS + QKV_BLOCKS + 2 * n + hf
                        wait_block(pe, b)
                        for k in range(4):
                            for t in range(2):
                                c = 4 * hf + k
                                mm = pe.matmul(bank[4 + 2 * n + t][:, :], oT[:, c, t, :],
                                               ring[:, b % RING, k, :], start=(c == 0), stop=(c == DC - 1))
                        mm.then_inc(pe_used, 1)

            def convolution():
                pe.wait_ge(in_wdw, 16)
                for c in range(DC):
                    mm = pe.transpose(X[:, c * KW:(c + 1) * KW], wdw_rows[:, c * P:(c + 1) * P],
                                      ident[0:KW, 0:KW])
                mm.then_inc(wdw_mm, 1)
                b0 = BASE_MIX[1] + ADA_BLOCKS
                for n in range(4):
                    b = b0 + 2 * n
                    wait_block(pe, b)
                    wait_block(pe, b + 1)
                    if n == 3:
                        pe.wait_ge(wdw_ready, 1)
                    for k in range(4):
                        for c in range(DC):
                            mm = pe.matmul(bank[2 * n + k // 2][:, (k % 2) * 256:(k % 2) * 256 + 256],
                                           ring[:, (b + c // 4) % RING, c % 4, k * P:(k + 1) * P],
                                           hT[:, c, :, :], start=(c == 0), stop=(c == DC - 1))
                            if k == 3 and c % 4 == 3:
                                mm.then_inc(pe_used, 1)
                pe.wait_ge(conv_dve, CONV_DVE * KW)
                for c in range(DC):
                    mm = pe.matmul(bank[0][:, 0:256], ones, conv[:, c, :, :], start=(c == 0), stop=(c == DC - 1))
                mm.then_inc(sum_mm, 1)
                pe.wait_ge(squared, 1)
                for c in range(DC):
                    mm = pe.matmul(bank[1][:, 0:256], ones, conv_sq[:, c, :, :], start=(c == 0),
                                   stop=(c == DC - 1))
                mm.then_inc(var_mm, 1)
                pe.wait_ge(conv_silu, DC)
                for n in range(2):
                    for t in range(2):
                        row_bcast(bank[4 + 2 * n + t][:, :], R_PW2 + n, False)
                    for hf in range(2):
                        b = b0 + PW1_BLOCKS + 2 * n + hf
                        wait_block(pe, b)
                        for k in range(4):
                            for t in range(2):
                                c = 4 * hf + k
                                mm = pe.matmul(bank[4 + 2 * n + t][:, :], conv_act[:, c, t, :, :],
                                               ring[:, b % RING, k, :], start=False, stop=(c == DC - 1))
                        mm.then_inc(pe_used, 1)

            def routing(layer):
                pe.wait_ge(x_mix, 4 * layer + 4)
                for t in range(2):
                    for c in range(DC):
                        mm = pe.matmul(G[:, t * NE:(t + 1) * NE], hTm[:, c, t, :], router[:, c, :],
                                       start=(c == 0), stop=(c == DC - 1))
                mm.then_inc(logits_mm, 1)
                pe.wait_ge(assigned, layer + 1)
                tri = cst[:, C_TRI:C_TRI + P]
                pe.matmul(U[:, 0:NE], tri, asg[:, 0, :], start=True, stop=True)
                pe.matmul(U[:, NE:2 * NE], ones, asg[:, 0, :], start=True, stop=False)
                pe.matmul(U[:, NE:2 * NE], tri, asg[:, 1, :], start=False, stop=True)
                pe.matmul(U[:, 2 * NE:3 * NE], ones, asg[:, 0, :], start=True, stop=False)
                pe.matmul(U[:, 2 * NE:3 * NE], ones, asg[:, 1, :], start=False, stop=True).then_inc(pos_mm, 1)

            def experts(layer):
                eo, b0 = NE * layer, BASE_MOE[layer]

                def gather(e0, i=None):
                    par = e0 % 2
                    pe.wait_ge(p2_built, lin(i, 6, 3 * (eo + e0 + 1)))
                    for c in range(DC):
                        for t in range(2):
                            mm = pe.matmul(X[:, c * SLOTS:(c + 1) * SLOTS], h[:, t, c::DC],
                                           p2[:, par, t, 0:SLOTS], start=(t == 0), stop=(t == 1))
                    mm.then_inc(gathered, 1)

                def split_product(out, lhs, k0, i, chunks, first, last):
                    n = b0 + k0
                    k = split_index(n)
                    pe.wait_ge(lo_done, lin(i, RING, k + 1))
                    for c in range(4):
                        for part, w in enumerate((w_hi[:, k % HI], w_lo[n % RING][:, :, :])):
                            mm = pe.matmul(out, lhs(chunks + c), w[:, c, :],
                                           start=(first and c == 0 and part == 0),
                                           stop=(last and c == 3 and part == 1))
                            if c == 3 and part == 1:
                                mm.then_inc(pe_used, 1)

                def scatter(e0, i=None):
                    pe.wait_ge(sel_evac, lin(i, 4, 2 * (eo + e0) + 2))
                    for hf in range(2):
                        pe.wait_ge(yl_done, lin(i, 4, 2 * (eo + e0) + hf + 1))
                        for t in range(2):
                            for y in (yh, yl):
                                mm = pe.matmul(ACC[2 * t + hf][:, :], selT[:, e0 % 2, t, :], y[:, hf, :],
                                               start=(e0 == 0 and y is yh), stop=(e0 == NE - 1 and y is yl))
                        mm.then_inc(scat, 1)

                def down(e0, hf, i=None):
                    if hf == 0:
                        pe.wait_ge(as_lo, lin(i, 2, eo + e0))
                    if 2 * (eo + e0 - 1) + hf:
                        pe.wait_ge(yl_done, lin(i, 4, 2 * (eo + e0 - 1) + hf))
                    split_product(DN[:, :], lambda c: actT[:, c, :], expert_place(e0, f"D{hf}"), i, 0, True, True)

                def expert_step(e0, i=None):
                    par = e0 % 2
                    if e0 < NE:
                        pe.wait_ge(xs_lo, lin(i, 2, eo + e0 + 1))
                        if eo + e0:
                            pe.wait_ge(g_folded, lin(i, 2, eo + e0))
                        for q in range(2):
                            split_product(G[:, :], lambda c: xs[:, par, c, :], expert_place(e0, f"G{q}"), i,
                                          4 * q, q == 0, q == 1)
                    if e0:
                        pe.wait_ge(act_done, lin(i, 2, eo + e0))
                        pe.wait_ge(sel_evac, lin(i, 4, 2 * (eo + e0)))
                        for c in range(FC):
                            mm = pe.transpose(X[:, c * P:(c + 1) * P], act[:, c::FC], ident)
                        mm.then_inc(actT_mm, 1)
                    if e0 >= 2:
                        scatter(e0 - 2, i)
                    if e0:
                        down(e0, 0, i)
                    if e0 + 1 < NE:
                        if e0:
                            pe.wait_ge(as_lo, lin(i, 2, eo + e0))
                        gather(e0 + 1, i)
                    if e0:
                        down(e0, 1, i)
                    if e0 < NE:
                        if eo + e0:
                            pe.wait_ge(u_folded, lin(i, 2, eo + e0))
                        for q in range(2):
                            split_product(U[:, :], lambda c: xs[:, par, c, :], expert_place(e0, f"U{q}"), i,
                                          4 * q, q == 0, q == 1)
                            if q == 0:
                                if e0 + 1 < NE:
                                    pe.wait_ge(xs_lo, lin(i, 2, eo + e0 + 2))
                                else:
                                    pe.wait_ge(as_lo, lin(i, 2, eo + e0))
                                for t in range(2):
                                    pe.transpose(X[:, t * P:(t + 1) * P], p2[:, par, t, :], ident)
                                for t in range(2):
                                    mm = pe.matmul(X[:, 2 * P:2 * P + 1], p2[:, par, t, :],
                                                   gate_tok[:, par, t:t + 1], start=(t == 0), stop=(t == 1))
                                mm.then_inc(sel_mm, 1)

                gather(0)
                for e0 in range(4):
                    expert_step(e0)
                with pe.Fori(0, 5) as i:
                    expert_step(4, i)
                    expert_step(5, i)
                for e0 in range(14, NE + 1):
                    expert_step(e0)
                scatter(NE - 1)

            def overflow(layer):
                o = over[layer]
                n_over = pe.value_load(flag[0:1, 0:1], min_val=0, max_val=1)
                with pe.If(n_over > 0):
                    for r in range(OVER):
                        with pe.Fori(0, NE) as e:
                            def dve_at(s):
                                pe.wait_ge(o["dve"], e * OV_DVE + (r * NE * OV_DVE + 1 + s))

                            dve_at(3)
                            for c in range(DC):
                                for t in range(2):
                                    pe.matmul(bank[0][:, c * SLOTS:(c + 1) * SLOTS], h[:, t, c::DC],
                                              over_p[:, t, :], start=(t == 0), stop=(t == 1))
                            for t in range(2):
                                pe.transpose(bank[1][0:SLOTS, t * P:(t + 1) * P], over_p[:, t, :], ident)
                            for t in range(2):
                                mm = pe.matmul(bank[2][0:SLOTS, 0:1], over_p[:, t, :], gate_tok[:, 0, t:t + 1],
                                               start=(t == 0), stop=(t == 1))
                            mm.then_inc(o["pe"], 1)
                            dve_at(6)
                            pe.wait_ge(o["w"], e * 96 + (r * NE * 96 + 96))
                            for q, out in enumerate((G, U)):
                                for c in range(DC):
                                    mm = pe.matmul(out[0:SLOTS, :], over_x[:, c, :],
                                                   over_w[:, 2 * q + c // 4, c % 4, :],
                                                   start=(c == 0), stop=(c == DC - 1))
                            mm.then_inc(o["pe"], 1)
                            dve_at(7)
                            for c in range(FC):
                                mm = pe.transpose(bank[3][:, c * P:(c + 1) * P], over_g[:, 1, c::FC], ident)
                            mm.then_inc(o["pe"], 1)
                            dve_at(8)
                            for hf, out in enumerate((DN, X)):
                                for c in range(FC):
                                    mm = pe.matmul(out[0:SLOTS, :], over_aT[:, c, :], over_w[:, 4 + hf, c, :],
                                                   start=(c == 0), stop=(c == FC - 1))
                            mm.then_inc(o["pe"], 1)
                            dve_at(10)
                            for t in range(2):
                                for hf in range(2):
                                    mm = pe.matmul(ACC[2 * t + hf][:, :], over_pT[:, t, :],
                                                   over_y[:, hf * 512:(hf + 1) * 512], start=True, stop=True)
                            mm.then_inc(o["pe"], 1)

            pe.wait_ge(in_first, IN_FIRST)
            pe.wait_ge(in_vec, IN_VEC)
            pe.transpose(X[:, 0:V_ALL], chan_rows[:, :], ident[0:V_ALL, 0:V_ALL]).then_inc(chan_mm, 1)
            pe.wait_ge(chan_ready, 2)
            for layer in range(2):
                adaln(layer)
                pe.wait_ge(ada_evac, 12 * layer + 12)
                pe.wait_ge(ada_gcopy, 4 * layer + 4)
                transpose_h(2 * layer)
                if layer == 0:
                    attention()
                else:
                    convolution()
                pe.wait_ge(x_mix, 4 * layer + 4)
                transpose_h(2 * layer + 1)
                routing(layer)
                pe.wait_ge(routed, 3 * layer + 3)
                experts(layer)
                overflow(layer)
            pe.wait_ge(x_moe, 2)
            for q in range(2):
                mm = row_bcast(bank[4 + q][:, :], R_FIN + q, True)
            mm.then_inc(fin_mm, 1)

        @block.scalar
        def _(sc):
            def square_sums(ni):
                for t in range(2):
                    sc.activation(h[:, t, :], x[:, t, :], ACT.Square,
                                  accum_out=stat[:, t:t + 1]).then_inc(ssq, 1)
                sc.wait_ge(ms_ready, ni + 1)
                sc.activation(stat[:, 4:6], stat[:, 2:4], ACT.Sqrt).then_inc(rms_ready, 1)

            def evac_hT(ni):
                for q in range(2):
                    sc.wait_ge(hT_mm, 4 * ni + q + 1)
                    evac_transposed(lambda o, i_: sc.activation(o, i_, ACT.Copy), ni, 0, q).then_inc(hT_act, 1)

            def adaln(layer):
                if layer:
                    sc.wait_ge(x_moe, layer)

                def part(n):
                    sc.wait_ge(pe_used, BASE_MIX[layer] + 2 * n + 2)
                    if n >= 2:
                        sc.wait_ge(ada_mm, 12 * layer + n - 1)
                    sc.activation(ada_part[:, n % 2, :], bank[n % 2][:, :], ACT.Copy).then_inc(part_evac, 1)

                def weights(n):
                    i, j = n // 6, n % 6
                    if j in (2, 3):
                        q = j - 2
                        sc.wait_ge(ada_gmm, 4 * layer + 2 * i + q + 1)
                        sc.activation(mod[:, 3 * i + 1, q * 512:(q + 1) * 512], bank[6 + q][:, :],
                                      ACT.Copy).then_inc(ada_gcopy, 1)

                for n in range(14):
                    if n < 12:
                        high(sc, BASE_MIX[layer] + 2 * n)
                        high(sc, BASE_MIX[layer] + 2 * n + 1)
                    if 1 <= n < 13:
                        part(n - 1)
                    if n >= 2:
                        weights(n - 2)

            def attention():
                for n in range(6):
                    sc.wait_ge(pe_used, ADA_BLOCKS + 2 * n + 2)
                    sc.activation(qkv[:, 0, n * 512:(n + 1) * 512], bank[4 + 2 * (n % 2)][:, :],
                                  ACT.Copy).then_inc(qkv_c, 1)
                sc.wait_ge(qkv_c, 6)
                sc.dma_start(new_k, qkv[:, 0, D:2 * D]).then_inc(out_kv, 16)
                sc.dma_start(new_v, qkv[:, 0, 2 * D:3 * D]).then_inc(out_kv, 16)
                for m in range(0, len(QK_ITEMS), 2):
                    sc.wait_ge(qk_mm, m + 1)
                    if QK_ITEMS[m][:2] == (0, 0):
                        sc.wait_ge(roped, 1)
                    sc.activation(qk_target(m), bank[m % 4][:, :], ACT.Copy).then_inc(qkT_act, 1)
                for un in range(2 * NH + 2):
                    if un < 2 * NH:
                        g = un % 2
                        w = (g + 1) * P
                        sc.wait_ge(max_done, un + 1)
                        if un >= 2:
                            sc.wait_ge(pT_mm, un - 1)
                        else:
                            sc.wait_ge(qk_mm, len(QK_ITEMS))
                        for m in range(2):
                            sc.activation(probs[:, un % 2, m * 256:m * 256 + w],
                                          bank[4 + 2 * (un % 2) + m][:, 0:w], ACT.Exp,
                                          bias=stat[:, 8 + 2 * (un % 2) + m:9 + 2 * (un % 2) + m],
                                          scale=HD ** -0.5,
                                          accum_out=stat[:, 12 + 2 * (un % 2) + m:13 + 2 * (un % 2) + m])\
                              .then_inc(exp_done, 1)
                    if 1 <= un <= 2 * NH:
                        v = un - 1
                        w = (v % 2 + 1) * P
                        sc.wait_ge(pT_mm, v + 1)
                        if v >= 2:
                            sc.wait_ge(pv_mm, v - 1)
                        sc.activation(probsT[:, v % 2, 0:v % 2 + 1, :], bank[v % 2][:, 0:w],
                                      ACT.Copy).then_inc(pT_evac, 1)
                    if un >= 2:
                        v = un - 2
                        sc.wait_ge(pv_mm, v + 1)
                        sc.activation(h[:, v % 2, (v // 2) * P:(v // 2 + 1) * P], bank[2 + v % 2][:, 0:P],
                                      ACT.Copy).then_inc(o_evac, 1)
                sc.wait_ge(sub_ms, 1)
                sc.activation(stat[:, 32:48], stat[:, 16:32], ACT.Sqrt).then_inc(sub_rms, 1)
                for m in range(4):
                    g, q = m // 2, m % 2
                    sc.wait_ge(oT_mm, m + 1)
                    sc.activation(oT[:, 4 * q:4 * q + 4, :, g * HT:(g + 1) * HT],
                                  bank[m][:, :].rearrange("p (c t i) -> p c t i", c=4, t=2),
                                  ACT.Copy, scale=chan[:, V_SUB:V_SUB + 1]).then_inc(oT_evac, 1)

            def convolution():
                for cc in range(DC):
                    q, k = cc // 4, cc % 4
                    sc.wait_ge(pe_used, BASE_MIX[1] + ADA_BLOCKS + 4 * q + 4)
                    if cc >= 2:
                        sc.wait_ge(u_done, cc - 1)
                    sc.activation(sig[:, cc % 2, :], bank[4 * q + 2 + k // 2][:, (k % 2) * 256:(k % 2) * 256 + 256],
                                  ACT.Sigmoid, bias=chan[:, V_BPW1 + DC + cc:V_BPW1 + DC + cc + 1])\
                      .then_inc(sig_done, 1)
                sc.wait_ge(centred, 1)
                sc.activation(conv_sq[:, :, :, :], conv[:, :, :, :], ACT.Square).then_inc(squared, 1)
                sc.wait_ge(var_ready, 1)
                sc.activation(rstd_c[:, :], mean[:, :], ACT.Sqrt).then_inc(std_ready, 1)
                sc.wait_ge(scaled, 1)
                for c in range(DC):
                    sc.activation(conv_act[:, c, :, :, :].rearrange("p t g i -> p g t i"),
                                  conv[:, c, :, :].rearrange("p g (t i) -> p g t i", t=2),
                                  ACT.Silu, bias=chan[:, V_LNB + c:V_LNB + c + 1],
                                  scale=chan[:, V_LNG + c:V_LNG + c + 1]).then_inc(conv_silu, 1)

            def experts(layer):
                eo, b0 = NE * layer, BASE_MOE[layer]

                def high_tokens(e0, i=None):
                    par = e0 % 2
                    sc.wait_ge(gathered, lin(i, 2, eo + e0 + 1))
                    if eo + e0 >= 2:
                        sc.wait_ge(pe_used, lin(i, RING, b0 + (expert_place(e0 - 2, "U1") + 1 if e0 >= 2 else 0)))
                    sc.activation(xs[:, par, :, 0:SLOTS], X[:, :].rearrange("p (c s) -> p c s", c=DC),
                                  ACT.Copy).then_inc(xs_hi, 1)

                def expert_step(e0, i=None):
                    ahead = blocks_ahead(e0)

                    def split():
                        n = next(ahead)
                        if n is not None:
                            high(sc, b0 + n, i)

                    if e0:
                        sc.wait_ge(pe_used, lin(i, RING, b0 + expert_place(e0 - 1, "U1") + 1))
                        if eo + e0 >= 2:
                            sc.wait_ge(u_folded, lin(i, 2, eo + e0 - 1))
                        sc.activation(u_lo[:, :], U[SLOTS:P, :], ACT.Copy).then_inc(u_low, 1)
                    split()
                    if e0 < NE:
                        sc.wait_ge(pe_used, lin(i, RING, b0 + expert_place(e0, "G1") + 1))
                        if eo + e0:
                            sc.wait_ge(g_folded, lin(i, 2, eo + e0))
                        sc.activation(g_lo[:, :], G[SLOTS:P, :], ACT.Copy).then_inc(g_low, 1)
                    if e0:
                        sc.wait_ge(actT_mm, lin(i, 2, eo + e0))
                        if eo + e0 >= 2:
                            sc.wait_ge(pe_used, lin(i, RING, b0 + (expert_place(e0 - 1, "D1") + 1 if e0 >= 2 else 0)))
                        sc.activation(actT[:, :, 0:SLOTS], X[:, :].rearrange("p (c s) -> p c s", c=FC)[:, :, 0:SLOTS],
                                      ACT.Copy).then_inc(as_hi, 1)
                    split()
                    if e0 < NE:
                        sc.wait_ge(g_folded, lin(i, 2, eo + e0 + 1))
                        if eo + e0:
                            sc.wait_ge(act_done, lin(i, 2, eo + e0))
                        sc.activation(g_silu[:, :], g_sum[:, :], ACT.Silu).then_inc(silu_done, 1)
                    split()
                    if e0:
                        high_result(e0, 0, i)
                    split()
                    if e0 + 1 < NE:
                        high_tokens(e0 + 1, i)
                    split()
                    if e0:
                        high_result(e0, 1, i)
                    if e0 < NE:
                        sc.wait_ge(sel_mm, lin(i, 2, eo + e0 + 1))
                        if eo + e0 >= 2:
                            sc.wait_ge(scat, lin(i, 4, 2 * (eo + e0 - 1)))
                        if eo + e0:
                            sc.wait_ge(act_done, lin(i, 2, eo + e0))
                        sc.activation(selT[:, e0 % 2, :, :], X[:, 0:2 * P], ACT.Copy).then_inc(sel_evac, 1)
                        sc.activation(gate_slot[:, :], X[:, 2 * P:2 * P + 1], ACT.Copy).then_inc(sel_evac, 1)
                    split()

                def high_result(e0, hf, i=None):
                    sc.wait_ge(pe_used, lin(i, RING, b0 + expert_place(e0, f"D{hf}") + 1))
                    if eo + e0 >= 2:
                        sc.wait_ge(scat, lin(i, 4, 2 * (eo + e0 - 2) + hf + 1))
                    sc.activation(yh[:, hf, :], DN[:, :], ACT.Copy).then_inc(yh_done, 1)

                sc.wait_ge(out_kv, 32)
                high(sc, b0)
                high(sc, b0 + 1)
                high_tokens(0)
                expert_step(0)
                expert_step(1)
                with sc.Fori(0, 6) as i:
                    expert_step(2, i)
                    expert_step(3, i)
                for e0 in range(14, NE + 1):
                    expert_step(e0)

            def overflow(layer):
                o = over[layer]
                n_over = sc.value_load(flag[0:1, 0:1], min_val=0, max_val=1)
                with sc.If(n_over > 0):
                    for r in range(OVER):
                        with sc.Fori(0, NE) as e:
                            sc.wait_ge(o["pe"], e * OV_PE + (r * NE * OV_PE + 2))
                            sc.activation(over_g[0:SLOTS, 0, :], G[0:SLOTS, :], ACT.Silu).then_inc(o["act"], 1)

            for dst, src in SMALL:
                sc.dma_start(dst, src).then_inc(in_vec, 16)
            for t in range(2):
                sc.dma_start(x[0:HT, t, :], mixed(xp, t, 0)).then_inc(in_x, 16)
                sc.dma_start(x[HT:P, t, :], mixed(xl, t, 1)).then_inc(in_x, 16)
            sc.dma_start(cache_v_sb[:, :], a["cache_v"][0, 0].rearrange("t h e -> t (h e)")).then_inc(in_cache_v, 16)
            sc.wait_ge(in_first, IN_FIRST)
            sc.activation(silu_c[:, :, :], cond[:, :, :], ACT.Silu).then_inc(cond_silu, 1)
            sc.wait_ge(lam_sums, 2)
            sc.activation(lam[:, 2:4], lam[:, 0:2], ACT.Exp).then_inc(lam_exp, 1)
            for layer in range(2):
                adaln(layer)
                if layer:
                    sc.wait_ge(pe_used, BASE_MIX[1] + ADA_BLOCKS)
                    sc.dma_start(wdw_rows[:, :], a["conv_w_dw"][0]).then_inc(in_wdw, 16)
                else:
                    sc.wait_ge(pe_used, ADA_BLOCKS)
                    sc.dma_start(cache_k_sb[:, :], a["cache_k"][0, 0].rearrange("t h e -> t (h e)"))\
                      .then_inc(in_cache_k, 16)
                    sc.wait_ge(in_x, 64)
                square_sums(2 * layer)
                evac_hT(2 * layer)
                if layer == 0:
                    attention()
                else:
                    convolution()
                sc.wait_ge(x_mix, 4 * layer + 4)
                square_sums(2 * layer + 1)
                evac_hT(2 * layer + 1)
                sc.wait_ge(logits_mm, layer + 1)
                sc.activation(rs[:, 0, :], G[:, 0:2 * NE], ACT.Sigmoid).then_inc(scores_ready, 1)
                sc.wait_ge(routed, 3 * layer + 3)
                experts(layer)
                overflow(layer)
            sc.wait_ge(x_moe, 2)
            square_sums(4)

        def depthwise(eng, chunks, done):
            n = len(chunks)
            for k in range(KW):
                for ci, c in enumerate(chunks):
                    if k:
                        eng.wait_ge(done, (k - 1) * n + ci + 1)
                    shifted = u_pad[:, c, :, k:k + T]
                    if k == 0:
                        ins = eng.tensor_scalar(conv[:, c, :, :], shifted, wdw[:, c, 0:1],
                                                chan[:, V_BDW + c:V_BDW + c + 1], ALU.mult, ALU.add)
                    else:
                        ins = eng.scalar_tensor_tensor(out=conv[:, c, :, :], in0=shifted,
                                                       scalar=wdw[:, c, k:k + 1], in1=conv[:, c, :, :],
                                                       op0=ALU.mult, op1=ALU.add)
                    ins.then_inc(done, 1)

        @block.gpsimd
        def _(pool):
            pool.wait_ge(pe_used, BASE_MIX[1] + ADA_BLOCKS)
            for lo in (0, PAD + T):
                pool.memset(u_pad[:, :, :, lo:lo + PAD], 0.0).then_inc(pads_zero, 1)

        @block.vector
        def _(ve):
            chain = [0]

            def link(ins):
                chain[0] += 1
                ins.then_inc(dve_chain, 1)
                ve.wait_ge(dve_chain, chain[0])

            def adaln(layer):
                if layer:
                    ve.wait_ge(x_moe, layer)
                else:
                    ve.wait_ge(cond_silu, 1)
                for g in range(2):
                    c32 = silu_c[:, g, :].unsqueeze(2).broadcast_to([P, DC, 32])
                    ve.tensor_copy(condT[:, :, 2 * g, :], c32).then_inc(condT_ready, 1)
                    ve.wait_ge(condT_ready, 4 * layer + 2 * g + 1)
                    ve.tensor_tensor(condT[:, :, 2 * g + 1, :], c32, condT[:, :, 2 * g, :],
                                     ALU.subtract).then_inc(condT_ready, 1)

                def finish(n):
                    i, j = n // 6, n % 6
                    ve.wait_ge(ada_mm, 12 * layer + n + 1)
                    dst = mod[:, 3 * i + j // 2, (j % 2) * 512:(j % 2) * 512 + 512]
                    src = bank[2 + n % 4][:, :]
                    if j in (2, 3):
                        ve.wait_ge(ada_gcopy, 4 * layer + 2 * i + j - 1)
                        ins = ve.scalar_tensor_tensor(out=dst, in0=src, scalar=1.0, in1=dst,
                                                      op0=ALU.add, op1=ALU.mult)
                    else:
                        ins = ve.tensor_copy(dst, src)
                    ins.then_inc(ada_evac, 1)

                for n in range(14):
                    if n < 12:
                        low(ve, BASE_MIX[layer] + 2 * n)
                        low(ve, BASE_MIX[layer] + 2 * n + 1)
                    if n >= 2:
                        finish(n - 2)

            def rms(ni):
                ve.wait_ge(ssq, 2 * ni + 2)
                ve.tensor_scalar(stat[:, 2:4], stat[:, 0:2], 1.0 / D, EPS, ALU.mult, ALU.add).then_inc(ms_ready, 1)
                ve.wait_ge(rms_ready, ni + 1)
                link(ve.reciprocal(stat[:, 6:8], stat[:, 4:6]))

            def norm_mod(ni):
                layer, w = ni // 2, ni % 2
                rms(ni)
                ve.wait_ge(ada_evac, 12 * layer + 6 * w + 4)
                for t in range(2):
                    link(ve.scalar_tensor_tensor(out=h[:, t, :], in0=x[:, t, :], scalar=stat[:, 6 + t:7 + t],
                                                 in1=mod[:, 3 * w + 1, :], op0=ALU.mult, op1=ALU.mult))
                    ve.tensor_tensor(h[:, t, :], h[:, t, :], mod[:, 3 * w, :], ALU.add).then_inc(h_ready, 1)
                for q in range(2):
                    ve.wait_ge(hT_mm, 4 * ni + 2 + q + 1)
                    evac_transposed(ve.tensor_copy, ni, 1, q).then_inc(hT_dve, 1)

            def add_gated(layer, gate):
                for n in range(2):
                    ve.wait_ge(pe_used, BASE_MOE[layer] - 2 + 2 * n)
                    for t in range(2):
                        cols = slice(n * 512, (n + 1) * 512)
                        link(ve.tensor_tensor(h[:, t, cols], bank[4 + 2 * n + t][:, :], mod[:, gate, cols], ALU.mult))
                        ve.tensor_tensor(x[:, t, cols], x[:, t, cols], h[:, t, cols], ALU.add).then_inc(x_mix, 1)
                ve.wait_ge(x_mix, 4 * layer + 4)

            def attention():
                for n in range(6):
                    ve.wait_ge(pe_used, ADA_BLOCKS + 2 * n + 2)
                    ve.tensor_copy(qkv[:, 1, n * 512:(n + 1) * 512], bank[5 + 2 * (n % 2)][:, :]).then_inc(qkv_l, 1)
                ve.wait_ge(qkv_l, 6)
                qk = qkv[:, 1, 0:2 * D].rearrange("p (n a two f) -> p n a two f", n=32, a=2, two=2)
                x1, x2 = qk[:, :, :, 0, :], qk[:, :, :, 1, :]
                cos, sin = (cst[:, c0:c0 + 32].rearrange("p (a f) -> p a f", a=2).unsqueeze(1)
                            .broadcast_to([P, 32, 2, 16]) for c0 in (C_COS, C_SIN))
                s1, s2 = rope_tmp[:, 0], rope_tmp[:, 1]
                ve.tensor_tensor(s1, x1, sin, ALU.mult)
                link(ve.tensor_tensor(s2, x2, sin, ALU.mult))
                ve.tensor_tensor(x1, x1, cos, ALU.mult)
                link(ve.tensor_tensor(x2, x2, cos, ALU.mult))
                ve.tensor_tensor(x1, x1, s2, ALU.subtract)
                ve.tensor_tensor(x2, x2, s1, ALU.add).then_inc(roped, 1)
                for m in range(1, len(QK_ITEMS), 2):
                    ve.wait_ge(qk_mm, m + 1)
                    if QK_ITEMS[m][0] == 0:
                        ve.wait_ge(roped, 1)
                    ve.tensor_copy(qk_target(m), bank[m % 4][:, :].rearrange("p (c i) -> p c i", c=4))\
                      .then_inc(qkT_dve, 1)
                for un in range(2 * NH + 1):
                    if un < 2 * NH:
                        b = un % 2
                        w = (b + 1) * P
                        ve.wait_ge(scores_mm, un + 1)
                        for m in range(2):
                            ins = ve.reduce_max(stat[:, 48 + 2 * b + m:49 + 2 * b + m],
                                                bank[4 + 2 * b + m][:, 0:w], AX)
                        link(ins)
                        ve.tensor_scalar(stat[:, 8 + 2 * b:10 + 2 * b], stat[:, 48 + 2 * b:50 + 2 * b],
                                         -HD ** -0.5, None, ALU.mult).then_inc(max_done, 1)
                    if un:
                        v = un - 1
                        b = v % 2
                        w = (b + 1) * P
                        ve.wait_ge(exp_done, 2 * v + 2)
                        link(ve.reciprocal(stat[:, 52 + 2 * b:54 + 2 * b], stat[:, 12 + 2 * b:14 + 2 * b]))
                        link(ve.tensor_tensor(stat[:, 53 + 2 * b:54 + 2 * b], stat[:, 53 + 2 * b:54 + 2 * b],
                                              lam[:, 4:5], ALU.mult))
                        link(ve.tensor_scalar(probs[:, b, 256:256 + w], probs[:, b, 256:256 + w],
                                              stat[:, 53 + 2 * b:54 + 2 * b], None, ALU.mult))
                        ve.scalar_tensor_tensor(out=probs[:, b, 0:w], in0=probs[:, b, 0:w],
                                                scalar=stat[:, 52 + 2 * b:53 + 2 * b],
                                                in1=probs[:, b, 256:256 + w], op0=ALU.mult,
                                                op1=ALU.subtract).then_inc(combined, 1)
                ve.wait_ge(o_evac, 2 * NH)
                link(ve.tensor_tensor(o_sq[:, :, :], h[:, :, :], h[:, :, :], ALU.mult))
                link(ve.reduce_sum(stat[:, 16:32], o_sq[:, :, :].rearrange("p g (n e) -> p (g n) e", n=NH), AX))
                ve.tensor_scalar(stat[:, 16:32], stat[:, 16:32], 1.0 / P, EPS, ALU.mult, ALU.add).then_inc(sub_ms, 1)
                ve.wait_ge(sub_rms, 1)
                link(ve.reciprocal(stat[:, 56:72], stat[:, 32:48]))
                o = h[:, :, :].rearrange("p g (n e) -> p (g n) e", n=NH)
                ve.tensor_tensor(o, o, stat[:, 56:72].unsqueeze(2).broadcast_to([P, 16, P]), ALU.mult)\
                  .then_inc(o_normed, 1)

            def convolution():
                ve.wait_ge(wdw_mm, 1)
                ve.tensor_copy(wdw[:, :, :], X[:, 0:DC * KW].rearrange("p (c k) -> p c k", c=DC))\
                  .then_inc(wdw_ready, 1)
                ve.wait_ge(pads_zero, 2)
                for cc in range(DC):
                    q, k = cc // 4, cc % 4
                    ve.wait_ge(sig_done, cc + 1)
                    ve.scalar_tensor_tensor(out=u_pad[:, cc, :, PAD:PAD + T],
                                            in0=bank[4 * q + k // 2][:, (k % 2) * 256:(k % 2) * 256 + 256]
                                            .rearrange("p (g i) -> p g i", g=2),
                                            scalar=chan[:, V_BPW1 + cc:V_BPW1 + cc + 1],
                                            in1=sig[:, cc % 2, :].rearrange("p (g i) -> p g i", g=2),
                                            op0=ALU.add, op1=ALU.mult).then_inc(u_done, 1)
                ve.wait_ge(u_done, DC)
                depthwise(ve, range(CONV_DVE), conv_dve)
                ve.wait_ge(sum_mm, 1)
                link(ve.tensor_scalar(mean[:, :], bank[0][:, 0:256], 1.0 / D, None, ALU.mult))
                all_c = conv[:, :, :, :].rearrange("p c g i -> p c (g i)")
                ve.tensor_tensor(all_c, all_c, mean[:, :].unsqueeze(1).broadcast_to([P, DC, 2 * T]),
                                 ALU.subtract).then_inc(centred, 1)
                ve.wait_ge(var_mm, 1)
                ve.wait_ge(centred, 1)
                ve.tensor_scalar(mean[:, :], bank[1][:, 0:256], 1.0 / D, EPS, ALU.mult, ALU.add)\
                  .then_inc(var_ready, 1)
                ve.wait_ge(std_ready, 1)
                link(ve.reciprocal(rstd_c[:, :], rstd_c[:, :]))
                ve.tensor_tensor(all_c, all_c, rstd_c[:, :].unsqueeze(1).broadcast_to([P, DC, 2 * T]),
                                 ALU.mult).then_inc(scaled, 1)

            def first_max(out, v, n, prio, scratch, top):
                shape = [P, 2, n]
                link(ve.tensor_reduce(top, v, AX, ALU.max))
                link(ve.tensor_tensor(scratch, v, top.unsqueeze(2).broadcast_to(shape), ALU.is_equal))
                link(ve.tensor_tensor(scratch, scratch, prio.unsqueeze(1).broadcast_to(shape), ALU.mult))
                link(ve.tensor_reduce(top, scratch, AX, ALU.max))
                link(ve.tensor_tensor(out, scratch, top.unsqueeze(2).broadcast_to(shape), ALU.is_equal))

            def routing(layer):
                ve.wait_ge(scores_ready, layer + 1)
                def row(k, n=NE):
                    return rs[:, k, 0:2 * n].rearrange("p (t e) -> p t e", t=2)

                score, sel = row(0), row(1)
                prio4 = cst[:, C_PR4:C_PR4 + NG]
                prio16 = cst[:, C_PR16:C_PR16 + NE]
                link(ve.tensor_tensor(sel, score, bias_b[:, :].unsqueeze(1).broadcast_to([P, 2, NE]), ALU.add))
                s = rs[:, 1, :].rearrange("p (g k) -> p g k", k=4)
                pair = rs[:, 2:4, :].rearrange("p a b -> p (a b)")[:, 0:48].rearrange("p (g k) -> p g k", k=6)
                ve.tensor_tensor(pair[:, :, 0:2], s[:, :, 0:4:2], s[:, :, 1:4:2], ALU.add)
                ve.tensor_tensor(pair[:, :, 2:4], s[:, :, 0:2], s[:, :, 2:4], ALU.add)
                ve.tensor_tensor(pair[:, :, 4:5], s[:, :, 0:1], s[:, :, 3:4], ALU.add)
                link(ve.tensor_tensor(pair[:, :, 5:6], s[:, :, 1:2], s[:, :, 2:3], ALU.add))
                link(ve.tensor_reduce(rs[:, 4, 0:8], pair, AX, ALU.max))
                best = row(6, NG)
                first_max(best, row(4, NG), NG, prio4, row(5, NG), rs[:, 7, 0:2])
                link(ve.tensor_scalar(best, best, BIG, -BIG, ALU.mult, ALU.add))
                v4 = rs[:, 8, :].rearrange("p (g k) -> p g k", k=4)
                link(ve.tensor_tensor(v4, s, rs[:, 6, 0:8].unsqueeze(2).broadcast_to([P, 8, 4]), ALU.add))
                v, one, two = row(8), row(9), row(10)
                first_max(one, v, NE, prio16, row(5), rs[:, 7, 0:2])
                link(ve.scalar_tensor_tensor(out=v, in0=one, scalar=-2.0 * BIG, in1=v, op0=ALU.mult, op1=ALU.add))
                first_max(two, v, NE, prio16, row(5), rs[:, 7, 0:2])
                ve.tensor_tensor(asg[:, :, :], one, two, ALU.add).then_inc(assigned, 1)
                ve.wait_ge(assigned, layer + 1)
                link(ve.tensor_tensor(row(11), score, asg[:, :, :], ALU.mult))
                link(ve.reduce_sum(rs[:, 7, 0:2], row(11), AX))
                link(ve.reciprocal(rs[:, 7, 2:4], rs[:, 7, 0:2]))
                ve.tensor_tensor(gates[:, :, :], row(11), rs[:, 7, 2:4].unsqueeze(2).broadcast_to([P, 2, NE]),
                                 ALU.mult).then_inc(routed, 1)
                link(ve.tensor_scalar(row(9), asg[:, :, :], -FAR, FAR, ALU.mult, ALU.add))
                ve.wait_ge(pos_mm, layer + 1)
                ve.tensor_tensor(pos[:, :, :], row(9), U[:, 0:2 * NE].rearrange("p (t e) -> p t e", t=2),
                                 ALU.add).then_inc(routed, 1)
                link(ve.reduce_max(rs[:, 7, 4:5], U[:, 2 * NE:3 * NE], AX))
                link(ve.tensor_scalar(rs[:, 7, 5:6], rs[:, 7, 4:5], CAP + 0.5, None, ALU.is_gt))
                ve.tensor_copy(flag[:, 0:1], rs[:, 7, 5:6]).then_inc(routed, 1)
                ve.wait_ge(routed, 3 * layer + 3)

            def experts(layer):
                eo, b0 = NE * layer, BASE_MOE[layer]

                def build_p2(e0, i=None):
                    e = lin(i, 2, e0)
                    par = e0 % 2
                    if eo + e0 >= 2:
                        ve.wait_ge(sel_mm, lin(i, 2, eo + e0 - 1))
                    for t in range(2):
                        ve.tensor_scalar(p2[:, par, t, :], cst[:, C_SLOT:C_SLOT + P], pos[:, t, bass.ds(e, 1)],
                                         None, ALU.is_equal).then_inc(p2_built, 1)
                    ve.tensor_copy(gate_tok[:, par, :], gates[:, :, bass.ds(e, 1)].rearrange("p t o -> p (t o)"))\
                      .then_inc(p2_built, 1)

                def low_tokens(e0, i=None):
                    par = e0 % 2
                    ve.wait_ge(xs_hi, lin(i, 2, eo + e0 + 1))
                    ve.tensor_tensor(xs[:, par, :, SLOTS:P], X[:, :].rearrange("p (c s) -> p c s", c=DC),
                                     xs[:, par, :, 0:SLOTS], ALU.subtract).then_inc(xs_lo, 1)

                def low_result(e0, hf, i=None):
                    ve.wait_ge(yh_done, lin(i, 4, 2 * (eo + e0 - 1) + hf + 1))
                    ve.tensor_tensor(yl[:, hf, :], DN[:, :], yh[:, hf, :], ALU.subtract).then_inc(yl_done, 1)

                def expert_step(e0, i=None):
                    ahead = blocks_ahead(e0)

                    def split():
                        n = next(ahead)
                        if n is not None:
                            low(ve, b0 + n, i)

                    if e0:
                        ve.wait_ge(u_low, lin(i, 2, eo + e0))
                        if eo + e0 >= 2:
                            ve.wait_ge(act_done, lin(i, 2, eo + e0 - 1))
                        ve.tensor_tensor(u_sum[:, :], U[0:SLOTS, :], u_lo[:, :], ALU.add).then_inc(u_folded, 1)
                        ve.wait_ge(silu_done, lin(i, 2, eo + e0))
                        ve.wait_ge(u_folded, lin(i, 2, eo + e0))
                        ve.wait_ge(sel_evac, lin(i, 4, 2 * (eo + e0)))
                        if eo + e0 >= 2:
                            ve.wait_ge(actT_mm, lin(i, 2, eo + e0 - 1))
                        ve.scalar_tensor_tensor(out=act[0:SLOTS, :], in0=g_silu[:, :], scalar=gate_slot[0:SLOTS, :],
                                                in1=u_sum[:, :], op0=ALU.mult, op1=ALU.mult).then_inc(act_done, 1)
                    if e0 + 1 < NE:
                        build_p2(e0 + 1, i)
                    split()
                    if e0 < NE:
                        ve.wait_ge(g_low, lin(i, 2, eo + e0 + 1))
                        if eo + e0:
                            ve.wait_ge(silu_done, lin(i, 2, eo + e0))
                        ve.tensor_tensor(g_sum[:, :], G[0:SLOTS, :], g_lo[:, :], ALU.add).then_inc(g_folded, 1)
                    if e0:
                        ve.wait_ge(as_hi, lin(i, 2, eo + e0))
                        ve.tensor_tensor(actT[:, :, SLOTS:P],
                                         X[:, :].rearrange("p (c s) -> p c s", c=FC)[:, :, 0:SLOTS],
                                         actT[:, :, 0:SLOTS], ALU.subtract).then_inc(as_lo, 1)
                    split()
                    split()
                    if e0:
                        low_result(e0, 0, i)
                    split()
                    if e0 + 1 < NE:
                        low_tokens(e0 + 1, i)
                    split()
                    if e0:
                        low_result(e0, 1, i)
                    split()

                ve.memset(act[SLOTS:P, :], 0.0)
                build_p2(0)
                low(ve, b0)
                low(ve, b0 + 1)
                low_tokens(0)
                expert_step(0)
                expert_step(1)
                with ve.Fori(0, 6) as i:
                    expert_step(2, i)
                    expert_step(3, i)
                for e0 in range(14, NE + 1):
                    expert_step(e0)
                ve.wait_ge(scat, 2 * NE * (layer + 1))
                for t in range(2):
                    for hf in range(2):
                        cols = slice(hf * 512, (hf + 1) * 512)
                        link(ve.tensor_tensor(moe_tmp[:, 2 * t + hf, :], ACC[2 * t + hf][:, :], mod[:, 5, cols],
                                              ALU.mult))
                        ve.tensor_tensor(x[:, t, cols], x[:, t, cols], moe_tmp[:, 2 * t + hf, :],
                                         ALU.add).then_inc(x_add, 1)
                ve.wait_ge(x_add, 4 * layer + 4)

            def overflow(layer):
                o = over[layer]
                n_over = ve.value_load(flag[0:1, 0:1], min_val=0, max_val=1)
                with ve.If(n_over > 0):
                    ve.memset(over_g[SLOTS:P, 1, :], 0.0).then_inc(o["dve"], 1)
                    for r in range(OVER):
                        with ve.Fori(0, NE) as e:
                            done = [0]

                            def sig_step(ins):
                                done[0] += 1
                                ins.then_inc(o["dve"], 1)
                                ve.wait_ge(o["dve"], e * OV_DVE + (r * NE * OV_DVE + 1 + done[0]))

                            def pe_at(s):
                                ve.wait_ge(o["pe"], e * OV_PE + (r * NE * OV_PE + s))

                            for t in range(2):
                                sig_step(ve.tensor_scalar(over_p[:, t, :], cst[:, C_OVER:C_OVER + SLOTS],
                                                          float(r * SLOTS), pos[:, t, bass.ds(e, 1)],
                                                          ALU.add, ALU.is_equal))
                            sig_step(ve.tensor_copy(gate_tok[:, 0, :],
                                                    gates[:, :, bass.ds(e, 1)].rearrange("p t o -> p (t o)")))
                            pe_at(1)
                            sig_step(ve.tensor_copy(over_x[:, :, :],
                                                    bank[0][:, :].rearrange("p (c s) -> p c s", c=DC)))
                            sig_step(ve.tensor_copy(gate_slot[0:SLOTS, :], bank[2][0:SLOTS, 0:1]))
                            sig_step(ve.tensor_copy(over_pT[:, :, :], bank[1][0:SLOTS, 0:2 * P]
                                                    .rearrange("p (t i) -> p t i", t=2)))
                            ve.wait_ge(o["act"], e + (r * NE + 1))
                            sig_step(ve.scalar_tensor_tensor(out=over_g[0:SLOTS, 1, :],
                                                             in0=over_g[0:SLOTS, 0, :],
                                                             scalar=gate_slot[0:SLOTS, :], in1=U[0:SLOTS, :],
                                                             op0=ALU.mult, op1=ALU.mult))
                            pe_at(3)
                            sig_step(ve.tensor_copy(over_aT[:, :, :], bank[3][:, :]
                                                    .rearrange("p (c s) -> p c s", c=FC)[:, :, 0:SLOTS]))
                            pe_at(4)
                            for hf, y in enumerate((DN, X)):
                                sig_step(ve.tensor_copy(over_y[:, hf * 512:(hf + 1) * 512], y[0:SLOTS, :]))
                            pe_at(5)
                            for t in range(2):
                                for hf in range(2):
                                    cols = slice(hf * 512, (hf + 1) * 512)
                                    sig_step(ve.tensor_tensor(over_t[:, t, cols], ACC[2 * t + hf][:, :],
                                                              mod[:, 5, cols], ALU.mult))
                            for t in range(2):
                                for hf in range(2):
                                    cols = slice(hf * 512, (hf + 1) * 512)
                                    sig_step(ve.tensor_tensor(x[:, t, cols], x[:, t, cols],
                                                              over_t[:, t, cols], ALU.add))
                            assert done[0] == OV_DVE
                ve.memset(lam[:, 7:8], 0.0).then_inc(x_moe, 1)

            ve.wait_ge(in_vec, IN_VEC)
            ve.wait_ge(in_first, IN_FIRST)
            for k in range(2):
                link(ve.tensor_tensor(lam_in[:, 2 * k, :], lam_in[:, 2 * k, :], lam_in[:, 2 * k + 1, :], ALU.mult))
                ve.reduce_sum(lam[:, k:k + 1], lam_in[:, 2 * k, :], AX).then_inc(lam_sums, 1)
            ve.wait_ge(lam_exp, 1)
            link(ve.scalar_tensor_tensor(out=lam[:, 4:5], in0=lam[:, 2:3], scalar=LAMBDA_INIT, in1=lam[:, 3:4],
                                         op0=ALU.add, op1=ALU.subtract))
            ve.wait_ge(chan_mm, 1)
            ve.tensor_copy(chan[:, 0:V_SUB], X[:, 0:V_SUB]).then_inc(chan_ready, 1)
            ve.tensor_scalar(chan[:, V_SUB:V_ALL], X[:, V_SUB:V_ALL], 1.0 - LAMBDA_INIT, None, ALU.mult)\
              .then_inc(chan_ready, 1)
            for layer in range(2):
                adaln(layer)
                norm_mod(2 * layer)
                if layer == 0:
                    attention()
                else:
                    convolution()
                add_gated(layer, 2)
                norm_mod(2 * layer + 1)
                routing(layer)
                experts(layer)
                overflow(layer)
            rms(4)
            ve.wait_ge(fin_mm, 1)
            for t in range(2):
                for q in range(2):
                    cols = slice(q * 512, (q + 1) * 512)
                    ins = ve.scalar_tensor_tensor(out=h[:, t, cols], in0=x[:, t, cols],
                                                  scalar=stat[:, 6 + t:7 + t], in1=bank[4 + q][:, :],
                                                  op0=ALU.mult, op1=ALU.mult)
                ins.then_inc(h_ready, 1)


_INS = ['x_prompt', 'x_sample', 'cache_k', 'cache_v', 'c', 'c_ctx', 'norm1_g', 'norm2_g', 'ada_w', 'ada_b',
        'attn_w_qkv', 'attn_w_o', 'attn_lambda_q1', 'attn_lambda_k1', 'attn_lambda_q2', 'attn_lambda_k2',
        'attn_subln_g', 'conv_w_pw1', 'conv_b_pw1', 'conv_w_dw', 'conv_b_dw', 'conv_ln_g', 'conv_ln_b',
        'conv_w_pw2', 'conv_b_pw2', 'router_w', 'router_bias', 'moe_w_gate', 'moe_w_up', 'moe_w_down',
        'final_norm_g']


def kernel(**inputs):
    import concourse.bacc as bacc
    from concourse.bass_utils import run_bass_kernel_spmd

    nc = bacc.Bacc("TRN2", target_bir_lowering=False, num_devices=1)
    arrays, a = {}, {}
    for name in _INS:
        arr = np.ascontiguousarray(inputs[name])
        arrays[f"in_{name}"] = arr
        a[name] = nc.dram_tensor(f"in_{name}", arr.shape, F32, kind="ExternalInput").ap()
    arrays["in_consts"] = constants()
    a["consts"] = nc.dram_tensor("in_consts", (P, C_ALL), F32, kind="ExternalInput").ap()
    shapes = [(1, T, D), (1, T, D), (1, 1, T, NH, 2 * HD), (1, 1, T, NH, 2 * HD)]
    outs = [nc.dram_tensor(f"out_{i}", s, F32, kind="ExternalOutput").ap() for i, s in enumerate(shapes)]
    trunk_kernel(nc, a, outs[0], outs[1], outs[2][0, 0].rearrange("t h e -> t (h e)"),
                 outs[3][0, 0].rearrange("t h e -> t (h e)"))
    r = run_bass_kernel_spmd(nc, [arrays], core_ids=[0])
    return tuple(r.results[0][f"out_{i}"] for i in range(4))
```

```python
from contextlib import ExitStack

import numpy as np

import concourse.bass as bass
from concourse import mybir

F32 = mybir.dt.float32
F32R = mybir.dt.float32r
I32 = mybir.dt.int32
ALU = mybir.AluOpType
ACT = mybir.ActivationFunctionType
AX = mybir.AxisListType.X

P = 128
D = 1024
DC = D // P
T = 128
HT = T // 2
NH = 8
HD = 64
NE = 16
NG = 4
FE = 512
FC = FE // P
KW = 31
PAD = KW // 2
EPS = 1e-6
LAMBDA_INIT = 0.2
SLOTS = 64
CAP = 64
OVER = 3
FAR = 4096.0
BIG = 1e30

RING = 12
HI = 5
ADA_BLOCKS = 12
QKV_BLOCKS = 12
WO_BLOCKS = 4
PW1_BLOCKS = 8
PW2_BLOCKS = 4
MOE_BLOCKS = 96
MIX0_BLOCKS = ADA_BLOCKS + QKV_BLOCKS + ADA_BLOCKS + WO_BLOCKS
MIX1_BLOCKS = ADA_BLOCKS + PW1_BLOCKS + ADA_BLOCKS + PW2_BLOCKS
BASE_ADA1 = [0, MIX0_BLOCKS + MOE_BLOCKS]
BASE_PROJ = [BASE_ADA1[k] + ADA_BLOCKS for k in range(2)]
BASE_ADA2 = [BASE_PROJ[0] + QKV_BLOCKS, BASE_PROJ[1] + PW1_BLOCKS]
BASE_OUT = [BASE_ADA2[k] + ADA_BLOCKS for k in range(2)]
BASE_MOE = [BASE_OUT[0] + WO_BLOCKS, BASE_OUT[1] + PW2_BLOCKS]
CONV_DVE = DC - 1
TAPS_FIRST = 16
ADA2_BANKS = [(3,), (2, 3)]

C_ID, C_ONE, C_TRI, C_SLOT, C_COS, C_SIN, C_PR4, C_PR16 = 0, 128, 256, 384, 512, 544, 576, 580
C_OVER = 596
C_FOLD = C_OVER + 64
C_ALL = C_FOLD + P
OV_DVE, OV_PE = 18, 5
QK_ITEMS = [(2, 0, 0), (2, 0, 1), (1, 0, 0), (1, 0, 1), (0, 0, 0), (0, 0, 1),
            (0, 1, 0), (0, 1, 1), (1, 1, 0), (1, 1, 1)]
R_ADA = [0, 12]
R_G1 = [24, 26]
R_G2 = [28, 30]
R_FIN = 32
R_PW2 = 34
R_ALL = 36
V_BPW1, V_BDW, V_LNG, V_LNB, V_SUB, V_ALL = 0, 16, 24, 32, 40, 41


def constants():
    c = np.zeros((P, C_ALL), np.float32)
    c[:, C_ID:C_ID + P] = np.eye(P)
    c[:, C_ONE:C_ONE + P] = 1.0
    c[:, C_TRI:C_TRI + P] = np.triu(np.ones((P, P)), 1)
    slot = np.arange(P) % SLOTS
    c[:, C_SLOT:C_SLOT + P] = np.where(slot < CAP, slot, -1.0)
    c[:, C_OVER:C_OVER + SLOTS] = np.arange(SLOTS) + CAP
    for m in range(P):
        c[64 * (m // 64), C_FOLD + m] = c[64 * (m // 64) + 32, C_FOLD + m] = 1.0
    grid_w = 64
    rows = np.repeat(np.arange(T // grid_w, dtype=np.float32), grid_w)
    cols = np.tile(np.arange(grid_w, dtype=np.float32), T // grid_w)
    n_freq = HD // 4
    inv = (np.float32(10000.0) ** (-np.arange(n_freq, dtype=np.float32) / np.float32(n_freq))).astype(np.float32)
    ang = np.stack([rows[:, None] * inv, cols[:, None] * inv], axis=1).astype(np.float32)
    c[:, C_COS:C_COS + 32] = np.cos(ang).reshape(T, 32)
    c[:, C_SIN:C_SIN + 32] = np.sin(ang).reshape(T, 32)
    c[:, C_PR4:C_PR4 + NG] = np.arange(NG, 0, -1)
    c[:, C_PR16:C_PR16 + NE] = np.arange(NE, 0, -1)
    return c


def expert_place(e, what):
    kind, half = "GDU".index(what[0]), int(what[1])
    if e == 0:
        return (0, None, 2)[kind] + half
    return 6 * e - 2 + (half if e == NE else 2 * kind + half)


AHEAD_OF_ALL = [[(0, "G0"), (0, "G1"), (0, "U0")], [(1, "G0"), (1, "G1")]]
NATIVE = "U1"
NOT_SPLIT = {BASE_MOE[k] + expert_place(e, NATIVE) for k in range(2) for e in range(NE)}
for k in range(2):
    NOT_SPLIT |= set(range((BASE_ADA2[0], BASE_PROJ[1])[k], BASE_MOE[k]))
SPLIT = [n for n in range(BASE_MOE[1] + MOE_BLOCKS) if n not in NOT_SPLIT]
SPLITS = 10
HI_SLOT = {n: 3 + (n - BASE_PROJ[0]) % 2 if BASE_PROJ[0] <= n < BASE_ADA2[0]
           else sum(n0 <= b < n for b in SPLIT) % HI
           for n0, n1 in zip([0] + BASE_PROJ[:1] + BASE_MOE[:1] + BASE_ADA1[1:] + BASE_MOE[1:],
                             BASE_PROJ[:1] + BASE_MOE[:1] + BASE_ADA1[1:] + BASE_MOE[1:] + [BASE_MOE[1] + MOE_BLOCKS])
           for n in SPLIT if n0 <= n < n1}


def split_index(n):
    return sum(b < n for b in SPLIT)


def blocks_ahead(e):
    for step, what in ((e, "D1"), (e, "U0"), (e, "U1"), (e + 1, "G0"), (e + 1, "G1"), (e + 1, "D0")):
        exists = ((e > 0 or what == "D0") and what != NATIVE
                  and (0 < step <= NE if what[0] == "D" else step < NE))
        yield expert_place(step, what) if exists else None


def trunk_kernel(nc, a, y_prompt, y_sample, new_k, new_v):
    ctx = ExitStack()
    with ctx:
        base = 16512
        place = [base]

        def at(name, off, shape, dt=F32):
            return nc.alloc_sbuf_tensor_at(name, shape, dt, offset=off)

        def take(n_bytes):
            off = place[0]
            place[0] += (n_bytes + 31) // 32 * 32
            return off

        def sb(name, shape, dt=F32):
            return at(name, take(4 * int(np.prod(shape[1:]))), shape, dt)

        ring = sb("ring", [P, RING, 4, 512])
        w_lo = [at(f"w_lo{k}", base + 8192 * k, [P, 4, 512], F32R) for k in range(RING)]
        split_at = take(6 * 8192)
        w_hi = at("w_hi", split_at, [P, HI, 4, 512], F32R)
        x = sb("x", [P, 2, D])
        h_at = take(8192)
        h = at("h", h_at, [P, 2, D])
        hT_lo = at("hT_lo", h_at, [P, DC, 2, T], F32R)
        mod_at = take(6 * 4096)
        mod = at("mod", mod_at, [P, 6, D])
        hT_at = take(8192)
        hT = at("hT", hT_at, [P, DC, 2, T])
        hT_hi = at("hT_hi", hT_at, [P, DC, 2, T], F32R)
        hTm = at("hTm", hT_at, [P, DC, 2, P])
        moe_tmp = at("moe_tmp", hT_at, [P, 4, 512])
        condT = at("condT", hT_at, [P, DC, 4, 32], F32R)
        condM = at("condM", hT_at, [P, DC, 2, HT])
        g2 = at("g2", hT_at + 4096, [P, D])
        ada_part = at("ada_part", hT_at + 4096, [P, 2, 512])
        xs = at("xs", hT_at, [P, 2, DC, P], F32R)
        yh = at("yh", mod_at, [P, 2, 512], F32R)
        yl = at("yl", mod_at + 4096, [P, 2, 512], F32R)
        g_lo = at("g_lo", mod_at + 8192, [SLOTS, FE])
        g_sum = at("g_sum", mod_at + 10240, [SLOTS, FE])
        g_silu = at("g_silu", mod_at + 12288, [SLOTS, FE])
        u_lo = at("u_lo", mod_at + 14336, [SLOTS, FE])
        u_sum = at("u_sum", mod_at + 16384, [SLOTS, FE])
        act = at("act", mod_at + 18432, [P, FE])
        moe_at = take(2048 + 2048 + 2048)
        actT = at("actT", moe_at, [P, FC, P], F32R)
        selT = at("selT", moe_at + 2048, [P, 2, 2, P], F32R)
        p2 = at("p2", moe_at + 4096, [P, 2, 2, P])
        cache_v_sb = at("cache_v_sb", moe_at, [P, D])
        qkv = at("qkv", split_at, [P, 2, 3 * D])
        qT = at("qT", split_at + 24576, [P, NH, 2, T])
        kT = at("kT", split_at + 32768, [P, NH, 2, T])
        cache_k_sb = at("cache_k_sb", split_at + 40960, [P, D])
        ckT = at("ckT", split_at + 45056, [P, NH, T])
        probs = at("probs", split_at, [P, 2, 512])
        probsT = at("probsT", split_at + 12288, [P, 2, 2, P])
        rope_tmp = at("rope_tmp", split_at + 45056, [P, 2, 16, 2, 16])
        oT = at("oT", split_at + 24576, [P, NH, 2, P])
        o_sq = at("o_sq", split_at + 14336, [P, 2, P])
        u_pad = at("u_pad", split_at, [P, DC, 2, T + 2 * PAD])
        conv = at("conv", split_at + 10112, [P, DC, 2, T])
        conv_sq = at("conv_sq", split_at + 18304, [P, DC, 2, T])
        conv_act = at("conv_act", split_at + 26496, [P, DC, 2, 2, HT])
        diag = at("diag", split_at + 18304, [P, KW, P])
        mean = at("mean", split_at + 34688, [P, 2 * T])
        rstd_c = at("rstd_c", split_at + 35712, [P, 2 * T])
        sig = at("sig", split_at + 36736, [P, 2, 2 * T])
        wdw_rows = at("wdw_rows", split_at + 38784, [KW, D])
        over_w = at("over_w", split_at, [P, 6, 4, 512])
        over_p = at("over_p", moe_at, [P, 2, SLOTS])
        over_pT = at("over_pT", moe_at + 512, [SLOTS, 2, P])
        over_x = at("over_x", hT_at, [P, DC, SLOTS])
        over_aT = at("over_aT", hT_at + 2048, [P, FC, SLOTS])
        over_y = at("over_y", mod_at, [SLOTS, D])
        over_t = at("over_t", mod_at + 4096, [P, 2, D])
        over_g = at("over_g", mod_at + 12288, [P, 2, FE])
        cst = sb("cst", [P, C_ALL])
        rows = sb("rows", [R_ALL, 512])
        router = sb("router", [P, DC, NE])
        bias_b = sb("bias_b", [P, NE])
        chan_rows = sb("chan_rows", [V_ALL, P])
        chan = sb("chan", [P, V_ALL])
        wdw = sb("wdw", [P, DC, KW])
        cond = sb("cond", [P, 2, DC])
        silu_c = sb("silu_c", [P, 2, DC])
        lam_in = at("lam_in", mod_at + 20480, [P, 4, HD])
        lam = sb("lam", [P, 8])
        stat = sb("stat", [P, 72])
        asg = sb("asg", [P, 2, NE])
        rs = at("rs", mod_at, [P, 12, 2 * NE])
        pos = sb("pos", [P, 2, NE])
        gates = sb("gates", [P, 2, NE])
        gate_tok = sb("gate_tok", [P, 2, 2])
        gate_slot = sb("gate_slot", [P, 1])
        flag = sb("flag", [P, 2], I32)
        assert place[0] <= nc.sbuf_usable_end, place[0]

        ident = cst[:, C_ID:C_ID + P]
        ones = cst[:, C_ONE:C_ONE + P]
        bank = [ctx.enter_context(nc.psum_tensor(f"bank{i}", [P, 512], F32)) for i in range(8)]
        ACC, G, U, DN, X = bank[0:4], bank[4], bank[5], bank[6], bank[7]

        def sem(name):
            return ctx.enter_context(nc.semaphore(name))

        landed = [sem(f"landed{i}") for i in range(RING)]
        pe_used = sem("pe_used")
        hi_done, lo_done = sem("hi_done"), sem("lo_done")
        in_cond = sem("in_cond")
        in_first, in_x, in_vec = sem("in_first"), sem("in_x"), sem("in_vec")
        in_cache_k, in_cache_v, in_wdw = sem("in_cache_k"), sem("in_cache_v"), sem("in_wdw")
        out_kv, out_y = sem("out_kv"), sem("out_y")
        dve_chain = sem("dve_chain")
        cond_silu, condT_ready = sem("cond_silu"), sem("condT_ready")
        ada_mm, part_evac, ada_evac = sem("ada_mm"), sem("part_evac"), sem("ada_evac")
        ada_gmm, ada_gcopy = sem("ada_gmm"), sem("ada_gcopy")
        ada2_evac, scale2_done = sem("ada2_evac"), sem("scale2_done")
        condM_ready, g2_copied = sem("condM_ready"), sem("g2_copied")
        chan_mm, chan_ready = sem("chan_mm"), sem("chan_ready")
        lam_sums, lam_exp = sem("lam_sums"), sem("lam_exp")
        ssq, ms_ready, rms_ready, h_ready = sem("ssq"), sem("ms_ready"), sem("rms_ready"), sem("h_ready")
        hT_low = sem("hT_low")
        hT_mm, hT_act, hT_dve = sem("hT_mm"), sem("hT_act"), sem("hT_dve")
        x_mix, x_add, x_moe = sem("x_mix"), sem("x_add"), sem("x_moe")
        qkv_c, qkv_l, roped = sem("qkv_c"), sem("qkv_l"), sem("roped")
        qk_mm, qkT_act, qkT_dve = sem("qk_mm"), sem("qkT_act"), sem("qkT_dve")
        scores_mm, max_done, exp_done = sem("scores_mm"), sem("max_done"), sem("exp_done")
        combined, pT_mm, pT_evac = sem("combined"), sem("pT_mm"), sem("pT_evac")
        pv_mm, o_evac, o_normed, oT_mm, oT_evac = (sem("pv_mm"), sem("o_evac"), sem("o_normed"),
                                                   sem("oT_mm"), sem("oT_evac"))
        sub_ms, sub_rms = sem("sub_ms"), sem("sub_rms")
        wdw_mm, wdw_ready, sig_done, u_done = sem("wdw_mm"), sem("wdw_ready"), sem("sig_done"), sem("u_done")
        pads_zero, conv_dve = sem("pads_zero"), sem("conv_dve")
        diag_done, conv_mm = sem("diag_done"), sem("conv_mm")
        sum_mm, centred, squared, var_mm = sem("sum_mm"), sem("centred"), sem("squared"), sem("var_mm")
        var_ready, std_ready, scaled, conv_silu = (sem("var_ready"), sem("std_ready"), sem("scaled"),
                                                   sem("conv_silu"))
        logits_mm, scores_ready, assigned, pos_mm, routed = (
            sem("logits_mm"), sem("scores_ready"), sem("assigned"), sem("pos_mm"), sem("routed"))
        p2_built, gathered, xs_hi, xs_lo = sem("p2_built"), sem("gathered"), sem("xs_hi"), sem("xs_lo")
        g_low, g_folded = sem("g_low"), sem("g_folded")
        u_low, u_folded, silu_done = sem("u_low"), sem("u_folded"), sem("silu_done")
        sel_mm, sel_evac, act_done, actT_mm = sem("sel_mm"), sem("sel_evac"), sem("act_done"), sem("actT_mm")
        as_hi, as_lo = sem("as_hi"), sem("as_lo")
        yh_done, yl_done, scat = sem("yh_done"), sem("yl_done"), sem("scat")
        over = [{n: sem(f"over{k}_{n}") for n in ("w", "pe", "act", "dve")} for k in range(2)]
        fin_mm = sem("fin_mm")

        block = ctx.enter_context(nc.Block())

        def wait_block(eng, n, i=None):
            v = 16 * (n // RING + 1)
            eng.wait_ge(landed[n % RING], v if i is None else i * 16 + v)

        def high(sc, n, i=None):
            wait_block(sc, n, i)
            before = [b for b in SPLIT if b < n and HI_SLOT[b] == HI_SLOT[n]]
            if before:
                sc.wait_ge(pe_used, lin(i, RING, before[-1] + 1))
            sc.activation(w_hi[:, HI_SLOT[n], :, :], ring[:, n % RING, :, :], ACT.Copy).then_inc(hi_done, 1)

        def low(ve, n, i=None):
            k = split_index(n)
            ve.wait_ge(hi_done, lin(i, SPLITS, k + 1))
            ve.tensor_tensor(w_lo[n % RING][:, :, :], ring[:, n % RING, :, :], w_hi[:, HI_SLOT[n], :, :],
                             ALU.subtract).then_inc(lo_done, 1)

        def lin(i, per_i, const):
            return const if i is None else i * per_i + const

        def ada_block(layer, n):
            src = a["ada_w"][layer].rearrange("(p c) n -> p c n", c=DC)
            g, hf = n // 2, n % 2
            return src[:, 4 * hf:4 * hf + 4, g * 512:(g + 1) * 512]

        def qkv_block(n):
            src = a["attn_w_qkv"][0].rearrange("(p c) n -> p c n", c=DC)
            g, hf = n // 2, n % 2
            return src[:, 4 * hf:4 * hf + 4, g * 512:(g + 1) * 512]

        def wo_block(n):
            src = a["attn_w_o"][0].rearrange("(c p) n -> p c n", p=P)
            g, hf = n // 2, n % 2
            return src[:, 4 * hf:4 * hf + 4, g * 512:(g + 1) * 512]

        PW1_ORDER = [0, 2, 1, 3]

        def pw1_block(n):
            src = a["conv_w_pw1"][0].rearrange("(p c) n -> p c n", c=DC)
            g, hf = PW1_ORDER[n // 2], n % 2
            return src[:, 4 * hf:4 * hf + 4, g * 512:(g + 1) * 512]

        def pw2_block(n):
            src = a["conv_w_pw2"][0].rearrange("(c p) n -> p c n", p=P)
            g, hf = n // 2, n % 2
            return src[:, 4 * hf:4 * hf + 4, g * 512:(g + 1) * 512]

        def expert_block(layer, e, what):
            half = int(what[1])
            if what[0] == "D":
                src = a["moe_w_down"][layer, e].rearrange("(p c) n -> p c n", c=FC)
                return src[:, :, 512 * half:512 * half + 512]
            src = a["moe_w_gate" if what[0] == "G" else "moe_w_up"][layer, e].rearrange("(p c) f -> p c f", c=DC)
            return src[:, 4 * half:4 * half + 4, :]

        def mixed(dram, t, g):
            return dram[t * HT:(t + 1) * HT, :]

        xp, xl = a["x_prompt"][0], a["x_sample"][0]

        def transposed(tens, q, t):
            return tens[:, 4 * q:4 * q + 4, :, t * HT:(t + 1) * HT]

        def evac_transposed(copy, ni, t, q):
            src = bank[2 * t + q][:, :]
            if ni % 2:
                return copy(hTm[:, 4 * q:4 * q + 4, t, :], src.rearrange("p (c i) -> p c i", c=4))
            return copy(transposed(hT if ni else hT_hi, q, t), src.rearrange("p (c g i) -> p c g i", c=4, g=2))

        def ada2_bank(layer, n):
            return bank[ADA2_BANKS[layer][n % len(ADA2_BANKS[layer])]]

        def qk_target(m):
            what, g, q = QK_ITEMS[m]
            return (ckT[:, 4 * q:4 * q + 4, :] if what == 2
                    else (qT, kT)[what][:, 4 * q:4 * q + 4, g, :])

        COND = [
            (cond[:, 0, :], a["c_ctx"].rearrange("(p c) -> p c", c=DC)),
            (cond[:, 1, :], a["c"][0].rearrange("(p c) -> p c", c=DC)),
        ]
        FIRST = [
            (cst[:, :], a["consts"]),
            (rows[0:24, :], a["ada_b"].rearrange("l (r n) -> (l r) n", n=512)),
            (rows[24:28, :], a["norm1_g"].rearrange("l (r n) -> (l r) n", n=512)),
            (rows[28:32, :], a["norm2_g"].rearrange("l (r n) -> (l r) n", n=512)),
            (rows[32:34, :], a["final_norm_g"].rearrange("(r n) -> r n", n=512)),
            (rows[34:36, :], a["conv_b_pw2"][0].rearrange("(r n) -> r n", n=512)),
        ]
        SMALL = [
            (chan_rows[0:16, :], a["conv_b_pw1"][0].rearrange("(r n) -> r n", n=P)),
            (chan_rows[16:24, :], a["conv_b_dw"][0].rearrange("(r n) -> r n", n=P)),
            (chan_rows[24:32, :], a["conv_ln_g"][0].rearrange("(r n) -> r n", n=P)),
            (chan_rows[32:40, :], a["conv_ln_b"][0].rearrange("(r n) -> r n", n=P)),
            (chan_rows[40:41, :], a["attn_subln_g"]),
            (router[:, :, :], a["router_w"].rearrange("(p c) e -> p c e", c=DC)),
            (bias_b[:, :], a["router_bias"].partition_broadcast(P)),
            (lam_in[:, 0, :], a["attn_lambda_q1"][0].partition_broadcast(P)),
            (lam_in[:, 1, :], a["attn_lambda_k1"][0].partition_broadcast(P)),
            (lam_in[:, 2, :], a["attn_lambda_q2"][0].partition_broadcast(P)),
            (lam_in[:, 3, :], a["attn_lambda_k2"][0].partition_broadcast(P)),
        ]
        X_ROWS = [(x[HT * g:HT * g + HT, t, :], mixed((xp, xl)[g], t, g)) for t in range(2) for g in range(2)]
        IN_FIRST, IN_VEC = 16 * len(FIRST), 16 * len(SMALL)

        @block.sync
        def _(sp):
            def load(n, src, i=None):
                sp.dma_start(ring[:, n % RING, :, :], src).then_inc(landed[n % RING], 16)

            def free(n, i=None):
                if n >= 0:
                    sp.wait_ge(pe_used, lin(i, RING, n + 1))

            def moe_stream(layer):
                def expert_step(e0, i=None):
                    e = lin(i, 2, e0)
                    for what in ("G0", "G1", "D0", "D1", "U0", "U1"):
                        if (what[0] == "D" and e0 == 0) or (what[0] != "D" and e0 == NE):
                            continue
                        n = BASE_MOE[layer] + expert_place(e0, what)
                        free(n - RING, i)
                        load(n, expert_block(layer, e - 1 if what[0] == "D" else e, what))

                expert_step(0)
                expert_step(1)
                with sp.Fori(0, 6) as i:
                    expert_step(2, i)
                    expert_step(3, i)
                for e0 in range(14, NE + 1):
                    expert_step(e0)

            def overflow(layer):
                sp.wait_ge(routed, 3 * layer + 3)
                n_over = sp.value_load(flag[0:1, 0:1], min_val=0, max_val=1)
                with sp.If(n_over > 0):
                    o = over[layer]
                    for r in range(OVER):
                        with sp.Fori(0, NE) as e:
                            sp.wait_ge(o["dve"], e * OV_DVE + (r * NE * OV_DVE + 1))
                            for j, what in enumerate(("G0", "G1", "U0", "U1", "D0", "D1")):
                                sp.dma_start(over_w[:, j, :, :], expert_block(layer, e, what)).then_inc(o["w"], 16)

            for dst, src in COND:
                sp.dma_start(dst, src).then_inc(in_cond, 16)
            for layer, proj, n_proj, out, n_out in ((0, qkv_block, QKV_BLOCKS, wo_block, WO_BLOCKS),
                                                    (1, pw1_block, PW1_BLOCKS, pw2_block, PW2_BLOCKS)):
                for n in range(ADA_BLOCKS):
                    free(BASE_ADA1[layer] + n - RING)
                    load(BASE_ADA1[layer] + n, ada_block(layer, n))
                    if layer == 0 and n == 1:
                        for dst, src in FIRST:
                            sp.dma_start(dst, src).then_inc(in_first, 16)
                for n in range(n_proj):
                    free(BASE_PROJ[layer] + n - RING)
                    load(BASE_PROJ[layer] + n, proj(n))
                for n in range(ADA_BLOCKS):
                    free(BASE_ADA2[layer] + n - RING)
                    load(BASE_ADA2[layer] + n, ada_block(layer, ADA_BLOCKS + n))
                for n in range(n_out):
                    free(BASE_OUT[layer] + n - RING)
                    load(BASE_OUT[layer] + n, out(n))
                moe_stream(layer)
                overflow(layer)
            sp.wait_ge(h_ready, 10)
            for t in range(2):
                sp.dma_start(mixed(y_prompt[0], t, 0), h[0:HT, t, :]).then_inc(out_y, 16)
                sp.dma_start(mixed(y_sample[0], t, 1), h[HT:P, t, :]).then_inc(out_y, 16)
            sp.wait_ge(out_y, 64)
            sp.wait_ge(out_kv, 32)

        @block.tensor
        def _(pe):
            def row_bcast(out, r, stop):
                return pe.matmul(out, ident[0:R_ALL, r:r + 1].broadcast_to([R_ALL, P]), rows[:, :],
                                 start=True, stop=stop)

            def adaln(layer):
                pe.wait_ge(condT_ready, 4 * layer + 4)
                if layer:
                    pe.wait_ge(x_moe, layer)

                def products(n):
                    if n >= 2:
                        pe.wait_ge(part_evac, 6 * layer + n - 1)
                    for hf in range(2):
                        b = BASE_ADA1[layer] + 2 * n + hf
                        pe.wait_ge(lo_done, split_index(b) + 1)
                        for k in range(4):
                            for part, w in enumerate((w_hi[:, HI_SLOT[b]], w_lo[b % RING][:, :, :])):
                                mm = pe.matmul(bank[n % 2][:, :], condT[:, 4 * hf + k, :, :], w[:, k, :],
                                               start=(hf == 0 and k == 0 and part == 0),
                                               stop=(hf == 1 and k == 3 and part == 1))
                        mm.then_inc(pe_used, 1)

                def fold(n):
                    pe.wait_ge(part_evac, 6 * layer + n + 1)
                    if n >= 4:
                        pe.wait_ge(ada_evac, 6 * layer + n - 3)
                    if n == 0 and layer == 0:
                        pe.wait_ge(in_first, IN_FIRST)
                    row_bcast(bank[2 + n % 4][:, :], R_ADA[layer] + n, False)
                    pe.matmul(bank[2 + n % 4][:, :], cst[:, C_FOLD:C_FOLD + P], ada_part[:, n % 2, :],
                              start=False, stop=True).then_inc(ada_mm, 1)
                    if n in (2, 3):
                        row_bcast(bank[4 + n][:, :], R_G1[layer] + n - 2, True).then_inc(ada_gmm, 1)

                for n in range(7):
                    if n < 6:
                        products(n)
                    if n:
                        fold(n - 1)

            def ada2_chunk(layer, c):
                n, k = c // DC, c % DC
                b = BASE_ADA2[layer] + c // 4
                out = ada2_bank(layer, n)[:, :]
                if k == 0:
                    if n == 0:
                        pe.wait_ge(condM_ready, layer + 1)
                    if n >= len(ADA2_BANKS[layer]):
                        pe.wait_ge(ada2_evac, 6 * layer + n - len(ADA2_BANKS[layer]) + 1)
                    row_bcast(out, R_ADA[layer] + 6 + n, False)
                if k % 4 == 0:
                    wait_block(pe, b)
                mm = pe.matmul(out, condM[:, k, :, :], ring[:, b % RING, k % 4, :],
                               start=False, stop=(k == DC - 1))
                if k % 4 == 3:
                    mm.then_inc(pe_used, 1)

            def ada2_weights(layer):
                pe.wait_ge(ada2_evac, 6 * layer + 6)
                for q in range(2):
                    row_bcast(bank[2 + q][:, :], R_G2[layer] + q, True).then_inc(ada_gmm, 1)

            def transpose_h(ni):
                for t in range(2):
                    pe.wait_ge(h_ready, 2 * ni + t + 1)
                    for q in range(2):
                        for k in range(4):
                            c = 4 * q + k
                            mm = pe.transpose(bank[2 * t + q][:, k * P:(k + 1) * P],
                                              h[:, t, c::DC], ident)
                        mm.then_inc(hT_mm, 1)
                pe.wait_ge(hT_act, 2 * ni + 2)
                pe.wait_ge(hT_dve, 2 * ni + 2)

            def qkv_proj():
                for n in range(6):
                    if n == 1:
                        pe.wait_ge(chan_ready, 2)
                    if n >= 2:
                        pe.wait_ge(qkv_c, n - 1)
                        pe.wait_ge(qkv_l, n - 1)
                    for hf in range(2):
                        b = BASE_PROJ[0] + 2 * n + hf
                        pe.wait_ge(lo_done, split_index(b) + 1)
                        if n == 0:
                            pe.wait_ge(hT_low, 2 * hf + 2)
                        w_h, w_l = w_hi[:, HI_SLOT[b]], w_lo[b % RING][:, :, :]
                        for k in range(4):
                            for g in range(2):
                                c = 4 * hf + k
                                for part, (lhs, w) in enumerate(((hT_hi, w_h), (hT_lo, w_h), (hT_hi, w_l))):
                                    mm = pe.matmul(bank[4 + 2 * (n % 2) + g][:, :], lhs[:, c, g, :], w[:, k, :],
                                                   start=(c == 0 and part == 0), stop=(c == DC - 1 and part == 2))
                        mm.then_inc(pe_used, 1)

            def qk_transposes():
                pe.wait_ge(qkv_c, 6)
                pe.wait_ge(in_cache_k, 16)
                for m, (what, g, q) in enumerate(QK_ITEMS):
                    if g == 1:
                        pe.wait_ge(roped, 2)
                    if m >= 4:
                        pe.wait_ge(qkT_act if m % 2 == 0 else qkT_dve, (m - 4) // 2 + 1)
                    for k in range(4):
                        hd = 4 * q + k
                        src = (cache_k_sb[:, hd * P:(hd + 1) * P] if what == 2
                               else qkv[:, g, what * D + hd * P:what * D + (hd + 1) * P])
                        mm = pe.transpose(bank[m % 4][:, k * P:(k + 1) * P], src, ident)
                    mm.then_inc(qk_mm, 1)
                pe.wait_ge(qkT_act, len(QK_ITEMS) // 2)
                pe.wait_ge(qkT_dve, len(QK_ITEMS) // 2)
                pe.wait_ge(qkv_l, 6)
                pe.wait_ge(in_cache_v, 16)

            def scores(un):
                hd, g = un // 2, un % 2
                if un >= 2:
                    pe.wait_ge(exp_done, 2 * (un - 1))
                for m in range(2):
                    out = bank[4 + 2 * (un % 2) + m]
                    q = qT[HD * m:HD * m + HD, hd, g, :]
                    if g == 1:
                        pe.matmul(out[:, 0:P], q, ckT[HD * m:HD * m + HD, hd, :], start=True, stop=True)
                    mm = pe.matmul(out[:, g * P:(g + 1) * P], q, kT[HD * m:HD * m + HD, hd, g, :],
                                   start=True, stop=True)
                mm.then_inc(scores_mm, 1)

            def probs_transpose(un):
                g = un % 2
                pe.wait_ge(combined, un + 1)
                if un >= 2:
                    pe.wait_ge(pT_evac, un - 1)
                for kc in range(g + 1):
                    mm = pe.transpose(bank[un % 2][:, kc * P:(kc + 1) * P],
                                      probs[:, un % 2, kc * P:(kc + 1) * P], ident)
                mm.then_inc(pT_mm, 1)

            def pv(un):
                hd, g = un // 2, un % 2
                pe.wait_ge(pT_evac, un + 1)
                if un:
                    pe.wait_ge(o_evac, un)
                for kc in range(g + 1):
                    val = (cache_v_sb[:, hd * P:(hd + 1) * P] if kc < g
                           else qkv[:, g, 2 * D + hd * P:2 * D + (hd + 1) * P])
                    mm = pe.matmul(bank[2][:, 0:P], probsT[:, un % 2, kc, :], val,
                                   start=(kc == 0), stop=(kc == g))
                mm.then_inc(pv_mm, 1)

            def attention():
                qkv_proj()
                qk_transposes()
                for un in range(2 * NH + 2):
                    if un < 2 * NH:
                        scores(un)
                    for k in range(3 * (un % 3), min(3 * (un % 3) + 3, DC)):
                        ada2_chunk(0, DC * (un // 3) + k)
                    if 1 <= un <= 2 * NH:
                        probs_transpose(un - 1)
                    if un >= 2:
                        pv(un - 2)
                pe.wait_ge(o_evac, 2 * NH)
                ada2_weights(0)
                pe.wait_ge(pT_evac, 2 * NH)
                for g in range(2):
                    pe.wait_ge(o_normed, g + 1)
                    if g:
                        pe.wait_ge(g2_copied, 2)
                    for q in range(2):
                        for k in range(4):
                            hd = 4 * q + k
                            mm = pe.transpose(bank[2 * g + q][:, k * P:(k + 1) * P],
                                              h[:, g, hd * P:(hd + 1) * P], ident)
                        mm.then_inc(oT_mm, 1)
                pe.wait_ge(oT_evac, 4)
                for n in range(2):
                    for hf in range(2):
                        b = BASE_OUT[0] + 2 * n + hf
                        wait_block(pe, b)
                        for k in range(4):
                            for t in range(2):
                                c = 4 * hf + k
                                mm = pe.matmul(bank[4 + 2 * n + t][:, :], oT[:, c, t, :],
                                               ring[:, b % RING, k, :], start=(c == 0), stop=(c == DC - 1))
                        mm.then_inc(pe_used, 1)

            def convolution():
                pe.wait_ge(in_wdw, 16)
                for c in range(DC):
                    mm = pe.transpose(X[:, c * KW:(c + 1) * KW], wdw_rows[:, c * P:(c + 1) * P],
                                      ident[0:KW, 0:KW])
                mm.then_inc(wdw_mm, 1)
                b0 = BASE_PROJ[1]
                for n in range(4):
                    b = b0 + 2 * n
                    wait_block(pe, b)
                    wait_block(pe, b + 1)
                    if n == 3:
                        pe.wait_ge(wdw_ready, 1)
                    for k in range(4):
                        for c in range(DC):
                            mm = pe.matmul(bank[2 * n + k // 2][:, (k % 2) * 256:(k % 2) * 256 + 256],
                                           ring[:, (b + c // 4) % RING, c % 4, k * P:(k + 1) * P],
                                           hT[:, c, :, :], start=(c == 0), stop=(c == DC - 1))
                            if k == 3 and c % 4 == 3:
                                mm.then_inc(pe_used, 1)
                pe.wait_ge(sig_done, 4)
                for c in range(6 * DC):
                    ada2_chunk(1, c)
                ada2_weights(1)
                pe.wait_ge(u_done, DC)
                for k in range(KW):
                    pe.wait_ge(diag_done, k + 1)
                    mm = pe.matmul(bank[0][:, 0:256], diag[:, k, :], u_pad[:, DC - 1, :, k:k + T],
                                   start=(k == 0), stop=(k == KW - 1))
                mm.then_inc(conv_mm, 1)
                pe.wait_ge(conv_dve, 4 * KW)
                for c in range(DC):
                    if c == 4:
                        pe.wait_ge(conv_dve, CONV_DVE * KW + 1)
                    mm = pe.matmul(bank[5][:, 0:256], ones, conv[:, c, :, :], start=(c == 0), stop=(c == DC - 1))
                mm.then_inc(sum_mm, 1)
                for c in range(DC):
                    if c % 4 == 0:
                        pe.wait_ge(squared, c // 4 + 1)
                    mm = pe.matmul(bank[1][:, 0:256], ones, conv_sq[:, c, :, :], start=(c == 0),
                                   stop=(c == DC - 1))
                mm.then_inc(var_mm, 1)
                for n in range(2):
                    for t in range(2):
                        row_bcast(bank[4 + 2 * n + t][:, :], R_PW2 + n, False)
                    for hf in range(2):
                        pe.wait_ge(conv_silu, 4 * hf + 4)
                        b = BASE_OUT[1] + 2 * n + hf
                        wait_block(pe, b)
                        for k in range(4):
                            for t in range(2):
                                c = 4 * hf + k
                                mm = pe.matmul(bank[4 + 2 * n + t][:, :], conv_act[:, c, t, :, :],
                                               ring[:, b % RING, k, :], start=False, stop=(c == DC - 1))
                        mm.then_inc(pe_used, 1)

            def routing(layer):
                pe.wait_ge(x_mix, 4 * layer + 4)
                for t in range(2):
                    for c in range(DC):
                        mm = pe.matmul(G[:, t * NE:(t + 1) * NE], hTm[:, c, t, :], router[:, c, :],
                                       start=(c == 0), stop=(c == DC - 1))
                mm.then_inc(logits_mm, 1)
                pe.wait_ge(assigned, layer + 1)
                tri = cst[:, C_TRI:C_TRI + P]
                pe.matmul(U[:, 0:NE], tri, asg[:, 0, :], start=True, stop=True)
                pe.matmul(U[:, NE:2 * NE], ones, asg[:, 0, :], start=True, stop=False)
                pe.matmul(U[:, NE:2 * NE], tri, asg[:, 1, :], start=False, stop=True)
                pe.matmul(U[:, 2 * NE:3 * NE], ones, asg[:, 0, :], start=True, stop=False)
                pe.matmul(U[:, 2 * NE:3 * NE], ones, asg[:, 1, :], start=False, stop=True).then_inc(pos_mm, 1)

            def experts(layer):
                eo, b0 = NE * layer, BASE_MOE[layer]

                def gather(e0, i=None):
                    par = e0 % 2
                    pe.wait_ge(p2_built, lin(i, 6, 3 * (eo + e0 + 1)))
                    for c in range(DC):
                        for t in range(2):
                            mm = pe.matmul(X[:, c * SLOTS:(c + 1) * SLOTS], h[:, t, c::DC],
                                           p2[:, par, t, 0:SLOTS], start=(t == 0), stop=(t == 1))
                    mm.then_inc(gathered, 1)

                def split_product(out, lhs, k0, i, chunks, first, last):
                    n = b0 + k0
                    if n in NOT_SPLIT:
                        wait_block(pe, n, i)
                        for c in range(4):
                            mm = pe.matmul(out, lhs(chunks + c).bitcast(F32), ring[:, n % RING, c, :],
                                           start=(first and c == 0), stop=(last and c == 3))
                        mm.then_inc(pe_used, 1)
                        return
                    k = split_index(n)
                    pe.wait_ge(lo_done, lin(i, SPLITS, k + 1))
                    for c in range(4):
                        for part, w in enumerate((w_hi[:, HI_SLOT[n]], w_lo[n % RING][:, :, :])):
                            mm = pe.matmul(out, lhs(chunks + c), w[:, c, :],
                                           start=(first and c == 0 and part == 0),
                                           stop=(last and c == 3 and part == 1))
                            if c == 3 and part == 1:
                                mm.then_inc(pe_used, 1)

                def scatter(e0, i=None):
                    pe.wait_ge(sel_evac, lin(i, 4, 2 * (eo + e0) + 2))
                    for hf in range(2):
                        pe.wait_ge(yl_done, lin(i, 4, 2 * (eo + e0) + hf + 1))
                        for t in range(2):
                            for y in (yh, yl):
                                mm = pe.matmul(ACC[2 * t + hf][:, :], selT[:, e0 % 2, t, :], y[:, hf, :],
                                               start=(e0 == 0 and y is yh), stop=(e0 == NE - 1 and y is yl))
                        mm.then_inc(scat, 1)

                def down(e0, hf, i=None):
                    if hf == 0:
                        pe.wait_ge(as_lo, lin(i, 2, eo + e0))
                    if 2 * (eo + e0 - 1) + hf:
                        pe.wait_ge(yl_done, lin(i, 4, 2 * (eo + e0 - 1) + hf))
                    split_product(DN[:, :], lambda c: actT[:, c, :], expert_place(e0, f"D{hf}"), i, 0, True, True)

                def expert_step(e0, i=None):
                    par = e0 % 2
                    if e0 < NE:
                        pe.wait_ge(xs_lo, lin(i, 2, eo + e0 + 1))
                        if eo + e0:
                            pe.wait_ge(g_folded, lin(i, 2, eo + e0))
                        for q in range(2):
                            split_product(G[:, :], lambda c: xs[:, par, c, :], expert_place(e0, f"G{q}"), i,
                                          4 * q, q == 0, q == 1)
                    if e0:
                        pe.wait_ge(act_done, lin(i, 2, eo + e0))
                        pe.wait_ge(sel_evac, lin(i, 4, 2 * (eo + e0)))
                        for c in range(FC):
                            mm = pe.transpose(X[:, c * P:(c + 1) * P], act[:, c::FC], ident)
                        mm.then_inc(actT_mm, 1)
                    if e0 >= 2:
                        scatter(e0 - 2, i)
                    if e0:
                        down(e0, 0, i)
                    if e0 + 1 < NE:
                        if e0:
                            pe.wait_ge(as_lo, lin(i, 2, eo + e0))
                        gather(e0 + 1, i)
                    if e0:
                        down(e0, 1, i)
                    if e0 < NE:
                        if eo + e0:
                            pe.wait_ge(u_folded, lin(i, 2, eo + e0))
                        for q in range(2):
                            split_product(U[:, :], lambda c: xs[:, par, c, :], expert_place(e0, f"U{q}"), i,
                                          4 * q, q == 0, q == 1)
                            if q == 0:
                                if e0 + 1 < NE:
                                    pe.wait_ge(xs_lo, lin(i, 2, eo + e0 + 2))
                                else:
                                    pe.wait_ge(as_lo, lin(i, 2, eo + e0))
                                for t in range(2):
                                    pe.transpose(X[:, t * P:(t + 1) * P], p2[:, par, t, :], ident)
                                for t in range(2):
                                    mm = pe.matmul(X[:, 2 * P:2 * P + 1], p2[:, par, t, :],
                                                   gate_tok[:, par, t:t + 1], start=(t == 0), stop=(t == 1))
                                mm.then_inc(sel_mm, 1)

                gather(0)
                pe.wait_ge(routed, 3 * layer + 3)
                for e0 in range(4):
                    expert_step(e0)
                with pe.Fori(0, 5) as i:
                    expert_step(4, i)
                    expert_step(5, i)
                for e0 in range(14, NE + 1):
                    expert_step(e0)
                scatter(NE - 1)

            def overflow(layer):
                o = over[layer]
                n_over = pe.value_load(flag[0:1, 0:1], min_val=0, max_val=1)
                with pe.If(n_over > 0):
                    for r in range(OVER):
                        with pe.Fori(0, NE) as e:
                            def dve_at(s):
                                pe.wait_ge(o["dve"], e * OV_DVE + (r * NE * OV_DVE + 1 + s))

                            dve_at(3)
                            for c in range(DC):
                                for t in range(2):
                                    pe.matmul(bank[0][:, c * SLOTS:(c + 1) * SLOTS], h[:, t, c::DC],
                                              over_p[:, t, :], start=(t == 0), stop=(t == 1))
                            for t in range(2):
                                pe.transpose(bank[1][0:SLOTS, t * P:(t + 1) * P], over_p[:, t, :], ident)
                            for t in range(2):
                                mm = pe.matmul(bank[2][0:SLOTS, 0:1], over_p[:, t, :], gate_tok[:, 0, t:t + 1],
                                               start=(t == 0), stop=(t == 1))
                            mm.then_inc(o["pe"], 1)
                            dve_at(6)
                            pe.wait_ge(o["w"], e * 96 + (r * NE * 96 + 96))
                            for q, out in enumerate((G, U)):
                                for c in range(DC):
                                    mm = pe.matmul(out[0:SLOTS, :], over_x[:, c, :],
                                                   over_w[:, 2 * q + c // 4, c % 4, :],
                                                   start=(c == 0), stop=(c == DC - 1))
                            mm.then_inc(o["pe"], 1)
                            dve_at(7)
                            for c in range(FC):
                                mm = pe.transpose(bank[3][:, c * P:(c + 1) * P], over_g[:, 1, c::FC], ident)
                            mm.then_inc(o["pe"], 1)
                            dve_at(8)
                            for hf, out in enumerate((DN, X)):
                                for c in range(FC):
                                    mm = pe.matmul(out[0:SLOTS, :], over_aT[:, c, :], over_w[:, 4 + hf, c, :],
                                                   start=(c == 0), stop=(c == FC - 1))
                            mm.then_inc(o["pe"], 1)
                            dve_at(10)
                            for t in range(2):
                                for hf in range(2):
                                    mm = pe.matmul(ACC[2 * t + hf][:, :], over_pT[:, t, :],
                                                   over_y[:, hf * 512:(hf + 1) * 512], start=True, stop=True)
                            mm.then_inc(o["pe"], 1)

            for layer in range(2):
                adaln(layer)
                pe.wait_ge(ada_evac, 6 * layer + 6)
                pe.wait_ge(ada_gcopy, 2 * layer + 2)
                if layer == 0:
                    pe.wait_ge(in_vec, IN_VEC)
                    pe.transpose(X[:, 0:V_ALL], chan_rows[:, :], ident[0:V_ALL, 0:V_ALL]).then_inc(chan_mm, 1)
                transpose_h(2 * layer)
                if layer == 0:
                    attention()
                else:
                    convolution()
                pe.wait_ge(x_mix, 4 * layer + 4)
                transpose_h(2 * layer + 1)
                routing(layer)
                experts(layer)
                overflow(layer)
            pe.wait_ge(x_moe, 2)
            for q in range(2):
                mm = row_bcast(bank[4 + q][:, :], R_FIN + q, True)
            mm.then_inc(fin_mm, 1)

        @block.scalar
        def _(sc):
            def square_sums(ni):
                for n in range(2):
                    cols = slice(n * 512, (n + 1) * 512)
                    if ni in (1, 3):
                        sc.wait_ge(x_mix, 2 * (ni - 1) + 2 * n + 2)
                    elif ni == 4:
                        sc.wait_ge(x_moe, 2)
                    for t in range(2):
                        sc.activation(h[:, t, cols], x[:, t, cols], ACT.Square,
                                      accum_out=stat[:, 2 * n + t:2 * n + t + 1]).then_inc(ssq, 1)
                sc.wait_ge(ms_ready, ni + 1)
                sc.activation(stat[:, 4:6], stat[:, 48:50], ACT.Sqrt).then_inc(rms_ready, 1)

            def evac_hT(ni):
                for q in range(2):
                    sc.wait_ge(hT_mm, 4 * ni + q + 1)
                    evac_transposed(lambda o, i_: sc.activation(o, i_, ACT.Copy), ni, 0, q).then_inc(hT_act, 1)

            def adaln(layer):
                if layer:
                    sc.wait_ge(x_moe, layer)

                def part(n):
                    sc.wait_ge(pe_used, BASE_ADA1[layer] + 2 * n + 2)
                    if n >= 2:
                        sc.wait_ge(ada_mm, 6 * layer + n - 1)
                    sc.activation(ada_part[:, n % 2, :], bank[n % 2][:, :], ACT.Copy).then_inc(part_evac, 1)

                def weights(n):
                    if n in (2, 3):
                        sc.wait_ge(ada_gmm, 4 * layer + n - 1)
                        sc.activation(mod[:, 1, (n - 2) * 512:(n - 1) * 512], bank[4 + n][:, :],
                                      ACT.Copy).then_inc(ada_gcopy, 1)

                for n in range(8):
                    if n < 6:
                        high(sc, BASE_ADA1[layer] + 2 * n)
                        high(sc, BASE_ADA1[layer] + 2 * n + 1)
                    if 1 <= n < 7:
                        part(n - 1)
                    if n >= 2:
                        weights(n - 2)
                    if n == 4:
                        if layer == 0:
                            sc.wait_ge(in_x, 64)
                        square_sums(2 * layer)
                if layer == 0:
                    high(sc, BASE_PROJ[0])
                    high(sc, BASE_PROJ[0] + 1)

            def first_experts_high(layer, part):
                if layer == 0 and part == 0:
                    sc.wait_ge(out_kv, 32)
                for e, what in AHEAD_OF_ALL[part]:
                    high(sc, BASE_MOE[layer] + expert_place(e, what))

            def ada2_cond(layer):
                sc.wait_ge(pe_used, BASE_ADA2[layer])
                sc.activation(condM[:, :, :, :], silu_c[:, :, :].rearrange("p g c -> p c g").unsqueeze(3)
                              .broadcast_to([P, DC, 2, HT]), ACT.Copy).then_inc(condM_ready, 1)

            def g2_copy(layer):
                for q in range(2):
                    sc.wait_ge(ada_gmm, 4 * layer + 3 + q)
                    sc.activation(g2[:, q * 512:(q + 1) * 512], bank[2 + q][:, :], ACT.Copy).then_inc(g2_copied, 1)

            def ada2_copy(layer, n):
                sc.wait_ge(pe_used, BASE_ADA2[layer] + 2 * n + 2)
                sc.activation(mod[:, 3 + n // 2, (n % 2) * 512:(n % 2) * 512 + 512],
                              ada2_bank(layer, n)[:, :], ACT.Copy).then_inc(ada2_evac, 1)

            def attention():
                for n in range(7):
                    if 1 <= n < 6:
                        high(sc, BASE_PROJ[0] + 2 * n)
                        high(sc, BASE_PROJ[0] + 2 * n + 1)
                    if n == 0:
                        continue
                    n -= 1
                    sc.wait_ge(pe_used, BASE_PROJ[0] + 2 * n + 2)
                    sc.activation(qkv[:, 0, n * 512:(n + 1) * 512], bank[4 + 2 * (n % 2)][:, :],
                                  ACT.Copy).then_inc(qkv_c, 1)
                sc.wait_ge(qkv_c, 6)
                ada2_cond(0)
                sc.dma_start(new_k, qkv[:, 0, D:2 * D]).then_inc(out_kv, 16)
                sc.dma_start(new_v, qkv[:, 0, 2 * D:3 * D]).then_inc(out_kv, 16)
                for m in range(0, len(QK_ITEMS), 2):
                    sc.wait_ge(qk_mm, m + 1)
                    if m == 0:
                        sc.wait_ge(roped, 2)
                    sc.activation(qk_target(m), bank[m % 4][:, :], ACT.Copy).then_inc(qkT_act, 1)
                for un in range(2 * NH + 2):
                    if un and un % 3 == 0:
                        ada2_copy(0, un // 3 - 1)
                    if un < 2 * NH:
                        g = un % 2
                        w = (g + 1) * P
                        sc.wait_ge(max_done, un + 1)
                        if un >= 2:
                            sc.wait_ge(pT_mm, un - 1)
                        else:
                            sc.wait_ge(qk_mm, len(QK_ITEMS))
                        for m in range(2):
                            sc.activation(probs[:, un % 2, m * 256:m * 256 + w],
                                          bank[4 + 2 * (un % 2) + m][:, 0:w], ACT.Exp,
                                          bias=stat[:, 8 + 2 * (un % 2) + m:9 + 2 * (un % 2) + m],
                                          scale=HD ** -0.5,
                                          accum_out=stat[:, 12 + 2 * (un % 2) + m:13 + 2 * (un % 2) + m])\
                              .then_inc(exp_done, 1)
                    if 1 <= un <= 2 * NH:
                        v = un - 1
                        w = (v % 2 + 1) * P
                        sc.wait_ge(pT_mm, v + 1)
                        if v >= 2:
                            sc.wait_ge(pv_mm, v - 1)
                        sc.activation(probsT[:, v % 2, 0:v % 2 + 1, :], bank[v % 2][:, 0:w],
                                      ACT.Copy).then_inc(pT_evac, 1)
                    if un >= 2:
                        v = un - 2
                        sc.wait_ge(pv_mm, v + 1)
                        sc.activation(h[:, v % 2, (v // 2) * P:(v // 2 + 1) * P], bank[2][:, 0:P],
                                      ACT.Copy)
                        sc.activation(o_sq[:, v % 2, :], bank[2][:, 0:P], ACT.Square,
                                      accum_out=stat[:, 16 + NH * (v % 2) + v // 2:17 + NH * (v % 2) + v // 2])\
                          .then_inc(o_evac, 1)
                sc.wait_ge(sub_ms, 1)
                sc.activation(stat[:, 32:48], stat[:, 16:32], ACT.Sqrt).then_inc(sub_rms, 1)
                ada2_copy(0, 5)
                g2_copy(0)
                for m in range(4):
                    g, q = m // 2, m % 2
                    sc.wait_ge(oT_mm, m + 1)
                    sc.activation(oT[:, 4 * q:4 * q + 4, :, g * HT:(g + 1) * HT],
                                  bank[m][:, :].rearrange("p (c t i) -> p c t i", c=4, t=2),
                                  ACT.Copy, scale=chan[:, V_SUB:V_SUB + 1]).then_inc(oT_evac, 1)
                first_experts_high(0, 0)

            def convolution():
                for cc in range(DC):
                    q, k = cc // 4, cc % 4
                    sc.wait_ge(pe_used, BASE_PROJ[1] + 4 * q + 4)
                    if cc >= 2:
                        sc.wait_ge(u_done, cc - 1)
                    sc.activation(sig[:, cc % 2, :], bank[4 * q + 2 + k // 2][:, (k % 2) * 256:(k % 2) * 256 + 256],
                                  ACT.Sigmoid, bias=chan[:, V_BPW1 + DC + cc:V_BPW1 + DC + cc + 1])\
                      .then_inc(sig_done, 1)
                ada2_cond(1)
                for n in range(6):
                    ada2_copy(1, n)
                    if n < 5:
                        for k in range(KW * n // 5, KW * (n + 1) // 5):
                            sc.activation(diag[:, k, :], ident, ACT.Copy, scale=wdw[:, DC - 1, k:k + 1])\
                              .then_inc(diag_done, 1)
                g2_copy(1)
                for q in range(2):
                    sc.wait_ge(centred, q + 1)
                    if q == 0:
                        sc.wait_ge(conv_mm, 1)
                    sc.activation(conv_sq[:, 4 * q:4 * q + 4, :, :], conv[:, 4 * q:4 * q + 4, :, :],
                                  ACT.Square).then_inc(squared, 1)
                sc.wait_ge(var_ready, 1)
                sc.activation(rstd_c[:, :], mean[:, :], ACT.Sqrt).then_inc(std_ready, 1)
                for c in range(DC):
                    if c % 4 == 0:
                        sc.wait_ge(scaled, c // 4 + 1)
                    sc.activation(conv_act[:, c, :, :, :].rearrange("p t g i -> p g t i"),
                                  conv[:, c, :, :].rearrange("p g (t i) -> p g t i", t=2),
                                  ACT.Silu, bias=chan[:, V_LNB + c:V_LNB + c + 1],
                                  scale=chan[:, V_LNG + c:V_LNG + c + 1]).then_inc(conv_silu, 1)
                sc.wait_ge(conv_silu, DC)
                first_experts_high(1, 0)

            def experts(layer):
                eo, b0 = NE * layer, BASE_MOE[layer]

                def high_tokens(e0, i=None):
                    par = e0 % 2
                    sc.wait_ge(gathered, lin(i, 2, eo + e0 + 1))
                    if eo + e0 >= 2:
                        sc.wait_ge(pe_used, lin(i, RING, b0 + (expert_place(e0 - 2, "U1") + 1 if e0 >= 2 else 0)))
                    sc.activation(xs[:, par, :, 0:SLOTS], X[:, :].rearrange("p (c s) -> p c s", c=DC),
                                  ACT.Copy).then_inc(xs_hi, 1)

                def expert_step(e0, i=None):
                    ahead = blocks_ahead(e0)

                    def split():
                        n = next(ahead)
                        if n is not None:
                            high(sc, b0 + n, i)

                    if e0:
                        sc.wait_ge(pe_used, lin(i, RING, b0 + expert_place(e0 - 1, "U1") + 1))
                        if eo + e0 >= 2:
                            sc.wait_ge(u_folded, lin(i, 2, eo + e0 - 1))
                        sc.activation(u_lo[:, :], U[SLOTS:P, :], ACT.Copy).then_inc(u_low, 1)
                    split()
                    if e0:
                        sc.wait_ge(actT_mm, lin(i, 2, eo + e0))
                        if eo + e0 >= 2:
                            sc.wait_ge(pe_used, lin(i, RING, b0 + (expert_place(e0 - 1, "D1") + 1 if e0 >= 2 else 0)))
                        sc.activation(actT[:, :, 0:SLOTS], X[:, :].rearrange("p (c s) -> p c s", c=FC)[:, :, 0:SLOTS],
                                      ACT.Copy).then_inc(as_hi, 1)
                    if e0 < NE:
                        sc.wait_ge(pe_used, lin(i, RING, b0 + expert_place(e0, "G1") + 1))
                        if eo + e0:
                            sc.wait_ge(g_folded, lin(i, 2, eo + e0))
                        sc.activation(g_lo[:, :], G[SLOTS:P, :], ACT.Copy).then_inc(g_low, 1)
                    split()
                    if e0 < NE:
                        sc.wait_ge(g_folded, lin(i, 2, eo + e0 + 1))
                        if eo + e0:
                            sc.wait_ge(act_done, lin(i, 2, eo + e0))
                        sc.activation(g_silu[:, :], g_sum[:, :], ACT.Silu).then_inc(silu_done, 1)
                    split()
                    if e0:
                        high_result(e0, 0, i)
                    split()
                    if e0 + 1 < NE:
                        high_tokens(e0 + 1, i)
                    split()
                    if e0:
                        high_result(e0, 1, i)
                    if e0 < NE:
                        sc.wait_ge(sel_mm, lin(i, 2, eo + e0 + 1))
                        if eo + e0 >= 2:
                            sc.wait_ge(scat, lin(i, 4, 2 * (eo + e0 - 1)))
                        if eo + e0:
                            sc.wait_ge(act_done, lin(i, 2, eo + e0))
                        sc.activation(selT[:, e0 % 2, :, :], X[:, 0:2 * P], ACT.Copy).then_inc(sel_evac, 1)
                        sc.activation(gate_slot[:, :], X[:, 2 * P:2 * P + 1], ACT.Copy).then_inc(sel_evac, 1)
                    split()

                def high_result(e0, hf, i=None):
                    sc.wait_ge(pe_used, lin(i, RING, b0 + expert_place(e0, f"D{hf}") + 1))
                    if eo + e0 >= 2:
                        sc.wait_ge(scat, lin(i, 4, 2 * (eo + e0 - 2) + hf + 1))
                    sc.activation(yh[:, hf, :], DN[:, :], ACT.Copy).then_inc(yh_done, 1)

                high_tokens(0)
                expert_step(0)
                expert_step(1)
                with sc.Fori(0, 6) as i:
                    expert_step(2, i)
                    expert_step(3, i)
                for e0 in range(14, NE + 1):
                    expert_step(e0)

            def overflow(layer):
                o = over[layer]
                n_over = sc.value_load(flag[0:1, 0:1], min_val=0, max_val=1)
                with sc.If(n_over > 0):
                    for r in range(OVER):
                        with sc.Fori(0, NE) as e:
                            sc.wait_ge(o["pe"], e * OV_PE + (r * NE * OV_PE + 2))
                            sc.activation(over_g[0:SLOTS, 0, :], G[0:SLOTS, :], ACT.Silu).then_inc(o["act"], 1)

            sc.wait_ge(in_cond, 32)
            sc.activation(silu_c[:, :, :], cond[:, :, :], ACT.Silu).then_inc(cond_silu, 1)
            for layer in range(2):
                adaln(layer)
                if layer:
                    sc.wait_ge(pe_used, BASE_PROJ[1])
                    sc.dma_start(wdw_rows[:, :], a["conv_w_dw"][0]).then_inc(in_wdw, 16)
                evac_hT(2 * layer)
                if layer == 0:
                    sc.wait_ge(lam_sums, 2)
                    sc.activation(lam[:, 2:4], lam[:, 0:2], ACT.Exp).then_inc(lam_exp, 1)
                if layer == 0:
                    attention()
                else:
                    convolution()
                square_sums(2 * layer + 1)
                evac_hT(2 * layer + 1)
                sc.wait_ge(logits_mm, layer + 1)
                sc.activation(rs[:, 0, :], G[:, 0:2 * NE], ACT.Sigmoid).then_inc(scores_ready, 1)
                first_experts_high(layer, 1)
                sc.wait_ge(routed, 3 * layer + 3)
                experts(layer)
                overflow(layer)
            sc.wait_ge(x_moe, 2)
            square_sums(4)

        @block.gpsimd
        def _(pool):
            for loads, landed_sem in ((X_ROWS, in_x), (SMALL, in_vec)):
                for dst, src in loads:
                    pool.dma_start(dst, src).then_inc(landed_sem, 16)
            pool.dma_start(cache_k_sb[:, :], a["cache_k"][0, 0].rearrange("t h e -> t (h e)")).then_inc(in_cache_k, 16)
            pool.dma_start(cache_v_sb[:, :], a["cache_v"][0, 0].rearrange("t h e -> t (h e)")).then_inc(in_cache_v, 16)
            pool.wait_ge(pe_used, BASE_PROJ[1])
            for lo in (0, PAD + T):
                pool.memset(u_pad[:, :, :, lo:lo + PAD], 0.0).then_inc(pads_zero, 1)

        @block.vector
        def _(ve):
            chain = [0]

            def link(ins):
                chain[0] += 1
                ins.then_inc(dve_chain, 1)
                ve.wait_ge(dve_chain, chain[0])

            def adaln(layer):
                if layer:
                    ve.wait_ge(x_moe, layer)
                else:
                    ve.wait_ge(cond_silu, 1)
                for g in range(2):
                    c32 = silu_c[:, g, :].unsqueeze(2).broadcast_to([P, DC, 32])
                    ve.tensor_copy(condT[:, :, 2 * g, :], c32).then_inc(condT_ready, 1)
                    ve.wait_ge(condT_ready, 4 * layer + 2 * g + 1)
                    ve.tensor_tensor(condT[:, :, 2 * g + 1, :], c32, condT[:, :, 2 * g, :],
                                     ALU.subtract).then_inc(condT_ready, 1)

                def finish(n):
                    ve.wait_ge(ada_mm, 6 * layer + n + 1)
                    dst = mod[:, n // 2, (n % 2) * 512:(n % 2) * 512 + 512]
                    src = bank[2 + n % 4][:, :]
                    if n in (2, 3):
                        ve.wait_ge(ada_gcopy, 2 * layer + n - 1)
                        ins = ve.scalar_tensor_tensor(out=dst, in0=src, scalar=1.0, in1=dst,
                                                      op0=ALU.add, op1=ALU.mult)
                    else:
                        ins = ve.tensor_copy(dst, src)
                    ins.then_inc(ada_evac, 1)

                for n in range(8):
                    if n < 6:
                        low(ve, BASE_ADA1[layer] + 2 * n)
                        low(ve, BASE_ADA1[layer] + 2 * n + 1)
                    if n >= 2:
                        finish(n - 2)
                    if n == 4:
                        rms(2 * layer)
                    if n == 5:
                        norm_rows(2 * layer)
                if layer == 0:
                    low(ve, BASE_PROJ[0])

            def first_experts_low(layer, part):
                for e, what in AHEAD_OF_ALL[part]:
                    low(ve, BASE_MOE[layer] + expert_place(e, what))

            def ada2_scale(layer):
                ve.wait_ge(g2_copied, 2 * layer + 2)
                ve.wait_ge(ada2_evac, 6 * layer + 6)
                ve.scalar_tensor_tensor(out=mod[:, 4, :], in0=mod[:, 4, :], scalar=1.0, in1=g2[:, :],
                                        op0=ALU.add, op1=ALU.mult).then_inc(scale2_done, 1)

            def rms(ni):
                ve.wait_ge(ssq, 4 * ni + 4)
                link(ve.tensor_tensor(stat[:, 48:50], stat[:, 0:2], stat[:, 2:4], ALU.add))
                ve.tensor_scalar(stat[:, 48:50], stat[:, 48:50], 1.0 / D, EPS, ALU.mult, ALU.add)\
                  .then_inc(ms_ready, 1)
                ve.wait_ge(rms_ready, ni + 1)
                link(ve.reciprocal(stat[:, 6:8], stat[:, 4:6]))

            def norm_rows(ni):
                layer, w = ni // 2, ni % 2
                if w:
                    ve.wait_ge(scale2_done, layer + 1)
                else:
                    ve.wait_ge(ada_evac, 6 * layer + 4)
                for t in range(2):
                    link(ve.scalar_tensor_tensor(out=h[:, t, :], in0=x[:, t, :], scalar=stat[:, 6 + t:7 + t],
                                                 in1=mod[:, 3 * w + 1, :], op0=ALU.mult, op1=ALU.mult))
                    ve.tensor_tensor(h[:, t, :], h[:, t, :], mod[:, 3 * w, :], ALU.add).then_inc(h_ready, 1)

            def evac_hT(ni):
                for q in range(2):
                    ve.wait_ge(hT_mm, 4 * ni + 2 + q + 1)
                    evac_transposed(ve.tensor_copy, ni, 1, q).then_inc(hT_dve, 1)

            def add_gated(layer, gate):
                for n in range(2):
                    ve.wait_ge(pe_used, BASE_MOE[layer] - 2 + 2 * n)
                    for t in range(2):
                        cols = slice(n * 512, (n + 1) * 512)
                        link(ve.tensor_tensor(h[:, t, cols], bank[4 + 2 * n + t][:, :], mod[:, gate, cols], ALU.mult))
                        ve.tensor_tensor(x[:, t, cols], x[:, t, cols], h[:, t, cols], ALU.add).then_inc(x_mix, 1)
                ve.wait_ge(x_mix, 4 * layer + 4)

            def vectors():
                ve.wait_ge(in_vec, IN_VEC)
                for k in range(2):
                    link(ve.tensor_tensor(lam_in[:, 2 * k, :], lam_in[:, 2 * k, :], lam_in[:, 2 * k + 1, :], ALU.mult))
                    ve.reduce_sum(lam[:, k:k + 1], lam_in[:, 2 * k, :], AX).then_inc(lam_sums, 1)
                ve.wait_ge(lam_exp, 1)
                link(ve.scalar_tensor_tensor(out=lam[:, 4:5], in0=lam[:, 2:3], scalar=LAMBDA_INIT, in1=lam[:, 3:4],
                                             op0=ALU.add, op1=ALU.subtract))
                ve.wait_ge(chan_mm, 1)
                ve.tensor_copy(chan[:, 0:V_SUB], X[:, 0:V_SUB]).then_inc(chan_ready, 1)
                ve.tensor_scalar(chan[:, V_SUB:V_ALL], X[:, V_SUB:V_ALL], 1.0 - LAMBDA_INIT, None, ALU.mult)\
                  .then_inc(chan_ready, 1)

            def rotate(what):
                ve.wait_ge(qkv_l, 2 * what + 2)
                v = qkv[:, 1, what * D:(what + 1) * D].rearrange("p (n a two f) -> p n a two f", n=16, a=2, two=2)
                x1, x2 = v[:, :, :, 0, :], v[:, :, :, 1, :]
                cos, sin = (cst[:, c0:c0 + 32].rearrange("p (a f) -> p a f", a=2).unsqueeze(1)
                            .broadcast_to([P, 16, 2, 16]) for c0 in (C_COS, C_SIN))
                s1, s2 = rope_tmp[:, 0], rope_tmp[:, 1]
                if what:
                    ve.wait_ge(roped, 1)
                ve.tensor_tensor(s1, x1, sin, ALU.mult)
                link(ve.tensor_tensor(s2, x2, sin, ALU.mult))
                ve.tensor_tensor(x1, x1, cos, ALU.mult)
                link(ve.tensor_tensor(x2, x2, cos, ALU.mult))
                ve.tensor_tensor(x1, x1, s2, ALU.subtract)
                ve.tensor_tensor(x2, x2, s1, ALU.add).then_inc(roped, 1)

            def attention():
                for n in range(7):
                    if 1 <= n < 6:
                        low(ve, BASE_PROJ[0] + 2 * n)
                        low(ve, BASE_PROJ[0] + 2 * n + 1)
                    if n == 0:
                        for q in range(2):
                            for t in range(2):
                                ve.wait_ge(hT_mm, 4)
                                ve.wait_ge((hT_act, hT_dve)[t], q + 1)
                                ve.tensor_tensor(transposed(hT_lo, q, t),
                                                 bank[2 * t + q][:, :].rearrange("p (c g i) -> p c g i", c=4, g=2),
                                                 transposed(hT_hi, q, t), ALU.subtract).then_inc(hT_low, 1)
                        low(ve, BASE_PROJ[0] + 1)
                        vectors()
                        continue
                    n -= 1
                    ve.wait_ge(pe_used, BASE_PROJ[0] + 2 * n + 2)
                    ve.tensor_copy(qkv[:, 1, n * 512:(n + 1) * 512], bank[5 + 2 * (n % 2)][:, :]).then_inc(qkv_l, 1)
                    if n in (1, 3):
                        rotate(n // 2)
                for m in range(1, len(QK_ITEMS), 2):
                    ve.wait_ge(qk_mm, m + 1)
                    if m == 1:
                        ve.wait_ge(roped, 2)
                    ve.tensor_copy(qk_target(m), bank[m % 4][:, :].rearrange("p (c i) -> p c i", c=4))\
                      .then_inc(qkT_dve, 1)
                for un in range(2 * NH + 1):
                    if un < 2 * NH:
                        b = un % 2
                        w = (b + 1) * P
                        ve.wait_ge(scores_mm, un + 1)
                        for m in range(2):
                            ins = ve.reduce_max(stat[:, 48 + 2 * b + m:49 + 2 * b + m],
                                                bank[4 + 2 * b + m][:, 0:w], AX)
                        link(ins)
                        ve.tensor_scalar(stat[:, 8 + 2 * b:10 + 2 * b], stat[:, 48 + 2 * b:50 + 2 * b],
                                         -HD ** -0.5, None, ALU.mult).then_inc(max_done, 1)
                    if un:
                        v = un - 1
                        b = v % 2
                        w = (b + 1) * P
                        ve.wait_ge(exp_done, 2 * v + 2)
                        link(ve.reciprocal(stat[:, 52 + 2 * b:54 + 2 * b], stat[:, 12 + 2 * b:14 + 2 * b]))
                        link(ve.tensor_tensor(stat[:, 53 + 2 * b:54 + 2 * b], stat[:, 53 + 2 * b:54 + 2 * b],
                                              lam[:, 4:5], ALU.mult))
                        link(ve.tensor_scalar(probs[:, b, 256:256 + w], probs[:, b, 256:256 + w],
                                              stat[:, 53 + 2 * b:54 + 2 * b], None, ALU.mult))
                        ve.scalar_tensor_tensor(out=probs[:, b, 0:w], in0=probs[:, b, 0:w],
                                                scalar=stat[:, 52 + 2 * b:53 + 2 * b],
                                                in1=probs[:, b, 256:256 + w], op0=ALU.mult,
                                                op1=ALU.subtract).then_inc(combined, 1)
                ve.wait_ge(o_evac, 2 * NH)
                ve.tensor_scalar(stat[:, 16:32], stat[:, 16:32], 1.0 / P, EPS, ALU.mult, ALU.add).then_inc(sub_ms, 1)
                ve.wait_ge(sub_rms, 1)
                link(ve.reciprocal(stat[:, 56:72], stat[:, 32:48]))
                for g in range(2):
                    o = h[:, g, :].rearrange("p (n e) -> p n e", n=NH)
                    ve.tensor_tensor(o, o, stat[:, 56 + NH * g:56 + NH * (g + 1)].unsqueeze(2)
                                     .broadcast_to([P, NH, P]), ALU.mult).then_inc(o_normed, 1)
                ada2_scale(0)
                first_experts_low(0, 0)

            steps = [0]

            def depthwise(chunks, taps):
                for k in taps:
                    for c in chunks:
                        if k:
                            ve.wait_ge(conv_dve, steps[0] - len(chunks) + 1)
                        shifted = u_pad[:, c, :, k:k + T]
                        if k == 0:
                            ins = ve.tensor_scalar(conv[:, c, :, :], shifted, wdw[:, c, 0:1],
                                                   chan[:, V_BDW + c:V_BDW + c + 1], ALU.mult, ALU.add)
                        else:
                            ins = ve.scalar_tensor_tensor(out=conv[:, c, :, :], in0=shifted,
                                                          scalar=wdw[:, c, k:k + 1], in1=conv[:, c, :, :],
                                                          op0=ALU.mult, op1=ALU.add)
                        ins.then_inc(conv_dve, 1)
                        steps[0] += 1

            def convolution():
                ve.wait_ge(wdw_mm, 1)
                ve.tensor_copy(wdw[:, :, :], X[:, 0:DC * KW].rearrange("p (c k) -> p c k", c=DC))\
                  .then_inc(wdw_ready, 1)
                ve.wait_ge(pads_zero, 2)
                for cc in range(DC):
                    q, k = cc // 4, cc % 4
                    ve.wait_ge(sig_done, cc + 1)
                    ve.scalar_tensor_tensor(out=u_pad[:, cc, :, PAD:PAD + T],
                                            in0=bank[4 * q + k // 2][:, (k % 2) * 256:(k % 2) * 256 + 256]
                                            .rearrange("p (g i) -> p g i", g=2),
                                            scalar=chan[:, V_BPW1 + cc:V_BPW1 + cc + 1],
                                            in1=sig[:, cc % 2, :].rearrange("p (g i) -> p g i", g=2),
                                            op0=ALU.add, op1=ALU.mult).then_inc(u_done, 1)
                    if cc == 3:
                        ve.wait_ge(u_done, 4)
                        depthwise(range(4), range(TAPS_FIRST))
                depthwise(range(4), range(TAPS_FIRST, KW))
                ve.wait_ge(u_done, DC)
                depthwise(range(4, CONV_DVE), range(KW))
                ve.wait_ge(conv_mm, 1)
                ve.tensor_scalar(conv[:, DC - 1, :, :], bank[0][:, 0:256].rearrange("p (g i) -> p g i", g=2),
                                 chan[:, V_BDW + DC - 1:V_BDW + DC], None, ALU.add).then_inc(conv_dve, 1)
                ve.wait_ge(sum_mm, 1)
                link(ve.tensor_scalar(mean[:, :], bank[5][:, 0:256], 1.0 / D, None, ALU.mult))

                def each_chunk(row, op, done):
                    for q in range(2):
                        part = conv[:, 4 * q:4 * q + 4, :, :].rearrange("p c g i -> p c (g i)")
                        ve.tensor_tensor(part, part, row.unsqueeze(1).broadcast_to([P, 4, 2 * T]), op)\
                          .then_inc(done, 1)

                each_chunk(mean[:, :], ALU.subtract, centred)
                ve.wait_ge(var_mm, 1)
                ve.wait_ge(centred, 2)
                ve.tensor_scalar(mean[:, :], bank[1][:, 0:256], 1.0 / D, EPS, ALU.mult, ALU.add)\
                  .then_inc(var_ready, 1)
                ve.wait_ge(std_ready, 1)
                link(ve.reciprocal(rstd_c[:, :], rstd_c[:, :]))
                each_chunk(rstd_c[:, :], ALU.mult, scaled)
                ada2_scale(1)
                first_experts_low(1, 0)

            def first_max(out, v, n, prio, scratch, top):
                shape = [P, 2, n]
                link(ve.tensor_reduce(top, v, AX, ALU.max))
                link(ve.tensor_tensor(scratch, v, top.unsqueeze(2).broadcast_to(shape), ALU.is_equal))
                link(ve.tensor_tensor(scratch, scratch, prio.unsqueeze(1).broadcast_to(shape), ALU.mult))
                link(ve.tensor_reduce(top, scratch, AX, ALU.max))
                link(ve.tensor_tensor(out, scratch, top.unsqueeze(2).broadcast_to(shape), ALU.is_equal))

            def routing(layer):
                ve.memset(act[SLOTS:P, :], 0.0)
                ve.wait_ge(scores_ready, layer + 1)
                def row(k, n=NE):
                    return rs[:, k, 0:2 * n].rearrange("p (t e) -> p t e", t=2)

                score, sel = row(0), row(1)
                prio4 = cst[:, C_PR4:C_PR4 + NG]
                prio16 = cst[:, C_PR16:C_PR16 + NE]
                link(ve.tensor_tensor(sel, score, bias_b[:, :].unsqueeze(1).broadcast_to([P, 2, NE]), ALU.add))
                s = rs[:, 1, :].rearrange("p (g k) -> p g k", k=4)
                pair = rs[:, 2:4, :].rearrange("p a b -> p (a b)")[:, 0:48].rearrange("p (g k) -> p g k", k=6)
                ve.tensor_tensor(pair[:, :, 0:2], s[:, :, 0:4:2], s[:, :, 1:4:2], ALU.add)
                ve.tensor_tensor(pair[:, :, 2:4], s[:, :, 0:2], s[:, :, 2:4], ALU.add)
                ve.tensor_tensor(pair[:, :, 4:5], s[:, :, 0:1], s[:, :, 3:4], ALU.add)
                link(ve.tensor_tensor(pair[:, :, 5:6], s[:, :, 1:2], s[:, :, 2:3], ALU.add))
                link(ve.tensor_reduce(rs[:, 4, 0:8], pair, AX, ALU.max))
                best = row(6, NG)
                first_max(best, row(4, NG), NG, prio4, row(5, NG), rs[:, 7, 0:2])
                link(ve.tensor_scalar(best, best, BIG, -BIG, ALU.mult, ALU.add))
                v4 = rs[:, 8, :].rearrange("p (g k) -> p g k", k=4)
                link(ve.tensor_tensor(v4, s, rs[:, 6, 0:8].unsqueeze(2).broadcast_to([P, 8, 4]), ALU.add))
                v, one, two = row(8), row(9), row(10)
                first_max(one, v, NE, prio16, row(5), rs[:, 7, 0:2])
                link(ve.scalar_tensor_tensor(out=v, in0=one, scalar=-2.0 * BIG, in1=v, op0=ALU.mult, op1=ALU.add))
                first_max(two, v, NE, prio16, row(5), rs[:, 7, 0:2])
                ve.tensor_tensor(asg[:, :, :], one, two, ALU.add).then_inc(assigned, 1)
                ve.wait_ge(assigned, layer + 1)
                link(ve.tensor_tensor(row(11), score, asg[:, :, :], ALU.mult))
                link(ve.reduce_sum(rs[:, 7, 0:2], row(11), AX))
                link(ve.reciprocal(rs[:, 7, 2:4], rs[:, 7, 0:2]))
                ve.tensor_tensor(gates[:, :, :], row(11), rs[:, 7, 2:4].unsqueeze(2).broadcast_to([P, 2, NE]),
                                 ALU.mult).then_inc(routed, 1)
                link(ve.tensor_scalar(row(9), asg[:, :, :], -FAR, FAR, ALU.mult, ALU.add))
                ve.wait_ge(pos_mm, layer + 1)
                ve.tensor_tensor(pos[:, :, :], row(9), U[:, 0:2 * NE].rearrange("p (t e) -> p t e", t=2),
                                 ALU.add).then_inc(routed, 1)
                link(ve.reduce_max(rs[:, 7, 4:5], U[:, 2 * NE:3 * NE], AX))
                link(ve.tensor_scalar(rs[:, 7, 5:6], rs[:, 7, 4:5], CAP + 0.5, None, ALU.is_gt))
                ve.tensor_copy(flag[:, 0:1], rs[:, 7, 5:6]).then_inc(routed, 1)
                ve.wait_ge(routed, 3 * layer + 3)

            def experts(layer):
                eo, b0 = NE * layer, BASE_MOE[layer]

                def build_p2(e0, i=None):
                    e = lin(i, 2, e0)
                    par = e0 % 2
                    if eo + e0 >= 2:
                        ve.wait_ge(sel_mm, lin(i, 2, eo + e0 - 1))
                    for t in range(2):
                        ve.tensor_scalar(p2[:, par, t, :], cst[:, C_SLOT:C_SLOT + P], pos[:, t, bass.ds(e, 1)],
                                         None, ALU.is_equal).then_inc(p2_built, 1)
                    ve.tensor_copy(gate_tok[:, par, :], gates[:, :, bass.ds(e, 1)].rearrange("p t o -> p (t o)"))\
                      .then_inc(p2_built, 1)

                def low_tokens(e0, i=None):
                    par = e0 % 2
                    ve.wait_ge(xs_hi, lin(i, 2, eo + e0 + 1))
                    ve.tensor_tensor(xs[:, par, :, SLOTS:P], X[:, :].rearrange("p (c s) -> p c s", c=DC),
                                     xs[:, par, :, 0:SLOTS], ALU.subtract).then_inc(xs_lo, 1)

                def low_result(e0, hf, i=None):
                    ve.wait_ge(yh_done, lin(i, 4, 2 * (eo + e0 - 1) + hf + 1))
                    ve.tensor_tensor(yl[:, hf, :], DN[:, :], yh[:, hf, :], ALU.subtract).then_inc(yl_done, 1)

                def expert_step(e0, i=None):
                    ahead = blocks_ahead(e0)

                    def split():
                        n = next(ahead)
                        if n is not None:
                            low(ve, b0 + n, i)

                    if e0:
                        ve.wait_ge(u_low, lin(i, 2, eo + e0))
                        if eo + e0 >= 2:
                            ve.wait_ge(act_done, lin(i, 2, eo + e0 - 1))
                        ve.tensor_tensor(u_sum[:, :], U[0:SLOTS, :], u_lo[:, :], ALU.add).then_inc(u_folded, 1)
                        ve.wait_ge(silu_done, lin(i, 2, eo + e0))
                        ve.wait_ge(u_folded, lin(i, 2, eo + e0))
                        ve.wait_ge(sel_evac, lin(i, 4, 2 * (eo + e0)))
                        if eo + e0 >= 2:
                            ve.wait_ge(actT_mm, lin(i, 2, eo + e0 - 1))
                        ve.scalar_tensor_tensor(out=act[0:SLOTS, :], in0=g_silu[:, :], scalar=gate_slot[0:SLOTS, :],
                                                in1=u_sum[:, :], op0=ALU.mult, op1=ALU.mult).then_inc(act_done, 1)
                    if e0 + 1 < NE:
                        build_p2(e0 + 1, i)
                    if e0:
                        ve.wait_ge(as_hi, lin(i, 2, eo + e0))
                        ve.tensor_tensor(actT[:, :, SLOTS:P],
                                         X[:, :].rearrange("p (c s) -> p c s", c=FC)[:, :, 0:SLOTS],
                                         actT[:, :, 0:SLOTS], ALU.subtract).then_inc(as_lo, 1)
                    split()
                    if e0 < NE:
                        ve.wait_ge(g_low, lin(i, 2, eo + e0 + 1))
                        if eo + e0:
                            ve.wait_ge(silu_done, lin(i, 2, eo + e0))
                        ve.tensor_tensor(g_sum[:, :], G[0:SLOTS, :], g_lo[:, :], ALU.add).then_inc(g_folded, 1)
                    split()
                    split()
                    if e0:
                        low_result(e0, 0, i)
                    split()
                    if e0 + 1 < NE:
                        low_tokens(e0 + 1, i)
                    split()
                    if e0:
                        low_result(e0, 1, i)
                    split()

                build_p2(0)
                first_experts_low(layer, 1)
                low_tokens(0)
                expert_step(0)
                expert_step(1)
                with ve.Fori(0, 6) as i:
                    expert_step(2, i)
                    expert_step(3, i)
                for e0 in range(14, NE + 1):
                    expert_step(e0)
                ve.wait_ge(scat, 2 * NE * (layer + 1))
                for t in range(2):
                    for hf in range(2):
                        cols = slice(hf * 512, (hf + 1) * 512)
                        link(ve.tensor_tensor(moe_tmp[:, 2 * t + hf, :], ACC[2 * t + hf][:, :], mod[:, 5, cols],
                                              ALU.mult))
                        ve.tensor_tensor(x[:, t, cols], x[:, t, cols], moe_tmp[:, 2 * t + hf, :],
                                         ALU.add).then_inc(x_add, 1)
                ve.wait_ge(x_add, 4 * layer + 4)

            def overflow(layer):
                o = over[layer]
                n_over = ve.value_load(flag[0:1, 0:1], min_val=0, max_val=1)
                with ve.If(n_over > 0):
                    ve.memset(over_g[SLOTS:P, 1, :], 0.0).then_inc(o["dve"], 1)
                    for r in range(OVER):
                        with ve.Fori(0, NE) as e:
                            done = [0]

                            def sig_step(ins):
                                done[0] += 1
                                ins.then_inc(o["dve"], 1)
                                ve.wait_ge(o["dve"], e * OV_DVE + (r * NE * OV_DVE + 1 + done[0]))

                            def pe_at(s):
                                ve.wait_ge(o["pe"], e * OV_PE + (r * NE * OV_PE + s))

                            for t in range(2):
                                sig_step(ve.tensor_scalar(over_p[:, t, :], cst[:, C_OVER:C_OVER + SLOTS],
                                                          float(r * SLOTS), pos[:, t, bass.ds(e, 1)],
                                                          ALU.add, ALU.is_equal))
                            sig_step(ve.tensor_copy(gate_tok[:, 0, :],
                                                    gates[:, :, bass.ds(e, 1)].rearrange("p t o -> p (t o)")))
                            pe_at(1)
                            sig_step(ve.tensor_copy(over_x[:, :, :],
                                                    bank[0][:, :].rearrange("p (c s) -> p c s", c=DC)))
                            sig_step(ve.tensor_copy(gate_slot[0:SLOTS, :], bank[2][0:SLOTS, 0:1]))
                            sig_step(ve.tensor_copy(over_pT[:, :, :], bank[1][0:SLOTS, 0:2 * P]
                                                    .rearrange("p (t i) -> p t i", t=2)))
                            ve.wait_ge(o["act"], e + (r * NE + 1))
                            sig_step(ve.scalar_tensor_tensor(out=over_g[0:SLOTS, 1, :],
                                                             in0=over_g[0:SLOTS, 0, :],
                                                             scalar=gate_slot[0:SLOTS, :], in1=U[0:SLOTS, :],
                                                             op0=ALU.mult, op1=ALU.mult))
                            pe_at(3)
                            sig_step(ve.tensor_copy(over_aT[:, :, :], bank[3][:, :]
                                                    .rearrange("p (c s) -> p c s", c=FC)[:, :, 0:SLOTS]))
                            pe_at(4)
                            for hf, y in enumerate((DN, X)):
                                sig_step(ve.tensor_copy(over_y[:, hf * 512:(hf + 1) * 512], y[0:SLOTS, :]))
                            pe_at(5)
                            for t in range(2):
                                for hf in range(2):
                                    cols = slice(hf * 512, (hf + 1) * 512)
                                    sig_step(ve.tensor_tensor(over_t[:, t, cols], ACC[2 * t + hf][:, :],
                                                              mod[:, 5, cols], ALU.mult))
                            for t in range(2):
                                for hf in range(2):
                                    cols = slice(hf * 512, (hf + 1) * 512)
                                    sig_step(ve.tensor_tensor(x[:, t, cols], x[:, t, cols],
                                                              over_t[:, t, cols], ALU.add))
                            assert done[0] == OV_DVE
                ve.memset(lam[:, 7:8], 0.0).then_inc(x_moe, 1)

            for layer in range(2):
                adaln(layer)
                evac_hT(2 * layer)
                if layer == 0:
                    attention()
                else:
                    convolution()
                add_gated(layer, 2)
                rms(2 * layer + 1)
                norm_rows(2 * layer + 1)
                evac_hT(2 * layer + 1)
                routing(layer)
                experts(layer)
                overflow(layer)
            rms(4)
            ve.wait_ge(fin_mm, 1)
            for t in range(2):
                for q in range(2):
                    cols = slice(q * 512, (q + 1) * 512)
                    ins = ve.scalar_tensor_tensor(out=h[:, t, cols], in0=x[:, t, cols],
                                                  scalar=stat[:, 6 + t:7 + t], in1=bank[4 + q][:, :],
                                                  op0=ALU.mult, op1=ALU.mult)
                ins.then_inc(h_ready, 1)


_INS = ['x_prompt', 'x_sample', 'cache_k', 'cache_v', 'c', 'c_ctx', 'norm1_g', 'norm2_g', 'ada_w', 'ada_b',
        'attn_w_qkv', 'attn_w_o', 'attn_lambda_q1', 'attn_lambda_k1', 'attn_lambda_q2', 'attn_lambda_k2',
        'attn_subln_g', 'conv_w_pw1', 'conv_b_pw1', 'conv_w_dw', 'conv_b_dw', 'conv_ln_g', 'conv_ln_b',
        'conv_w_pw2', 'conv_b_pw2', 'router_w', 'router_bias', 'moe_w_gate', 'moe_w_up', 'moe_w_down',
        'final_norm_g']


def kernel(**inputs):
    import concourse.bacc as bacc
    from concourse.bass_utils import run_bass_kernel_spmd

    nc = bacc.Bacc("TRN2", target_bir_lowering=False, num_devices=1)
    arrays, a = {}, {}
    for name in _INS:
        arr = np.ascontiguousarray(inputs[name])
        arrays[f"in_{name}"] = arr
        a[name] = nc.dram_tensor(f"in_{name}", arr.shape, F32, kind="ExternalInput").ap()
    arrays["in_consts"] = constants()
    a["consts"] = nc.dram_tensor("in_consts", (P, C_ALL), F32, kind="ExternalInput").ap()
    shapes = [(1, T, D), (1, T, D), (1, 1, T, NH, 2 * HD), (1, 1, T, NH, 2 * HD)]
    outs = [nc.dram_tensor(f"out_{i}", s, F32, kind="ExternalOutput").ap() for i, s in enumerate(shapes)]
    trunk_kernel(nc, a, outs[0], outs[1], outs[2][0, 0].rearrange("t h e -> t (h e)"),
                 outs[3][0, 0].rearrange("t h e -> t (h e)"))
    r = run_bass_kernel_spmd(nc, [arrays], core_ids=[0])
    return tuple(r.results[0][f"out_{i}"] for i in range(4))
```
